# Optimizing a Trainium2 kernel written in Bass

```python
import functools
import jax, jax.numpy as jnp
from jax import lax
import numpy as np

D_MODEL = 2048
BATCH = 1
SEQ = 512
DEPTH = 2
DEC_BATCH = 8
DEC_SEQ = 1
PAST_LEN = 2048
PAGE_SIZE = 128

N_EVEN = (DEPTH + 1) // 2
N_ODD = DEPTH // 2
BRANCH = D_MODEL // 2
HA = 4
DVA = BRANCH // HA
DKA = DVA // 2
GLA_RANK = 16
GLA_TAU = 16.0
GLA_CHUNK = 64
HB = 4
DVB = BRANCH // HB
DKB = DVB // 2
RET_CHUNK = 128
ROPE_BASE = 10000.0
HC = 8
DC = BRANCH // HC
SB_BLOCK = 128
SB_OFFSET_NEAR = 4.0
SB_OFFSET_FAR = 10.0
DG = 8
DGC = BRANCH // DG
D_CHUNK = 128
RMS_EPS = 1e-6
EVEN_SIZES = (HA * DKA, HA * DKA, HA * DVA, GLA_RANK, HA * DVA, HB * DKB, HB * DKB, HB * DVB, HB * DVB)
ODD_SIZES = (HC * DC, HC * DC, HC * DC, HC * DC, BRANCH, BRANCH, BRANCH)
W_EVEN = HA * DVA + HB * DVB
W_ODD = HC * DC + BRANCH

kernel_name = 'hybrid_gla_retnet_stickbreak_chunkmlp_step'

def rms_norm(x, g, eps=RMS_EPS):
    xf = x.astype(jnp.float32)
    y = xf * lax.rsqrt(jnp.mean(xf * xf, axis=-1, keepdims=True) + eps)
    return (y * g.astype(jnp.float32)).astype(x.dtype)

def split_cols(x, sizes):
    return jnp.split(x, np.cumsum(sizes)[:-1].tolist(), axis=-1)

def ada_modulation(c, w, b):
    m = jax.nn.silu(c) @ w + b
    shift, scale, gate = jnp.split(m[:, None, :], 3, axis=-1)
    return shift, scale, gate

def rotary(x, pos):
    half = x.shape[-1] // 2
    inv = ROPE_BASE ** (-jnp.arange(half, dtype=jnp.float32) / half)
    ang = pos.astype(jnp.float32)[:, None] * inv[None, :]
    cos = jnp.cos(ang)[None, :, None, :]
    sin = jnp.sin(ang)[None, :, None, :]
    x1, x2 = x[..., :half], x[..., half:]
    return jnp.concatenate([x1 * cos - x2 * sin, x1 * sin + x2 * cos], axis=-1)

def retention_log_gamma():
    return jnp.log1p(-jnp.exp2(-5.0 - jnp.arange(HB, dtype=jnp.float32)))

def gla_chunk(q, k, v, log_a, state):
    C = q.shape[1]
    b = jnp.cumsum(log_a, axis=1)
    o_inter = jnp.einsum('bthk,bhkv->bthv', q * jnp.exp(b), state)
    causal = jnp.tril(jnp.ones((C, C), dtype=bool))[None, :, :, None, None]
    diff = b[:, :, None] - b[:, None, :]
    decay = jnp.exp(jnp.where(causal, diff, -jnp.inf))
    scores = jnp.einsum('btshk,bthk,bshk->bhts', decay, q, k)
    o_intra = jnp.einsum('bhts,bshv->bthv', scores, v)
    b_last = b[:, -1]
    k_dec = k * jnp.exp(b_last[:, None] - b)
    new_state = jnp.exp(b_last)[..., None] * state + jnp.einsum('bshk,bshv->bhkv', k_dec, v)
    return o_inter + o_intra, new_state

def retention_chunk(q, k, v, state, log_gamma):
    C = q.shape[1]
    idx = jnp.arange(C, dtype=jnp.float32)
    inter_decay = jnp.exp((idx + 1.0)[:, None] * log_gamma[None, :])
    o_inter = jnp.einsum('bthk,bhkv->bthv', q, state) * inter_decay[None, :, :, None]
    rel = idx[:, None] - idx[None, :]
    decay = jnp.exp(jnp.where((rel >= 0)[..., None], rel[..., None] * log_gamma, -jnp.inf))
    scores = jnp.einsum('bthk,bshk->bhts', q, k) * jnp.transpose(decay, (2, 0, 1))[None]
    o_intra = jnp.einsum('bhts,bshv->bthv', scores, v)
    k_decay = jnp.exp((C - 1.0 - idx)[:, None] * log_gamma[None, :])
    new_state = (jnp.exp(C * log_gamma)[:, None, None] * state
                 + jnp.einsum('bshk,bshv->bhkv', k * k_decay[None, :, :, None], v))
    return o_inter + o_intra, new_state

def chunked_recurrence(chunk_fn, state0, xs, chunk):
    B, T = xs[0].shape[:2]
    L = min(chunk, T)
    n = T // L
    xs_c = tuple(a.reshape(B, n, L, *a.shape[2:]).swapaxes(0, 1) for a in xs)

    def step(s, xc):
        o, s = chunk_fn(*xc, s)
        return s, o

    s, o = lax.scan(step, state0.astype(jnp.float32), xs_c)
    return o.swapaxes(0, 1).reshape(B, T, *o.shape[3:]), s

def stick_breaking_block(q, k, v, q_pos, k_pos, offset):
    z = (jnp.einsum('bqhd,bshd->bhqs', q, k) * (q.shape[-1] ** -0.5)
         + offset.astype(jnp.float32)[None, :, None, None])
    mask = (k_pos[None, :] < q_pos[:, None])[None, None]
    log_beta = jax.nn.log_sigmoid(z)
    log_rest = jnp.where(mask, jax.nn.log_sigmoid(-z), 0.0)
    between = lax.cumsum(log_rest, axis=3, reverse=True) - log_rest
    weight = jnp.where(mask, jnp.exp(log_beta + between), 0.0)
    return jnp.einsum('bhqs,bshd->bqhd', weight, v)

def stick_breaking_sweep(q, k, v, n_past, offset):
    B, T, H, d = q.shape
    L = min(SB_BLOCK, T)
    n = T // L
    k_pos = jnp.arange(k.shape[1])
    q_blocks = q.reshape(B, n, L, H, d).swapaxes(0, 1)
    q_pos = (n_past + jnp.arange(T)).reshape(n, L)
    out = lax.map(lambda a: stick_breaking_block(a[0], k, v, a[1], k_pos, offset), (q_blocks, q_pos))
    return out.swapaxes(0, 1).reshape(B, T, H, d)

def chunk_spatial_gate(u, v, w_s, b_s):
    B, T, G, c = v.shape
    L = min(D_CHUNK, T)
    n = T // L
    w = jnp.tril(w_s[:, :L, :L])
    vc = v.reshape(B, n, L, G, c)
    mixed = jnp.einsum('gts,bnsgc->bntgc', w, vc) + jnp.transpose(b_s[:, :L])[None, None, :, :, None]
    return u * mixed.reshape(B, T, G, c)

def even_layer(x, c, pos, gla_s0, ret_s0, norm_g, w_ada, b_ada, w_in, w_a2, b_a,
               gla_norm_g, ret_norm_g, w_out):
    B, T, _ = x.shape
    f32 = jnp.float32
    shift, scale, gate = ada_modulation(c, w_ada, b_ada)
    h = rms_norm(x, norm_g) * (1.0 + scale) + shift
    qa, ka, va, ra, ga, qb, kb, vb, gb = split_cols(h @ w_in, EVEN_SIZES)
    heads = lambda t, H: t.astype(f32).reshape(B, T, H, -1)
    log_a = jax.nn.log_sigmoid((ra @ w_a2 + b_a).astype(f32)) / GLA_TAU
    oa, gla_s = chunked_recurrence(
        gla_chunk, gla_s0,
        (heads(qa, HA) * DKA ** -0.5, heads(ka, HA), heads(va, HA), log_a.reshape(B, T, HA, DKA)),
        GLA_CHUNK)
    oa = rms_norm(oa, gla_norm_g.reshape(HA, DVA)).reshape(B, T, -1) * jax.nn.silu(ga.astype(f32))
    qr = rotary(heads(qb, HB), pos) * DKB ** -0.5
    kr = rotary(heads(kb, HB), pos)
    ob, ret_s = chunked_recurrence(
        functools.partial(retention_chunk, log_gamma=retention_log_gamma()), ret_s0,
        (qr, kr, heads(vb, HB)), RET_CHUNK)
    ob = rms_norm(ob, ret_norm_g.reshape(HB, DVB)).reshape(B, T, -1) * jax.nn.silu(gb.astype(f32))
    mixed = jnp.concatenate([oa, ob], axis=-1).astype(x.dtype) @ w_out
    return x + gate * mixed, gla_s, ret_s

def odd_layer(x, c, k_past, v_past, norm_g, w_ada, b_ada, w_in, q_norm_g, k_norm_g,
              sb_offset, v_norm_g, w_s, b_s, w_out):
    B, T, _ = x.shape
    f32 = jnp.float32
    shift, scale, gate = ada_modulation(c, w_ada, b_ada)
    h = rms_norm(x, norm_g) * (1.0 + scale) + shift
    qc, kc, vc, gc, ud, vd, gd = split_cols(h @ w_in, ODD_SIZES)
    heads = lambda t: t.astype(f32).reshape(B, T, HC, DC)
    qc = rms_norm(heads(qc), q_norm_g)
    kc = rms_norm(heads(kc), k_norm_g)
    vc = heads(vc)
    if k_past is None:
        k_all, v_all, n_past = kc, vc, 0
    else:
        k_all = jnp.concatenate([k_past.astype(f32), kc], axis=1)
        v_all = jnp.concatenate([v_past.astype(f32), vc], axis=1)
        n_past = k_past.shape[1]
    oc = stick_breaking_sweep(qc, k_all, v_all, n_past, sb_offset).reshape(B, T, -1)
    oc = oc * jax.nn.silu(gc.astype(f32))
    u = jax.nn.gelu(ud.astype(f32))
    vn = rms_norm(jax.nn.gelu(vd.astype(f32)), v_norm_g)
    od = chunk_spatial_gate(u.reshape(B, T, DG, DGC), vn.reshape(B, T, DG, DGC),
                            w_s.astype(f32), b_s.astype(f32)).reshape(B, T, -1)
    od = od * jax.nn.silu(gd.astype(f32))
    mixed = jnp.concatenate([oc, od], axis=-1).astype(x.dtype) @ w_out
    return x + gate * mixed, kc, vc, vn

def setup_inputs(seed: int = 0) -> dict:
    key = jax.random.key(seed)
    ks = iter(jax.random.split(key, 64))
    f32 = jnp.float32

    def normal(shape, scale=1.0):
        return jax.random.normal(next(ks), shape, f32) * scale

    def gain(shape):
        return 1.0 + normal(shape, 0.02)

    n_pages = PAST_LEN // PAGE_SIZE
    n_used = DEC_BATCH * n_pages
    n_pool = n_used + max(1, n_used // 4)
    perm = jax.random.permutation(next(ks), n_pool)
    page_table = perm[:n_used].reshape(DEC_BATCH, n_pages).astype(jnp.int32)
    p_even = sum(EVEN_SIZES)
    p_odd = sum(ODD_SIZES)
    sb_offset = (-jnp.linspace(SB_OFFSET_NEAR, SB_OFFSET_FAR, HC, dtype=f32)[None, :]
                 + normal((N_ODD, HC), 0.1))
    return {
        'x_prompt': normal((BATCH, SEQ, D_MODEL)),
        'x_sample': normal((DEC_BATCH, DEC_SEQ, D_MODEL)),
        'state_gla': normal((N_EVEN, DEC_BATCH, HA, DKA, DVA)),
        'state_ret': normal((N_EVEN, DEC_BATCH, HB, DKB, DVB)),
        'cache_k': normal((N_ODD, n_pool, PAGE_SIZE, HC, DC)),
        'cache_v': normal((N_ODD, n_pool, PAGE_SIZE, HC, DC)),
        'page_table': page_table,
        'c_prompt': normal((BATCH, D_MODEL)),
        'c_sample': normal((DEC_BATCH, D_MODEL)),
        'e_norm_g': gain((N_EVEN, D_MODEL)),
        'e_w_ada': normal((N_EVEN, D_MODEL, 3 * D_MODEL), 0.5 * D_MODEL ** -0.5),
        'e_b_ada': normal((N_EVEN, 3 * D_MODEL), 0.02),
        'e_w_in': normal((N_EVEN, D_MODEL, p_even), D_MODEL ** -0.5),
        'e_w_a2': normal((N_EVEN, GLA_RANK, HA * DKA), GLA_RANK ** -0.5),
        'e_b_a': normal((N_EVEN, HA * DKA), 0.1),
        'e_gla_norm_g': gain((N_EVEN, HA * DVA)),
        'e_ret_norm_g': gain((N_EVEN, HB * DVB)),
        'e_w_out': normal((N_EVEN, W_EVEN, D_MODEL), W_EVEN ** -0.5),
        'o_norm_g': gain((N_ODD, D_MODEL)),
        'o_w_ada': normal((N_ODD, D_MODEL, 3 * D_MODEL), 0.5 * D_MODEL ** -0.5),
        'o_b_ada': normal((N_ODD, 3 * D_MODEL), 0.02),
        'o_w_in': normal((N_ODD, D_MODEL, p_odd), D_MODEL ** -0.5),
        'o_q_norm_g': gain((N_ODD, DC)),
        'o_k_norm_g': gain((N_ODD, DC)),
        'o_sb_offset': sb_offset,
        'o_v_norm_g': gain((N_ODD, BRANCH)),
        'o_w_s': normal((N_ODD, DG, D_CHUNK, D_CHUNK), D_CHUNK ** -0.5),
        'o_b_s': 1.0 + normal((N_ODD, DG, D_CHUNK), 0.1),
        'o_w_out': normal((N_ODD, W_ODD, D_MODEL), W_ODD ** -0.5),
    }

def reference(x_prompt, x_sample, state_gla, state_ret, cache_k, cache_v, page_table,
              c_prompt, c_sample, e_norm_g, e_w_ada, e_b_ada, e_w_in, e_w_a2, e_b_a,
              e_gla_norm_g, e_ret_norm_g, e_w_out, o_norm_g, o_w_ada, o_b_ada, o_w_in,
              o_q_norm_g, o_k_norm_g, o_sb_offset, o_v_norm_g, o_w_s, o_b_s, o_w_out):
    f32 = jnp.float32
    dec_b = page_table.shape[0]
    n_past = page_table.shape[1] * cache_k.shape[2]
    pos_prompt = jnp.arange(x_prompt.shape[1])
    pos_sample = n_past + jnp.arange(x_sample.shape[1])
    xp, xs = x_prompt, x_sample
    gla_p, gla_s, ret_p, ret_s = [], [], [], []
    k_p, v_p, k_s, v_s, chunk_v = [], [], [], [], []
    for layer in range(DEPTH):
        i = layer // 2
        if layer % 2 == 0:
            w = (e_norm_g[i], e_w_ada[i], e_b_ada[i], e_w_in[i], e_w_a2[i], e_b_a[i],
                 e_gla_norm_g[i], e_ret_norm_g[i], e_w_out[i])
            zero_gla = jnp.zeros((xp.shape[0], HA, DKA, DVA), f32)
            zero_ret = jnp.zeros((xp.shape[0], HB, DKB, DVB), f32)
            xp, sg, sr = even_layer(xp, c_prompt, pos_prompt, zero_gla, zero_ret, *w)
            gla_p.append(sg)
            ret_p.append(sr)
            xs, sg, sr = even_layer(xs, c_sample, pos_sample, state_gla[i], state_ret[i], *w)
            gla_s.append(sg)
            ret_s.append(sr)
        else:
            w = (o_norm_g[i], o_w_ada[i], o_b_ada[i], o_w_in[i], o_q_norm_g[i], o_k_norm_g[i],
                 o_sb_offset[i], o_v_norm_g[i], o_w_s[i], o_b_s[i], o_w_out[i])
            xp, kk, vv, _ = odd_layer(xp, c_prompt, None, None, *w)
            k_p.append(kk)
            v_p.append(vv)
            k_past = cache_k[i][page_table].reshape(dec_b, n_past, HC, DC)
            v_past = cache_v[i][page_table].reshape(dec_b, n_past, HC, DC)
            xs, kk, vv, cv = odd_layer(xs, c_sample, k_past, v_past, *w)
            k_s.append(kk)
            v_s.append(vv)
            chunk_v.append(cv)
    return (xp, xs, jnp.stack(gla_p), jnp.stack(gla_s), jnp.stack(ret_p), jnp.stack(ret_s),
            jnp.stack(k_p), jnp.stack(v_p), jnp.stack(k_s), jnp.stack(v_s), jnp.stack(chunk_v))


_drawn_inputs = setup_inputs


def setup_inputs(seed=0):
    import zlib

    import numpy as np

    out = dict(_drawn_inputs(seed))
    spreads = {}
    factors = {'cache_k': 6.515,
     'cache_v': 4.941,
     'e_gla_norm_g': 8.0,
     'e_ret_norm_g': 8.0,
     'o_norm_g': 2.956,
     'o_q_norm_g': 8.0,
     'o_k_norm_g': 2.9,
     'o_sb_offset': 2.903,
     'o_v_norm_g': 2.874,
     'o_b_s': 6.552}
    for name, (base, spread) in spreads.items():
        noise = np.random.default_rng([zlib.crc32(name.encode()), seed]).standard_normal(out[name].shape)
        drawn = base * np.exp(spread * noise) if base else spread * noise
        out[name] = __import__('jax').numpy.asarray(drawn.astype(out[name].dtype))
    for name, factor in factors.items():
        out[name] = (out[name] * factor).astype(out[name].dtype)
    return out
```

```python
from contextlib import ExitStack

import numpy as np
import concourse.bass as bass
from concourse import mybir

F32 = mybir.dt.float32
F32R = mybir.dt.float32r
I32 = mybir.dt.int32
ALU = mybir.AluOpType
ACT = mybir.ActivationFunctionType

P = 128
D = 2048
KC = D // P
T = 512
NB = 8
N = T + NB
HALF = N // 2
NT = T // P
HEADS = 4
RANK = 16
CH = 64
NCH = T // CH
NPAGE, PAGE, NPOOL = 16, 128, 160
HC = 8
BR = D // 2
EPS = 1e-6
DH = P
SCALE = float(DH) ** -0.5
GELU = 1.5957691216057308
SB_OFF = {0: 0, 1: 512, 3: 896, 2: 1024}
SB_ALL = 1280
BIG = 3.0e38

E_QA, E_KA, E_VA, E_RA, E_GA = 0, 512, 1024, 2048, 2064
E_QB, E_KB, E_VB, E_GB = 3088, 3600, 4112, 5136
O_Q, O_K, O_V, O_G, O_U, O_VD, O_GD = (BR * n for n in range(7))

U_ADA0, U_RA, U_L0, U_OUT0, U_L1A, U_L1B, U_OUT1 = 0, 96, 98, 258, 290, 354, 434
T_RA, T_L0, T_OUT0, T_L1A, T_L1B, T_OUT1 = 0, 1, 49, 65, 81, 121
RAW_DEPTH = 4
TILE, MOD = "tile", "mod"
L0_ORDER = [TILE, MOD, TILE, MOD, TILE, MOD, TILE, MOD, TILE, TILE]
L1A_ORDER = [TILE, MOD, TILE, MOD, TILE, MOD, TILE, MOD]
L1B_ORDER = [TILE] * 5
OUT_ORDER = [TILE] * 2
L1B_SLOTS = [2, 3, 0, 1, 4]

C_BADA, C_NORM, C_MIX, C_VN, C_QN, C_KN = (0, 48), (96, 112), 128, 144, 152, 153


def constants():
    c = {}
    c["ident"] = np.eye(P)
    t = np.arange(P)
    same = (t[:, None] // CH) == (t[None, :] // CH)
    mid = (t // CH) * CH + CH // 2 - 1
    upto = (same & (t[:, None] <= t[None, :])).astype(np.float64)
    to_mid = (same & (t[:, None] <= mid[None, :])).astype(np.float64)
    c["cum_mid"] = (upto - to_mid) / 16.0
    small = np.zeros((P, 6))
    for n in range(2):
        m, last = to_mid[:, n * CH], upto[:, n * CH + CH - 1]
        small[:, n], small[:, 2 + n], small[:, 4 + n] = m, last, last - m
    c["cum_small"] = small / 16.0
    c["chunk_mask"] = same & (t[:, None] <= t[None, :])
    c["below"] = t[:, None] < t[None, :]
    c["from_key"] = t[:, None] >= t[None, :]
    c["upto_t"] = t[:, None] <= t[None, :]
    c["swap"] = np.roll(np.eye(P), P // 2, axis=0)
    c["fold"] = np.concatenate([np.eye(9)] * 2, 0)
    c = {k: np.ascontiguousarray(v, dtype=np.float32) for k, v in c.items()}
    pos = np.concatenate([np.arange(T), np.full(NB, NPAGE * PAGE)]).astype(np.float32)
    half = P // 2
    inv = (np.float32(10000.0) ** (-np.arange(half, dtype=np.float32) / np.float32(half))).astype(np.float32)
    ang = (pos[None, :] * inv[:, None]).astype(np.float32).astype(np.float64)
    c["rope"] = np.stack([np.concatenate([np.cos(ang)] * 2, 0),
                          np.concatenate([-np.sin(ang), np.sin(ang)], 0)], 1).astype(np.float32)
    lg = np.log1p(-np.exp2(-5.0 - np.arange(HEADS)))
    rel = np.arange(T) % CH - (CH // 2 - 1)
    m, last = CH // 2, CH
    sm = np.zeros((HEADS, 32))
    for tile in range(NT):
        sm[:, 6 * tile:6 * tile + 6] = np.exp(lg[:, None] * np.array([m, m, last, last, last - m, last - m]))
    sm[:, 24:] = np.exp(lg)[:, None]
    ret = np.concatenate([np.exp(lg[:, None] * rel), np.exp(-lg[:, None] * rel), sm], 1)
    c["ret"] = ret[:, None, :].repeat(P, 1).astype(np.float32)
    return c


CHIP = ("ident", "cum_mid", "cum_small", "chunk_mask", "below", "from_key", "upto_t", "swap", "fold")


def build(nc, a, o, cst):
    ctx = ExitStack()
    with ctx:
        def sb(name, shape, dt=F32):
            return ctx.enter_context(nc.sbuf_tensor(name, shape, dt))

        sems = {}

        def s(name):
            if name not in sems:
                sems[name] = ctx.enter_context(nc.semaphore(name))
            return sems[name]

        xt_dram = nc.dram_tensor("xt_scratch", [P, KC, N], F32).ap()
        x1_dram = nc.dram_tensor("x1_scratch", [P, KC, N], F32).ap()

        act_hi = sb("act_hi", [P, KC, N], F32R)
        act_lo = sb("act_lo", [P, KC, N], F32R)
        wide = sb("wide", [P, KC, N])
        raw = sb("raw", [P, 5, 1024])
        w_hi = sb("w_hi", [P, 2, 1024], F32R)
        w_lo = sb("w_lo", [P, 2, 1024], F32R)
        cm = {k: sb("c_" + k, list(cst[k].shape)) for k in CHIP}
        ident = cm["ident"]
        ones = sb("ones", [P, P])
        mod = [sb("mod0", [P, 48, 9]), sb("mod1", [P, 48, 9])]
        cols = sb("cols", [P, 154])
        per_head = sb("per_head", [P, 3, HC])
        cond = sb("cond", [P, KC, 66], F32R)
        arena = sb("arena", [P, 15600])
        used = [0]

        def region(n):
            at = used[0]
            used[0] += n
            assert used[0] <= 15600, used[0]
            return arena[:, at:at + n]

        mrow = region(512)
        G = [region(N) for _ in range(6)]
        t0_at = used[0]
        tmp = [region(N) for _ in range(5)]
        base = used[0]
        la = region(NT * T).rearrange("p (t k) -> p t k", t=NT)
        rope = arena[:, base:base + 2 * N].rearrange("p (a n) -> p a n", a=2)
        decays = region(2 * T + 32)
        up, down, small = decays[:, 0:T], decays[:, T:2 * T], decays[:, 2 * T:2 * T + 32]
        vtok = region(NT * 256).rearrange("p (t d) -> p t d", t=NT)
        ktok = region(NT * P).rearrange("p (t d) -> p t d", t=NT)
        carry = region(8 * 256).rearrange("p (n d) -> p n d", n=8)
        st = region(8 * 256).rearrange("p (n d) -> p n d", n=8)
        S = region(2 * 256).rearrange("p (n d) -> p n d", n=2)
        sdec = region(32)
        lah = raw[:, 4, 0:512].rearrange("p (t k) -> p t k", t=NT)
        sct = raw[:, 4, 512:1024].rearrange("p (t k) -> p t k", t=NT)
        kmask = arena[0:NB, t0_at + N:t0_at + N + 1024].rearrange("p (b k) -> p b k", b=NB)
        srow0 = tmp[0][0:NB, 0:384]
        used[0] = 512
        xin = region(5 * D).rearrange("p (t d) -> p t d", t=5)
        crow = region(D)
        rowa, rowb = region(P), region(P)
        csm = region(9 * KC)
        csm2 = region(9 * KC)
        wa2 = region(T)[0:RANK + 1, :]
        used[0] = base
        z = region(SB_ALL)
        za = region(SB_ALL)
        ktok1 = region(512).rearrange("p (t d) -> p t d", t=NT)
        vtok1 = region(512).rearrange("p (t d) -> p t d", t=NT)
        vntok = tmp[2][:, 0:T].rearrange("p (t d) -> p t d", t=NT)
        wst = region(P)
        ws = region(P)
        qb = za[:, 0:1024]
        pages = region(4 * 1024).rearrange("p (n d) -> p n d", n=4)
        srow = region(384)
        brow = mrow
        pair_a = arena[:, t0_at:t0_at + 2 * N]
        pair_b = arena[:, t0_at + 2 * N:t0_at + 4 * N]
        pair_c = arena[:, t0_at + 3 * N:t0_at + 5 * N]
        g01, g23, g45 = (arena[:, 512 + 2 * N * n:512 + 2 * N * n + 2 * N] for n in range(3))
        OS = region(64).rearrange("p (h b) -> p h b", h=HC)
        GS = region(64).rearrange("p (h b) -> p h b", h=HC)
        zs = region(128)
        zsa = region(128)
        dg = z[:, 0:1024]
        orow = z[0:NB, 0:1024]
        eps = sb("eps", [P, 1])
        vla = arena[:, 512:512 + 2048]
        sda = arena[:, 512 + 2048:512 + 2080]
        ptab = sb("ptab", [1, NB * NPAGE], I32)
        yrow = arena[0:NB, base:base + D]
        yo = [arena[:, base + D + 512 * n:base + D + 512 * n + 512] for n in range(2)]

        pt = [ctx.enter_context(nc.psum_tensor(f"pt{n}", [P, 2, 512], F32)) for n in range(2)]
        m012 = ctx.enter_context(nc.psum_tensor("m012", [P, 1536], F32))
        m3 = ctx.enter_context(nc.psum_tensor("m3", [P, 512], F32))
        M = [m012[:, 512 * n:512 * n + 512] for n in range(3)] + [m3[:, :]]

        ra_rows = G[0][0:RANK + 1, :]

        phases = {}
        have = [0] * 5
        for name, first, iters, order in (("ada0", U_ADA0, 12, [MOD] * 4), ("ra", U_RA, 1, [TILE]),
                                          ("l0", U_L0, 8, L0_ORDER), ("out0", U_OUT0, 8, OUT_ORDER),
                                          ("l1a", U_L1A, 4, L1A_ORDER), ("l1b", U_L1B, 8, L1B_ORDER),
                                          ("out1", U_OUT1, 8, OUT_ORDER)):
            units = 2 * len(order)
            slots = [L1B_SLOTS[u % 5] if name == "l1b" else (first + u) % 4 for u in range(units)]
            rank = [slots[:u].count(slots[u]) for u in range(units)]
            per = [slots.count(x) for x in range(5)]
            phases[name] = (first, units, slots, rank, per, list(have))
            have = [h + iters * p for h, p in zip(have, per)]

        def unit(name, i, u):
            first, units, slots, rank, per, before = phases[name]
            sl = slots[u]
            return first + i * units + u, sl, (i * per[sl] + (before[sl] + rank[u] + 1)) * 16

        class Chain:

            def __init__(self, eng, name):
                self.eng, self.name, self.base, self.at, self.n = eng, name, 0, 0, 0

            def body(self, i, first, per):
                self.at, self.n = self.base + (i - first) * per, 0

            def end(self, iters, per):
                assert self.n == per, (self.name, self.n)
                self.base += iters * per
                self.at, self.n = self.base, 0

            def __call__(self, ins):
                ins.then_inc(s(self.name), 1)
                self.n += 1
                self.eng.wait_ge(s(self.name), self.at + self.n)

            def straight(self):
                self.base, self.at, self.n = self.base + self.n, self.base + self.n, 0

        NCONST = len(CHIP) + 3 + 9 + 2 + 2
        block = ctx.enter_context(nc.Block())

        @block.sync
        def _(sp):
            def const(dst, src):
                sp.dma_start(dst, src).then_inc(s("const_in"), 16)

            const(crow[0:1, :], a["c_prompt"])
            const(crow[1:9, :], a["c_sample"])
            for k in CHIP:
                const(cm[k][:, :], cst[k])
            for n, src in enumerate((a["o_sb_offset"][0, :], a["o_w_s"][0, :, 0, 0], a["o_b_s"][0, :, 0])):
                with nc.allow_non_contiguous_dma(reason="eight scalars"):
                    const(per_head[:, n, :], src.partition_broadcast(P))
            const(rowa[0:48, :], a["e_b_ada"].rearrange("o (r c) -> (o r) c", c=P))
            const(rowa[48:96, :], a["o_b_ada"].rearrange("o (r c) -> (o r) c", c=P))
            at = 0
            for name, k in (("e_norm_g", 16), ("o_norm_g", 16), ("e_gla_norm_g", 8), ("e_ret_norm_g", 8),
                            ("o_v_norm_g", 8), ("o_q_norm_g", 1), ("o_k_norm_g", 1)):
                const(rowb[at:at + k, :], a[name].rearrange("o (r c) -> (o r) c", c=P))
                at += k
            const(wa2[0:RANK, :], a["e_w_a2"][0])
            const(wa2[RANK:RANK + 1, :], a["e_b_a"])
            for t in range(NT):
                sp.dma_start(xin[:, t, :], a["x_prompt"][0, P * t:P * t + P, :]).then_inc(s("x_in"), 16)
            sp.dma_start(xin[0:NB, 4, :], a["x_sample"].rearrange("b o d -> (b o) d")).then_inc(s("x_in"), 16)

            def load(name, i, u, src):
                n, sl, _ = unit(name, i, u)
                if not (isinstance(n, int) and n < RAW_DEPTH):
                    sp.wait_ge(s("split_hi"), n - (RAW_DEPTH - 1))
                    sp.wait_ge(s("split_lo"), n - (RAW_DEPTH - 1))
                sp.dma_start(raw[:, sl, :].rearrange("p (c n) -> p c n", c=src.shape[1]), src)\
                    .then_inc(s(f"raw{sl}"), 16)

            def load_tile(name, i, u, w, col):
                for hh in range(2):
                    load(name, i, u + hh, w[:, 8 * hh:8 * hh + 8, bass.ds(col, P)])

            def load_mod(name, i, u, w, col, pair):
                for hh in range(2):
                    k = 2 * (2 * pair + hh)
                    load(name, i, u + hh, w[:, k:k + 2, bass.ds(col, 512)])

            def weights(name, i, order, w_tile, tile_cols, w_mod=None, mod_col=None):
                t = m = 0
                for n, what in enumerate(order):
                    if what is TILE:
                        load_tile(name, i, 2 * n, w_tile, tile_cols[t])
                        t += 1
                    else:
                        load_mod(name, i, 2 * n, w_mod, mod_col, m)
                        m += 1

            v = {k: a[k][0].rearrange("(c p) n -> p c n", p=P)
                 for k in ("e_w_ada", "o_w_ada", "e_w_in", "o_w_in", "e_w_out", "o_w_out")}
            for u in range(4):
                load("ada0", 0, u, v["e_w_ada"][:, 2 * u:2 * u + 2, 0:512])
            for u in range(4, 8):
                load("ada0", 0, u, v["e_w_ada"][:, 2 * u:2 * u + 2, 0:512])
            with sp.Fori(1, 12) as g:
                weights("ada0", g, [MOD] * 4, None, None, v["e_w_ada"], g * 512)
            load_tile("ra", 0, 0, v["e_w_in"], E_RA)

            def gla_cols(i):
                return [i * 256 + E_VA, i * 256 + (E_VA + P), i * P + E_QA, i * P + E_KA,
                        i * 256 + E_GA, i * 256 + (E_GA + P)]

            def ret_cols(i):
                b = HEADS
                return [i * 256 + (E_VB - 256 * b), i * 256 + (E_VB + P - 256 * b), i * P + (E_QB - P * b),
                        i * P + (E_KB - P * b), i * 256 + (E_GB - 256 * b), i * 256 + (E_GB + P - 256 * b)]

            with sp.Fori(0, HEADS) as i:
                weights("l0", i, L0_ORDER, v["e_w_in"], gla_cols(i), v["o_w_ada"], i * 512)
            with sp.Fori(HEADS, 2 * HEADS) as i:
                weights("l0", i, L0_ORDER, v["e_w_in"], ret_cols(i), v["o_w_ada"], i * 512)
            with sp.Fori(0, 8) as j:
                weights("out0", j, OUT_ORDER, v["e_w_out"], [j * 256, j * 256 + P])
            with sp.Fori(0, 4) as j:
                weights("l1a", j, L1A_ORDER, v["o_w_in"],
                        [j * 256 + O_Q, j * 256 + (O_Q + P), j * 256 + O_VD, j * 256 + (O_VD + P)],
                        v["o_w_ada"], j * 512 + 2 * D)
            with sp.Fori(0, 8) as i:
                weights("l1b", i, L1B_ORDER, v["o_w_in"], [i * P + c for c in (O_K, O_V, O_G, O_U, O_GD)])
            with sp.Fori(0, 8) as j:
                weights("out1", j, OUT_ORDER, v["o_w_out"], [j * 256, j * 256 + P])

        @block.tensor
        def _(pe):
            def mm(out, lhsT, rhs, start=True, stop=True):
                return pe.matmul(out, lhsT, rhs, start=start, stop=stop, skip_group_check=True)

            def tr(out, x):
                k = x.shape[0]
                return pe.transpose(out, x, ident[0:k, 0:k])

            def unit_ready(name, i, u):
                n, _, _ = unit(name, i, u)
                pe.wait_ge(s("split_hi"), n + 1)
                pe.wait_ge(s("split_lo"), n + 1)
                return (phases[name][0] + u) % 2

            def tile(name, i, u, n_tile, par, stage, late=0):
                pe.wait_ge(s("evac"), n_tile - 1 + late)
                for hh in range(2):
                    b = unit_ready(name, i, u + hh)
                    for k in range(8):
                        c = 8 * hh + k
                        if stage is not None:
                            pe.wait_ge(s("act_ready"), 16 * stage + c + 1)
                        hi, lo = w_hi[:, b, P * k:P * k + P], w_lo[:, b, P * k:P * k + P]
                        for w, x in ((hi, act_hi), (hi, act_lo), (lo, act_hi)):
                            for h in range(2):
                                last = mm(pt[par][:, h, 0:HALF], w, x[:, c, HALF * h:HALF * h + HALF],
                                          start=(c == 0 and w is hi and x is act_hi), stop=(c == 15 and w is lo))
                    last.then_inc(s("pe_unit"), 1)
                return last

            def mod_pair(name, i, u, pair):
                for hh in range(2):
                    b = unit_ready(name, i, u + hh)
                    for k in range(2):
                        c = 2 * (2 * pair + hh) + k
                        for w in (w_hi, w_lo):
                            last = mm(M[3][0:66, :], cond[:, c, :], w[:, b, 512 * k:512 * k + 512],
                                      start=(c == 0 and w is w_hi), stop=(c == 15 and w is w_lo))
                    last.then_inc(s("pe_unit"), 1)
                return last

            def mod_fold(g):
                pe.wait_ge(s("mod_row"), g + 1)
                for j in range(4):
                    last = mm(M[2][:, 9 * j:9 * j + 9],
                              mrow[0:18, P * j:P * j + P], cm["fold"][:, :])
                last.then_inc(s("mod_col"), 1)

            def run(name, i, order, tile0, par0, stage, group=None, late0=0, first_stage=False):
                t = m = 0
                for n, what in enumerate(order):
                    if what is TILE:
                        tile(name, i, 2 * n, tile0 + t, (par0 + t) % 2, stage if t == 0 else None,
                             late0 if t == 0 else 0)
                        t += 1
                    else:
                        if m == 0:
                            pe.wait_ge(s("mod_read"), group)
                        last = mod_pair(name, i, 2 * n, m)
                        m += 1
                        if m == 4:
                            mod_fold(group)

            pe.wait_ge(s("const_in"), 16 * NCONST)
            tr(M[0][:, 0:96], rowa[0:96, :])
            tr(M[0][:, 96:154], rowb[0:58, :]).then_inc(s("cols_t"), 1)
            for k in range(KC):
                last = tr(M[1][:, 9 * k:9 * k + 9], crow[0:9, P * k:P * k + P])
            last.then_inc(s("cond_t"), 1)
            pe.wait_ge(s("x_in"), 80)
            pe.wait_ge(s("cols"), 1)
            pe.wait_ge(s("cond_cols"), 1)
            for c in range(KC):
                b = c % 2
                if c >= 2:
                    pe.wait_ge(s("xt_a"), c - 1)
                    pe.wait_ge(s("xt_s"), c - 1)
                for t in range(NT):
                    tr(M[b][:, P * t:P * t + P], xin[:, t, P * c:P * c + P])
                tr(M[2 + b][:, 0:8], xin[0:NB, 4, P * c:P * c + P]).then_inc(s("xt"), 1)
            pe.wait_ge(s("cond"), 1)
            run("ada0", 0, [MOD] * 4, None, None, None, 0)
            with pe.Fori(1, 12) as g:
                run("ada0", g, [MOD] * 4, None, None, None, g)

            def feature_sum(src, big, small_, done):
                mm(big, ones[:, :], src[:, 0:T])
                mm(small_, ones[:, :], src[:, T:N]).then_inc(s(done), 1)

            pe.wait_ge(s("x_sq"), 1)
            feature_sum(tmp[0], M[0], M[1][:, 0:8], "x_ss")
            tile("ra", 0, 0, 1, 0, 0)
            pe.wait_ge(s("ra"), 1)
            for t in range(NT):
                mm(M[t], ra_rows[:, P * t:P * t + P], wa2)
            mm_s = [mm(pt[1][:, 0, 8 * h:8 * h + 8], wa2[:, P * h:P * h + P], ra_rows[:, T:N])
                    for h in range(HEADS)]
            mm_s[-1].then_inc(s("la_x"), 1)
            pe.wait_ge(s("la"), 1)

            def mix0(i, gla):
                if gla:
                    pe.wait_ge(s("lah"), i + 1)
                    for t in range(NT):
                        mm(M[0][:, P * t:P * t + P], lah[:, t, :], cm["cum_mid"][:, :])
                        last = mm(M[1][:, 6 * t:6 * t + 6], lah[:, t, :], cm["cum_small"][:, :])
                    last.then_inc(s("cum"), 1)
                else:
                    pe.wait_ge(s("evac"), T_L0 + 6 * i + 4)
                    mm(M[0], cm["swap"][:, :], G[2][:, 0:T])
                    mm(M[1], cm["swap"][:, :], G[3][:, 0:T])
                    mm(M[2][:, 0:8], cm["swap"][:, :], G[2][:, T:N])
                    mm(M[2][:, 8:16], cm["swap"][:, :], G[3][:, T:N]).then_inc(s("swapped"), 1)
                    pe.wait_ge(s("rotated"), i + (1 - HEADS))
                pe.wait_ge(s("evac"), T_L0 + 6 * i + 6)
                for t in range(NT):
                    for d in range(2):
                        last = tr(M[2 + t // 2][:, 256 * (t % 2) + P * d:256 * (t % 2) + P * d + P],
                                  G[d][:, P * t:P * t + P])
                last.then_inc(s("v_t"), 1)
                pe.wait_ge(s("qk"), i + 1)
                for t in range(NT):
                    tr(M[0][:, P * t:P * t + P], G[3][:, P * t:P * t + P])
                tr(M[1][0:NB, 0:P], G[3][:, T:N])
                tr(M[1][0:NB, P:2 * P], G[0][:, T:N])
                tr(M[1][0:NB, 2 * P:3 * P], G[1][:, T:N]).then_inc(s("k_t"), 1)
                pe.wait_ge(s("vtok"), i + 1)
                for t in range(NT):
                    last = mm(M[2][:, P * t:P * t + P], G[3][:, P * t:P * t + P], G[2][:, P * t:P * t + P])
                last.then_inc(s("sc"), 1)
                pe.wait_ge(s("ktok"), i + 1)
                pe.wait_ge(s("srow0"), i + 1)
                for n in range(NCH):
                    if n == 4:
                        pe.wait_ge(s("s_step"), 8 * i + 4)
                    r = CH * (n % 2)
                    last = mm(M[n % 2][:, 128 * (n % 4 - n % 2):128 * (n % 4 - n % 2) + 256],
                              ktok[r:r + CH, n // 2, :], vtok[r:r + CH, n // 2, :])
                    if n % 4 == 3:
                        last.then_inc(s("kv"), 1)
                pe.wait_ge(s("kmask"), i + 1)
                for b in range(NB):
                    if b == 0:
                        pe.wait_ge(s("s_step"), 8 * i + 8)
                    if b >= 4 and b % 2 == 0:
                        pe.wait_ge(s("st_step"), 8 * i + b - 2)
                    last = mm(M[(b // 2) % 2][:, 256 * (b % 2):256 * (b % 2) + 256], kmask[:, b, :], srow0[:, P:3 * P])
                    if b % 2:
                        last.then_inc(s("outer"), 1)
                pe.wait_ge(s("sct"), i + 1)
                pe.wait_ge(s("carry"), 7 * i + 7)
                for d in range(2):
                    for t in range(NT):
                        mm(M[2 + d][:, P * t:P * t + P], vtok[:, t, P * d:P * d + P], sct[:, t, :],
                           start=True, stop=False)
                        for n in (2 * t, 2 * t + 1):
                            if n:
                                last = mm(M[2 + d][:, CH * n:CH * n + CH], carry[:, n, P * d:P * d + P],
                                          G[2][:, CH * n:CH * n + CH], start=False, stop=True)
                last.then_inc(s("o"), 1)
                pe.wait_ge(s("st_step"), 8 * i + 8)
                for d in range(2):
                    for b in range(NB):
                        last = mm(M[0][:, 8 * d + b:8 * d + b + 1], st[:, b, P * d:P * d + P], G[2][:, T + b:T + b + 1])
                last.then_inc(s("os"), 1)
                pe.wait_ge(s("osq"), i + 1)
                feature_sum(tmp[2], M[0], M[1][:, 0:8], "oss")

            with pe.Fori(0, HEADS) as i:
                run("l0", i, L0_ORDER, i * 6 + T_L0, 1, None, i + 12)
                mix0(i, True)
            with pe.Fori(HEADS, 2 * HEADS) as i:
                run("l0", i, L0_ORDER, i * 6 + T_L0, 1, None, i + 12)
                mix0(i, False)
            pe.wait_ge(s("act_ready"), 32)
            with pe.Fori(0, 8) as j:
                run("out0", j, OUT_ORDER, j * 2 + T_OUT0, T_OUT0 % 2, None)
            pe.wait_ge(s("x_sq"), 2)
            feature_sum(tmp[0], M[0], M[1][:, 0:8], "x_ss")
            pe.wait_ge(s("act_ready"), 48)

            def l1a(j):
                run("l1a", j, L1A_ORDER, j * 4 + T_L1A, T_L1A % 2, None, j + 20)
                pe.wait_ge(s("q_sq"), j + 1)
                for t in range(2):
                    mm(M[t], ones[:, :], tmp[t][:, 0:T])
                    last = mm(M[3][:, 8 * t:8 * t + 8], ones[:, :], tmp[t][:, T:N])
                last.then_inc(s("q_ss"), 1)
                pe.wait_ge(s("q_rs"), j + 1)

            with pe.Fori(0, 4) as j:
                l1a(j)
            pe.wait_ge(s("vd_sq"), 4)
            feature_sum(tmp[4], M[0], M[1][:, 0:8], "vd_ss")

            def mix1(i):
                pe.wait_ge(s("k_sq"), i + 1)
                feature_sum(tmp[0], M[0], M[1][:, 0:8], "k_ss")
                pe.wait_ge(s("kn"), i + 1)
                pe.wait_ge(s("ws_in"), 32 * i + 32)
                for t in range(NT):
                    tr(M[2][:, P * t:P * t + P], G[0][:, P * t:P * t + P])
                    tr(M[3][:, P * t:P * t + P], G[1][:, P * t:P * t + P])
                    tr(M[0][:, P * t:P * t + P], tmp[2][:, P * t:P * t + P])
                tr(M[1][0:NB, 0:P], G[0][:, T:N])
                tr(M[1][0:NB, P:2 * P], G[1][:, T:N])
                tr(M[1][0:NB, 2 * P:3 * P], tmp[2][:, T:N])
                tr(M[1][:, 384:512], ws).then_inc(s("tok_t"), 1)
                pe.wait_ge(s("tok_a"), i + 1)
                pe.wait_ge(s("tok_v"), i + 1)
                for t in range(NT):
                    mm(M[3][:, P * t:P * t + P], vntok[:, t, :], wst, start=True, stop=False)
                    last = mm(M[3][:, P * t:P * t + P], ones[0:1, :], brow[0:1, 0:P], start=False, stop=True)
                last.then_inc(s("sg"), 1)
                for b in range(NT):
                    last = mm(m012[:, SB_OFF[b]:SB_OFF[b] + T - P * b], G[0][:, P * b:P * b + P],
                              tmp[1][:, P * b:T])
                last.then_inc(s("z"), 1)
                pe.wait_ge(s("rest"), i + 1)
                for b in range(NT):
                    off = SB_OFF[b]
                    last = mm(m012[:, off:off + T - P * b], cm["from_key"][:, :], za[:, off:off + T - P * b],
                              start=True, stop=(b == 3))
                    for l in range(b + 1, NT):
                        last = mm(m012[:, off + P * (l - b):off + T - P * b], ones[:, :],
                                  za[:, SB_OFF[l]:SB_OFF[l] + T - P * l], start=False, stop=(l == 3))
                last.then_inc(s("between"), 1)
                pe.wait_ge(s("weight"), i + 1)
                for b in range(NT):
                    last = mm(M[3][:, P * b:T], vtok1[:, b, :], za[:, SB_OFF[b]:SB_OFF[b] + T - P * b],
                              start=(b == 0), stop=(b == 3))
                last.then_inc(s("oc"), 1)
                pe.wait_ge(s("dg"), i + 1)
                for h in range(2):
                    last = mm(M[h], ones[:, :], dg[:, 512 * h:512 * h + 512])
                last.then_inc(s("qb_t"), 1)
                pe.wait_ge(s("s_rest"), i + 1)
                mm(M[3][:, 0:128], cm["from_key"][:, :], zsa, start=True, stop=False)
                for j in range(1, NPAGE):
                    last = mm(M[3][:, 0:128 - 8 * j], ones[:, :], zsa[:, 8 * j:128], start=False, stop=(j == 15))
                last.then_inc(s("s_between"), 1)
                pe.wait_ge(s("s_weight"), i + 1)
                for p in range(NPAGE):
                    pe.wait_ge(s(f"page{p % 4}"), (i * 8 + 4 + p // 4 + 1) * 16)
                    for h in range(2):
                        last = mm(M[h][0:NB, :], zs[:, 8 * p:8 * p + 8], pages[:, p % 4, 512 * h:512 * h + 512],
                                  start=(p == 0), stop=(p == NPAGE - 1))
                    last.then_inc(s("v_free"), 1)
                pe.wait_ge(s("orow"), i + 1)
                for h in range(HC):
                    last = mm(M[2][:, h:h + 1], orow[:, P * h:P * h + P], ident[0:NB, h:h + 1])
                last.then_inc(s("os1"), 1)
                pe.wait_ge(s("mixed1"), i + 1)

            with pe.Fori(0, 8) as i:
                run("l1b", i, L1B_ORDER, i * 5 + T_L1B, T_L1B % 2, None, late0=1)
                mix1(i)
            pe.wait_ge(s("act_ready"), 64)
            with pe.Fori(0, 8) as j:
                for t in range(2):
                    tile("out1", j, 2 * t, j * 2 + (T_OUT1 + t), t, None)
                    pe.wait_ge(s("evac"), 2 * j + (T_OUT1 + t + 1))
                    y = G[2 + t]
                    for q in range(NT):
                        tr(M[t][:, P * q:P * q + P], y[:, P * q:P * q + P])
                    tr(M[2][0:NB, P * t:P * t + P], y[:, T:N]).then_inc(s("y1_t"), 1)

        @block.scalar
        def _(act):
            step = Chain(act, "act_step")

            def f(out, x, fn, **kw):
                return act.activation(out, x, fn, **kw)

            def hi(name, i, units):
                for u in units:
                    n, sl, loaded = unit(name, i, u)
                    act.wait_ge(s(f"raw{sl}"), loaded)
                    if not (isinstance(n, int) and n < 2):
                        act.wait_ge(s("pe_unit"), n - 1)
                    f(w_hi[:, (phases[name][0] + u) % 2, :], raw[:, sl, :], ACT.Copy).then_inc(s("split_hi"), 1)

            def sigmoid(x):
                step(f(x, x, ACT.Exp, scale=-1.0))
                step(f(x, x, ACT.Ln, bias=1.0))
                return f(x, x, ACT.Exp, scale=-1.0)

            def rstd(dst, big, small_, width):
                f(dst[:, 0:T], big, ACT.Ln, scale=1.0 / width, bias=eps[:, 0:1])
                step(f(dst[:, T:N], small_, ACT.Ln, scale=1.0 / width, bias=eps[:, 0:1]))
                return f(dst, dst, ACT.Exp, scale=-0.5)

            def squares(k):
                for c in range(KC):
                    if c >= 2:
                        act.wait_ge(s("x_acc"), 16 * k + c - 1)
                    f(tmp[1 + c % 2], wide[:, c, :], ACT.Square).then_inc(s("x_sqc"), 1)
                act.wait_ge(s("x_ss"), k + 1)
                rstd(tmp[0], M[0], M[1][:, 0:8], D).then_inc(s("x_rs"), 1)

            def norm(k, stage):
                act.wait_ge(s("mod_scale"), k + 1)
                for c in range(KC):
                    act.wait_ge(s("n_t"), 16 * k + c + 1)
                    f(tmp[3 + c % 2][:, 0:T], tmp[1 + c % 2][:, 0:T], ACT.Identity,
                      scale=mod[k][:, 16 + c, 0:1], bias=mod[k][:, c, 0:1]).then_inc(s("n_a"), 1)
                    act.wait_ge(s("n_a"), 16 * k + c + 1)
                    act.wait_ge(s("n_s"), 16 * k + c + 1)
                    f(act_hi[:, c, :], tmp[3 + c % 2], ACT.Copy).then_inc(s("act_hi"), 1)

            def take_mixed(stage):
                for c in range(KC):
                    f(act_hi[:, c, :], wide[:, c, :], ACT.Copy).then_inc(s("act_hi"), 1)

            act.preload_act_table_set("natural_log_exp_and_others")
            act.wait_ge(s("cond_cols"), 1)
            sigmoid(csm2).then_inc(s("cond_sig"), 1)
            act.wait_ge(s("cond_v"), 1)
            f(cond[:, :, 0:9], csm.rearrange("p (c n) -> p c n", n=9), ACT.Copy).then_inc(s("cond_hi"), 1)
            for c in range(KC):
                act.wait_ge(s("xt"), c + 1)
                f(wide[:, c, 0:T], M[c % 2], ACT.Copy).then_inc(s("xt_a"), 1)
            hi("ada0", 0, range(8))
            step.straight()
            with act.Fori(1, 12) as g:
                hi("ada0", g, range(8))
            act.wait_ge(s("xt_s"), KC)
            squares(0)
            norm(0, 0)
            hi("ra", 0, range(2))
            act.wait_ge(s("la_abs"), 1)
            step(f(vla, vla, ACT.Exp, scale=-1.0))
            f(vla, vla, ACT.Ln, bias=1.0)
            step(f(sda, sda, ACT.Exp, scale=-1.0))
            f(sda, sda, ACT.Ln, bias=1.0).then_inc(s("la_l"), 1)
            act.wait_ge(s("sd"), 1)
            f(sdec, sdec, ACT.Exp, scale=1.0 / 16.0).then_inc(s("sdec"), 1)
            act.wait_ge(s("sdec"), 1)
            act.wait_ge(s("la"), 1)
            step.straight()

            def mix0(i, gla):
                if gla:
                    f(lah, la[:, :, bass.ds(i * P, P)], ACT.Copy).then_inc(s("lah"), 1)
                    act.wait_ge(s("cum"), i + 1)
                    f(up, M[0], ACT.Exp)
                    f(down, M[0], ACT.Exp, scale=-1.0)
                    f(small[:, 0:24], M[1][:, 0:24], ACT.Exp)
                    f(small[:, 24:32], sdec[:, bass.ds(i * NB, NB)], ACT.Copy).then_inc(s("decay"), 1)
                act.wait_ge(s("v_t"), i + 1)
                f(vtok[:, 0:2, :], M[2].rearrange("p (t d) -> p t d", t=2), ACT.Copy)
                f(vtok[:, 2:4, :], M[3].rearrange("p (t d) -> p t d", t=2), ACT.Copy).then_inc(s("vtok"), 1)
                act.wait_ge(s("k_t"), i + 1)
                f(ktok, M[0].rearrange("p (t d) -> p t d", t=NT), ACT.Copy).then_inc(s("ktok"), 1)
                act.wait_ge(s("g_clamp"), i + 1)
                sigmoid(g01).then_inc(s("g_sig"), 1)
                act.wait_ge(s("o"), i + 1)
                f(tmp[0][:, 0:T], M[2], ACT.Copy)
                f(tmp[1][:, 0:T], M[3], ACT.Copy).then_inc(s("o_a"), 1)
                act.wait_ge(s("o_a"), i + 1)
                act.wait_ge(s("o_s"), i + 1)
                f(pair_b, pair_a, ACT.Square).then_inc(s("o_sq"), 1)
                act.wait_ge(s("oss"), i + 1)
                rstd(tmp[3], M[0], M[1][:, 0:8], 256.0).then_inc(s("o_rs"), 1)

            for first, gla in ((0, True), (HEADS, False)):
                with act.Fori(first, first + HEADS) as i:
                    step.body(i, first, 3)
                    hi("l0", i, range(20))
                    mix0(i, gla)
                step.end(HEADS, 3)
            act.wait_ge(s("mixed"), 16)
            take_mixed(1)
            with act.Fori(0, 8) as j:
                hi("out0", j, range(4))
            act.wait_ge(s("evac"), T_OUT0 + 16)
            squares(1)
            norm(1, 2)
            step.straight()

            with act.Fori(0, 4) as j:
                step.body(j, 0, 3)
                hi("l1a", j, range(16))
                act.wait_ge(s("evac"), 4 * j + T_L1A + 4)
                f(pair_a, g01, ACT.Square).then_inc(s("q_sq"), 1)
                f(pair_b, g23, ACT.Square).then_inc(s("vd_x2"), 1)
                act.wait_ge(s("q_ss"), j + 1)
                for t in range(2):
                    f(tmp[t][:, 0:T], M[t], ACT.Ln, scale=1.0 / DH, bias=eps[:, 0:1])
                    last = f(tmp[t][:, T:N], M[3][:, 8 * t:8 * t + 8], ACT.Ln, scale=1.0 / DH, bias=eps[:, 0:1])
                step(last)
                f(pair_a, pair_a, ACT.Exp, scale=-0.5).then_inc(s("q_rs"), 1)
                act.wait_ge(s("vd_u"), j + 1)
                sigmoid(pair_b).then_inc(s("vd_sig"), 1)
                act.wait_ge(s("vd_g"), j + 1)
                f(pair_b, g23, ACT.Square).then_inc(s("vd_g2"), 1)
            step.end(4, 3)
            act.wait_ge(s("vd_ss"), 1)
            rstd(G[5], M[0], M[1][:, 0:8], BR).then_inc(s("rv"), 1)
            step.straight()

            kp_out = a["k_prompt_out"]
            with act.Fori(0, 8) as i:
                step.body(i, 0, 7)
                hi("l1b", i, range(10))
                act.wait_ge(s("evac"), 5 * i + T_L1B + 5)
                f(tmp[0], G[0], ACT.Square).then_inc(s("k_sq"), 1)
                act.wait_ge(s("k_ss"), i + 1)
                rstd(tmp[0], M[0], M[1][:, 0:8], DH).then_inc(s("k_rs"), 1)
                act.wait_ge(s("g1_clamp"), i + 1)
                sigmoid(pair_c).then_inc(s("g1_sig"), 1)
                act.wait_ge(s("tok_t"), i + 1)
                act.wait_ge(s("kv_out"), 64 * i)
                f(ktok1, M[2].rearrange("p (t d) -> p t d", t=NT), ACT.Copy)
                f(vtok1, M[3].rearrange("p (t d) -> p t d", t=NT), ACT.Copy).then_inc(s("tok_a"), 1)
                act.wait_ge(s("tok_a"), i + 1)
                act.wait_ge(s("tok_v"), i + 1)
                for n, (src, big, small_) in enumerate(((ktok1, kp_out, a["k_sample_out"]),
                                                       (vtok1, a["v_prompt_out"], a["v_sample_out"]))):
                    act.dma_start(big[0, 0].rearrange("(t p) h d -> p t h d", p=P)[:, :, bass.ds(i, 1), :]
                                  .rearrange("p t h d -> p t (h d)"), src).then_inc(s("kv_out"), 16)
                    act.dma_start(small_[0, :, 0, bass.ds(i, 1), :].rearrange("b h d -> b (h d)"),
                                  srow[0:NB, P * n:P * n + P]).then_inc(s("kv_out"), 16)
                act.dma_start(a["chunk_v_out"][0, :, 0, bass.ds(i * P, P)],
                              srow[0:NB, 2 * P:3 * P]).then_inc(s("cv_out"), 16)
                f(tmp[0], G[3], ACT.Square).then_inc(s("u_x2"), 1)
                act.wait_ge(s("u_u"), i + 1)
                sigmoid(tmp[0]).then_inc(s("u_sig"), 1)
                act.wait_ge(s("z_abs"), i + 1)
                step(f(za, za, ACT.Exp, scale=-1.0))
                f(za, za, ACT.Ln, bias=1.0).then_inc(s("z_l"), 1)
                act.wait_ge(s("lw"), i + 1)
                f(za, z, ACT.Exp).then_inc(s("w_e"), 1)
                act.wait_ge(s("qb_t"), i + 1)
                f(qb, m012[:, 0:1024], ACT.Copy).then_inc(s("qb"), 1)
                act.wait_ge(s("zs_abs"), i + 1)
                step(f(zsa, zsa, ACT.Exp, scale=-1.0))
                f(zsa, zsa, ACT.Ln, bias=1.0).then_inc(s("zs_l"), 1)
                act.wait_ge(s("s_lw"), i + 1)
                f(zs, zs, ACT.Exp).then_inc(s("s_weight"), 1)
            step.end(8, 7)
            act.wait_ge(s("mixed1_all"), 1)
            take_mixed(3)
            act.wait_ge(s("kv_out"), 64 * HC)
            with act.Fori(0, 8) as j:
                hi("out1", j, range(4))
                for t in range(2):
                    act.wait_ge(s("y1_t"), 2 * j + t + 1)
                    act.wait_ge(s("y_out"), 32 * j)
                    f(yo[t], M[t], ACT.Copy).then_inc(s("yo"), 1)

        @block.vector
        def _(dve):
            step = Chain(dve, "dve_step")
            tt, ts_, stt, copy = dve.tensor_tensor, dve.tensor_scalar, dve.scalar_tensor_tensor, dve.tensor_copy

            def lo(name, i, units):
                for u in units:
                    n, sl, _ = unit(name, i, u)
                    dve.wait_ge(s("split_hi"), n + 1)
                    if not (isinstance(n, int) and n < 2):
                        dve.wait_ge(s("pe_unit"), n - 1)
                    b = (phases[name][0] + u) % 2
                    tt(w_lo[:, b, :], raw[:, sl, :], w_hi[:, b, :].bitcast(F32), ALU.subtract)\
                        .then_inc(s("split_lo"), 1)

            def halves(x):
                return x.rearrange("p (a n) -> p a n", a=2)

            def mod_read(g, layer, col, products):
                dve.wait_ge(s("pe_unit"), products)
                copy(mrow[0:18, :], M[3][0:18, :]).then_inc(s("mod_row"), 1)
                dve.wait_ge(s("mod_col"), g + 1)
                tt(mod[layer][:, bass.ds(col, 4), :], M[2][:, 0:36].rearrange("p (j n) -> p j n", j=4),
                   cols[:, bass.ds(col + C_BADA[layer], 4)].unsqueeze(2).to_broadcast([P, 4, 9]),
                   ALU.add).then_inc(s("mod_read"), 1)

            def run(name, i, order, n_tile0, par0, evac, group=None, layer=None, col=None):
                t = m = 0
                todo = []
                for n, what in enumerate(order + [None]):
                    if what is not None:
                        lo(name, i, (2 * n, 2 * n + 1))
                    if todo:
                        kind, k, done = todo.pop()
                        if kind is TILE:
                            dve.wait_ge(s("pe_unit"), done)
                            evac(k, halves_of(pt[(par0 + k) % 2])).then_inc(s("evac"), 1)
                        elif k == 3:
                            mod_read(group, layer, col, done)
                    if what is TILE:
                        todo.append((TILE, t, unit(name, i, 2 * n + 1)[0] + 1))
                        t += 1
                    elif what is MOD:
                        todo.append((MOD, m, unit(name, i, 2 * n + 1)[0] + 1))
                        m += 1

            def halves_of(x):
                return x[:, :, 0:HALF]

            def squares(k):
                dve.wait_ge(s("x_sqc"), 16 * k + 1)
                copy(tmp[0], tmp[1]).then_inc(s("x_acc"), 1)
                for c in range(1, KC):
                    dve.wait_ge(s("x_sqc"), 16 * k + c + 1)
                    dve.wait_ge(s("x_acc"), 16 * k + c)
                    tt(tmp[0], tmp[0], tmp[1 + c % 2], ALU.add).then_inc(s("x_acc"), 1)
                dve.wait_ge(s("x_acc"), 16 * k + 16)
                dve.engine_nop().then_inc(s("x_sq"), 1)
                g = cols[:, C_NORM[k]:C_NORM[k] + 16].unsqueeze(2).to_broadcast([P, 16, 9])
                stt(mod[k][:, 16:32, :], mod[k][:, 16:32, :], 1.0, g, ALU.add, ALU.mult)\
                    .then_inc(s("mod_scale"), 1)
                dve.wait_ge(s("mod_scale"), k + 1)

            def norm(k):
                dve.wait_ge(s("x_rs"), k + 1)
                for c in range(KC):
                    b = c % 2
                    if c >= 2:
                        dve.wait_ge(s("n_a"), 16 * k + c - 1)
                    tt(tmp[1 + b], wide[:, c, :], tmp[0], ALU.mult).then_inc(s("n_t"), 1)
                    dve.wait_ge(s("n_t"), 16 * k + c + 1)
                    x = tmp[3 + b][:, T:N]
                    if c >= 2:
                        dve.wait_ge(s("act_ready"), 32 * k + c - 1)
                    step(tt(x, tmp[1 + b][:, T:N], mod[k][:, 16 + c, 1:9], ALU.mult))
                    tt(x, x, mod[k][:, c, 1:9], ALU.add).then_inc(s("n_s"), 1)
                    dve.wait_ge(s("act_hi"), 32 * k + c + 1)
                    tt(act_lo[:, c, :], tmp[3 + b], act_hi[:, c, :].bitcast(F32), ALU.subtract)\
                        .then_inc(s("act_ready"), 1)

            def take_mixed(stage):
                for c in range(KC):
                    dve.wait_ge(s("act_hi"), 16 * stage + c + 1)
                    tt(act_lo[:, c, :], wide[:, c, :], act_hi[:, c, :].bitcast(F32), ALU.subtract)\
                        .then_inc(s("act_ready"), 1)

            dve.memset(eps[:, :], EPS)
            dve.memset(cond[:, :, :].bitcast(I32), 0)
            dve.memset(ones[:, :], 1.0).then_inc(s("ones"), 1)
            dve.wait_ge(s("ones"), 1)
            dve.wait_ge(s("cols_t"), 1)
            copy(cols[:, :], M[0][:, 0:154]).then_inc(s("cols"), 1)
            dve.wait_ge(s("cond_t"), 1)
            step(copy(csm, M[1][:, 0:144]))
            ts_(csm2, csm, -40.0, None, ALU.max).then_inc(s("cond_cols"), 1)
            dve.wait_ge(s("cond_sig"), 1)
            tt(csm, csm, csm2, ALU.mult).then_inc(s("cond_v"), 1)
            dve.wait_ge(s("cond_hi"), 1)
            tt(cond[:, :, 9:18], csm.rearrange("p (c n) -> p c n", n=9), cond[:, :, 0:9].bitcast(F32),
               ALU.subtract).then_inc(s("cond"), 1)
            for c in range(KC):
                dve.wait_ge(s("xt"), c + 1)
                copy(wide[:, c, T:N], M[2 + c % 2][:, 0:8]).then_inc(s("xt_s"), 1)
            run("ada0", 0, [MOD] * 4, None, 0, None, 0, 0, 0)
            step.straight()
            with dve.Fori(1, 12) as g:
                run("ada0", g, [MOD] * 4, None, 0, None, g, 0, g * 4)
            squares(0)
            norm(0)
            step(dve.memset(ra_rows, 1.0))
            run("ra", 0, [TILE], 0, 0, lambda k, x: copy(G[0][0:RANK, :].rearrange("p (a n) -> p a n", a=2),
                                                        x[0:RANK]))
            dve.wait_ge(s("evac"), 1)
            dve.engine_nop().then_inc(s("ra"), 1)
            dve.wait_ge(s("la_x"), 1)
            for t in range(NT):
                copy(la[:, t, :], M[t])
            step(copy(sdec, pt[1][:, 0, 0:32]))
            laf = la.rearrange("p t k -> p (t k)")
            stt(vla, laf, -1.0, laf, ALU.mult, ALU.max)
            stt(sda, sdec, -1.0, sdec, ALU.mult, ALU.max).then_inc(s("la_abs"), 1)
            dve.wait_ge(s("la_l"), 1)
            stt(laf, laf, 0.0, vla, ALU.min, ALU.subtract).then_inc(s("la"), 1)
            stt(sdec, sdec, 0.0, sda, ALU.min, ALU.subtract).then_inc(s("sd"), 1)
            dve.wait_ge(s("sd"), 1)
            step.straight()

            def evac0(k, x):
                d = G[k].rearrange("p (a n) -> p a n", a=2)
                return ts_(d, x, SCALE, None, ALU.mult) if k == 2 else copy(d, x)

            def mix0(i, gla):
                if gla:
                    dve.wait_ge(s("decay"), i + 1)
                else:
                    dve.wait_ge(s("ret_in"), i * 16 + (16 - 16 * HEADS))
                    dve.wait_ge(s("rope_in"), 16)
                    dve.wait_ge(s("swapped"), i + (1 - HEADS))
                    for k in range(2):
                        tt(tmp[k][:, 0:T], M[k], rope[:, 1, 0:T], ALU.mult)
                        tt(tmp[k][:, T:N], M[2][:, 8 * k:8 * k + 8], rope[:, 1, T:N], ALU.mult)
                        step(tt(G[2 + k], G[2 + k], rope[:, 0, :], ALU.mult))
                    tt(g23, g23, pair_a, ALU.add).then_inc(s("rotated"), 1)
                    dve.wait_ge(s("rotated"), i + (1 - HEADS))
                tt(G[2][:, 0:T], G[2][:, 0:T], up, ALU.mult)
                tt(G[3][:, 0:T], G[3][:, 0:T], down, ALU.mult).then_inc(s("qk"), 1)
                dve.wait_ge(s("k_t"), i + 1)
                ts_(g01, g45, -40.0, None, ALU.max).then_inc(s("g_clamp"), 1)
                copy(srow0, M[1][0:NB, 0:384]).then_inc(s("srow0"), 1)
                dve.wait_ge(s("srow0"), i + 1)
                tt(kmask, srow0[:, 0:P].unsqueeze(1).to_broadcast([NB, NB, P]),
                   ident[0:NB, 0:NB].unsqueeze(2).to_broadcast([NB, NB, P]), ALU.mult).then_inc(s("kmask"), 1)
                dve.wait_ge(s("sc"), i + 1)
                stt(sct, M[2].rearrange("p (t k) -> p t k", t=NT), BIG,
                    cm["chunk_mask"][:, :].unsqueeze(1).to_broadcast([P, NT, P]), ALU.min, ALU.mult)\
                    .then_inc(s("sct"), 1)
                for n in range(NCH):
                    at = 6 * (n // 2) + n % 2
                    if n % 4 == 0:
                        dve.wait_ge(s("kv"), 2 * i + n // 4 + 1)
                    kv = M[n % 2][:, 128 * (n % 4 - n % 2):128 * (n % 4 - n % 2) + 256]
                    if n == 0:
                        ts_(S[:, 0, :], kv, small[:, at + 4:at + 5], None, ALU.mult).then_inc(s("s_step"), 1)
                    else:
                        step(ts_(tmp[4][:, 0:256], kv, small[:, at + 4:at + 5], None, ALU.mult))
                        if n >= 2:
                            dve.wait_ge(s("carry"), 7 * i + n - 1)
                        elif n == 1:
                            dve.wait_ge(s("s_out"), 16 * i)
                        stt(S[:, n % 2, :], S[:, (n - 1) % 2, :], small[:, at + 2:at + 3], tmp[4][:, 0:256],
                            ALU.mult, ALU.add).then_inc(s("s_step"), 1)
                        dve.wait_ge(s("s_step"), 8 * i + n + 1)
                dve.wait_ge(s("st_in"), 16 * i + 16)
                for b in range(NB):
                    if b % 2 == 0:
                        dve.wait_ge(s("outer"), 4 * i + b // 2 + 1)
                    stt(st[:, b, :], st[:, b, :], small[:, 24 + b:25 + b],
                        M[(b // 2) % 2][:, 256 * (b % 2):256 * (b % 2) + 256], ALU.mult, ALU.add)\
                        .then_inc(s("st_step"), 1)
                dve.wait_ge(s("os"), i + 1)
                copy(pair_a.rearrange("p (d n) -> p d n", d=2)[:, :, T:N],
                     M[0][:, 0:16].rearrange("p (d n) -> p d n", d=2)).then_inc(s("o_s"), 1)
                dve.wait_ge(s("g_sig"), i + 1)
                tt(g45, g45, g01, ALU.mult)
                dve.wait_ge(s("o_sq"), i + 1)
                tt(tmp[2], tmp[2], tmp[3], ALU.add).then_inc(s("osq"), 1)
                dve.wait_ge(s("o_rs"), i + 1)
                for d in range(2):
                    step(stt(tmp[d], tmp[d], cols[:, bass.ds(i * 2 + (C_MIX + d), 1)], tmp[3], ALU.mult, ALU.mult))
                    tt(wide[:, bass.ds(i * 2 + d, 1), :].rearrange("p c n -> p (c n)"), tmp[d], G[4 + d],
                       ALU.mult).then_inc(s("mixed"), 1)

            for first, gla in ((0, True), (HEADS, False)):
                per = 9 if gla else 11
                with dve.Fori(first, first + HEADS) as i:
                    step.body(i, first, per)
                    run("l0", i, L0_ORDER, i * 6 + T_L0, 1, evac0, i + 12, 1, i * 4)
                    mix0(i, gla)
                step.end(HEADS, per)
            take_mixed(1)

            def residual(l, k, x, j, t, y):
                yt = tmp[t]
                step(copy(yt.rearrange("p (a n) -> p a n", a=2), x))
                dve.wait_ge(s(f"xj{t}"), (j + 1) * 16 + l * 128)
                gate = mod[l][:, bass.ds(j * 2 + (32 + t), 1), :].rearrange("p c n -> p (c n)")
                stt(y[:, 0:T], yt[:, 0:T], gate[:, 0:1], G[t][:, 0:T], ALU.mult, ALU.add)
                step(tt(yt[:, T:N], yt[:, T:N], gate[:, 1:9], ALU.mult))
                return tt(y[:, T:N], yt[:, T:N], G[t][:, T:N], ALU.add)

            with dve.Fori(0, 8) as j:
                step.body(j, 0, 4)
                for t in range(2):
                    lo("out0", j, (2 * t, 2 * t + 1))
                    dve.wait_ge(s("act_ready"), 32)
                    dve.wait_ge(s("pe_unit"), unit("out0", j, 2 * t + 1)[0] + 1)
                    y = wide[:, bass.ds(j * 2 + t, 1), :].rearrange("p c n -> p (c n)")
                    residual(0, 0, halves_of(pt[(T_OUT0 + t) % 2]), j, t, y).then_inc(s("evac"), 1)
                    dve.wait_ge(s("evac"), 2 * j + (T_OUT0 + t + 1))
            step.end(8, 4)
            squares(1)
            norm(1)
            dve.wait_ge(s("act_ready"), 48)
            dve.wait_ge(s("x1_out"), 16)
            step(dve.memset(tmp[4], 0.0))
            step.straight()

            def plain(k, x):
                return copy(G[k].rearrange("p (a n) -> p a n", a=2), x)

            def gelu_arg(y, x):
                step(ts_(y, y, 0.044715, 1.0, ALU.mult, ALU.add))
                step(stt(y, y, GELU, x, ALU.mult, ALU.mult))
                return ts_(y, y, -40.0, None, ALU.max)

            with dve.Fori(0, 4) as j:
                step.body(j, 0, 3)
                run("l1a", j, L1A_ORDER, j * 4 + T_L1A, T_L1A % 2, plain, j + 20, 1, j * 4 + 32)
                dve.wait_ge(s("vd_x2"), j + 1)
                gelu_arg(pair_b, g23).then_inc(s("vd_u"), 1)
                dve.wait_ge(s("q_rs"), j + 1)
                for t in range(2):
                    last = stt(wide[:, bass.ds(j * 2 + t, 1), :].rearrange("p c n -> p (c n)"), G[t],
                               cols[:, C_QN:C_QN + 1], tmp[t], ALU.mult, ALU.mult)
                dve.wait_ge(s("vd_sig"), j + 1)
                tt(g23, g23, pair_b, ALU.mult).then_inc(s("vd_g"), 1)
                dve.wait_ge(s("vd_g"), j + 1)
                copy(wide[:, bass.ds(j * 2 + 8, 2), :].rearrange("p c n -> p (c n)"), g23)
                dve.wait_ge(s("vd_g2"), j + 1)
                step(tt(tmp[4], tmp[4], tmp[2], ALU.add))
                tt(tmp[4], tmp[4], tmp[3], ALU.add).then_inc(s("vd_sq"), 1)
                dve.wait_ge(s("vd_sq"), j + 1)
            step.end(4, 3)
            dve.wait_ge(s("rv"), 1)

            def masks(x):
                for off in (0, 512, 896, 1024):
                    last = tt(x[:, off:off + P], x[:, off:off + P], cm["below"][:, :], ALU.mult)
                return last

            with dve.Fori(0, 8) as i:
                step.body(i, 0, 8)
                run("l1b", i, L1B_ORDER, i * 5 + T_L1B, T_L1B % 2, plain)
                copy(tmp[1], wide[:, bass.ds(i, 1), :].rearrange("p c n -> p (c n)"))
                stt(tmp[2], wide[:, bass.ds(i + 8, 1), :].rearrange("p c n -> p (c n)"),
                    cols[:, bass.ds(i + C_VN, 1)], G[5], ALU.mult, ALU.mult)
                dve.wait_ge(s("evac"), 5 * i + T_L1B + 5)
                ts_(tmp[3], G[2], -40.0, None, ALU.max)
                ts_(tmp[4], G[4], -40.0, None, ALU.max).then_inc(s("g1_clamp"), 1)
                dve.wait_ge(s("k_rs"), i + 1)
                stt(G[0], G[0], cols[:, C_KN:C_KN + 1], tmp[0], ALU.mult, ALU.mult).then_inc(s("kn"), 1)
                dve.wait_ge(s("tok_t"), i + 1)
                dve.wait_ge(s("kv_out"), 64 * i)
                dve.wait_ge(s("cv_out"), 16 * i)
                copy(vntok, M[0].rearrange("p (t d) -> p t d", t=NT))
                copy(srow[0:NB, :], M[1][0:NB, 0:384])
                tt(wst, M[1][:, 384:512], cm["upto_t"][:, :], ALU.mult).then_inc(s("tok_v"), 1)
                dve.wait_ge(s("u_x2"), i + 1)
                gelu_arg(tmp[0], G[3]).then_inc(s("u_u"), 1)
                ts_(tmp[2][:, T:N], tmp[2][:, T:N], per_head[:, 1, bass.ds(i, 1)], per_head[:, 2, bass.ds(i, 1)],
                    ALU.mult, ALU.add)
                dve.wait_ge(s("g1_sig"), i + 1)
                tt(G[4], G[4], tmp[4], ALU.mult)
                tt(G[2], G[2], tmp[3], ALU.mult)
                dve.wait_ge(s("u_sig"), i + 1)
                step(tt(G[3], G[3], tmp[0], ALU.mult))
                step(tt(G[3], G[3], G[4], ALU.mult))
                dve.wait_ge(s("sg"), i + 1)
                out = wide[:, bass.ds(i + 8, 1), :].rearrange("p c n -> p (c n)")
                tt(out[:, 0:T], G[3][:, 0:T], M[3], ALU.mult)
                tt(out[:, T:N], G[3][:, T:N], tmp[2][:, T:N], ALU.mult)
                copy(GS[:, bass.ds(i, 1), :].rearrange("p c n -> p (c n)"), G[2][:, T:N])
                dve.wait_ge(s("z"), i + 1)
                step(ts_(z, m012[:, 0:SB_ALL], SCALE, per_head[:, 0, bass.ds(i, 1)], ALU.mult, ALU.add))
                step(masks(z))
                stt(za, z, -1.0, z, ALU.mult, ALU.max).then_inc(s("z_abs"), 1)
                dve.wait_ge(s("z_l"), i + 1)
                step(stt(za, z, 0.0, za, ALU.max, ALU.add))
                masks(za).then_inc(s("rest"), 1)
                dve.wait_ge(s("between"), i + 1)
                tt(z, z, m012[:, 0:SB_ALL], ALU.subtract).then_inc(s("lw"), 1)
                dve.wait_ge(s("w_e"), i + 1)
                masks(za).then_inc(s("weight"), 1)
                tt(dg.rearrange("p (h d) -> p h d", h=HC), ident[:, :].unsqueeze(1).to_broadcast([P, HC, P]),
                   wide[:, 0:HC, bass.ds(i + T, 1)].to_broadcast([P, HC, P]), ALU.mult).then_inc(s("dg"), 1)
                dve.wait_ge(s("oc"), i + 1)
                tt(wide[:, bass.ds(i, 1), 0:T].rearrange("p c n -> p (c n)"), G[2][:, 0:T], M[3], ALU.mult)
                dve.wait_ge(s("qb"), i + 1)
                for p in range(NPAGE):
                    dve.wait_ge(s(f"page{p % 4}"), (i * 8 + p // 4 + 1) * 16)
                    for h in range(HC):
                        kpage = pages[:, p % 4, P * h:P * h + P]
                        last = dve.tensor_tensor_reduce(kpage, kpage, qb[:, P * h:P * h + P], 1.0, 0.0,
                                                        ALU.mult, ALU.add, zs[:, 8 * p + h:8 * p + h + 1])
                    last.then_inc(s("k_free"), 1)
                dve.wait_ge(s("k_free"), 16 * i + 16)
                zv = zs.rearrange("p (g h) -> p g h", h=HC)
                step(stt(zv, zv, SCALE, per_head[:, 0:1, :].to_broadcast([P, NPAGE, HC]), ALU.mult, ALU.add))
                stt(zsa, zs, -1.0, zs, ALU.mult, ALU.max).then_inc(s("zs_abs"), 1)
                dve.wait_ge(s("zs_l"), i + 1)
                stt(zsa, zs, 0.0, zsa, ALU.max, ALU.add).then_inc(s("s_rest"), 1)
                dve.wait_ge(s("s_between"), i + 1)
                tt(zs, zs, M[3][:, 0:128], ALU.subtract).then_inc(s("s_lw"), 1)
                dve.wait_ge(s("v_free"), 16 * i + 16)
                copy(orow, m012[0:NB, 0:1024]).then_inc(s("orow"), 1)
                dve.wait_ge(s("os1"), i + 1)
                copy(OS[:, :, bass.ds(i, 1)].rearrange("p h b -> p (h b)"), M[2][:, 0:HC]).then_inc(s("mixed1"), 1)
            step.end(8, 8)
            dve.wait_ge(s("mixed1"), HC)
            tt(wide[:, 0:HC, T:N], OS, GS, ALU.mult).then_inc(s("mixed1_all"), 1)
            dve.wait_ge(s("mixed1_all"), 1)
            take_mixed(3)
            with dve.Fori(0, 8) as j:
                step.body(j, 0, 4)
                for t in range(2):
                    lo("out1", j, (2 * t, 2 * t + 1))
                    dve.wait_ge(s("act_ready"), 64)
                    dve.wait_ge(s("pe_unit"), unit("out1", j, 2 * t + 1)[0] + 1)
                    residual(1, 0, halves_of(pt[t]), j, t, G[2 + t]).then_inc(s("evac"), 1)
                    dve.wait_ge(s("y1_t"), 2 * j + t + 1)
                    copy(yrow[:, bass.ds(j * 256 + P * t, P)], M[2][0:NB, P * t:P * t + P]).then_inc(s("ys"), 1)
            step.end(8, 4)

        def layer1_pages(pool):
            pool.wait_ge(s("ptab"), 16)
            pool.wait_ge(s("rv"), 1)
            ck, cv = a["cache_k"][0].rearrange("n s h d -> n s (h d)"), a["cache_v"][0].rearrange("n s h d -> n s (h d)")
            with pool.Fori(0, 8) as i:
                pool.wait_ge(s("sg"), i)
                pool.sem_inc(s("pool_waited"), 1)
                pool.dma_start(ws, a["o_w_s"][0, bass.ds(i, 1)].rearrange("g t s -> t (g s)")).then_inc(s("ws_in"), 16)
                pool.dma_start(brow[0:1, 0:P], a["o_b_s"][0, bass.ds(i, 1)]).then_inc(s("ws_in"), 16)
                for n in range(2 * NPAGE):
                    p = n % NPAGE
                    if n < 4:
                        pool.wait_ge(s("v_free"), 16 * i)
                        pool.sem_inc(s("pool_waited"), 1)
                    elif n < NPAGE + 4:
                        pool.wait_ge(s("k_free"), 16 * i + n - 3)
                        pool.sem_inc(s("pool_waited"), 1)
                    else:
                        pool.wait_ge(s("v_free"), 16 * i + n - 19)
                        pool.sem_inc(s("pool_waited"), 1)
                    page = pool.value_load(ptab[0:1, bass.ds(i * NPAGE + p, 1)], min_val=0, max_val=NPOOL - 1)
                    src = ck if n < NPAGE else cv
                    pool.dma_start(pages[:, n % 4, :], src[bass.ds(page, 1)].rearrange("n s d -> (n s) d"))\
                        .then_inc(s(f"page{n % 4}"), 16)

        @block.gpsimd
        def _(pool):
            pool.dma_start(ptab[:, :], a["page_table"].rearrange("(o b) p -> o (b p)", o=1)).then_inc(s("ptab"), 16)
            pool.wait_ge(s("xt_a"), KC)
            pool.wait_ge(s("xt_s"), KC)
            pool.dma_start(xt_dram, wide[:, :, :]).then_inc(s("xt_out"), 16)
            pool.wait_ge(s("xt_out"), 16)
            pool.wait_ge(s("la_x"), 1)

            def mix0(i, gla, states):
                pool.wait_ge(s("st_out"), 16 * i)
                pool.sem_inc(s("pool_waited"), 1)
                pool.wait_ge(s("os"), i)
                pool.dma_start(st[:, :, :], a[states][0, :, bass.ds(i if gla else i - HEADS, 1)]
                               .rearrange("b h k v -> k b (h v)")).then_inc(s("st_in"), 16)
                if not gla:
                    pool.wait_ge(s("mixed"), i * 2)
                    pool.sem_inc(s("pool_waited"), 1)
                    pool.dma_start(decays, a["ret"][bass.ds(i - HEADS, 1)].rearrange("h p n -> p (h n)"))\
                        .then_inc(s("ret_in"), 16)
                for n in range(1, NCH):
                    pool.wait_ge(s("s_step"), 8 * i + n)
                    pool.sem_inc(s("pool_waited"), 1)
                    pool.tensor_scalar(carry[:, n, :], S[:, (n - 1) % 2, :],
                                       small[:, 6 * (n // 2) + n % 2:6 * (n // 2) + n % 2 + 1], None,
                                       ALU.mult).then_inc(s("carry"), 1)
                pool.wait_ge(s("s_step"), 8 * i + 8)
                pool.sem_inc(s("pool_waited"), 1)
                kind = "gla" if gla else "ret"
                h = i if gla else i - HEADS
                pool.dma_start(a[kind + "_prompt_out"][0, 0, bass.ds(h, 1)].rearrange("h k v -> k (h v)"),
                               S[:, 1, :]).then_inc(s("s_out"), 16)
                pool.wait_ge(s("st_step"), 8 * i + 8)
                pool.sem_inc(s("pool_waited"), 1)
                pool.dma_start(a[kind + "_sample_out"][0, :, bass.ds(h, 1)].rearrange("b h k v -> k b (h v)"),
                               st[:, :, :]).then_inc(s("st_out"), 16)

            with pool.Fori(0, HEADS) as i:
                mix0(i, True, "state_gla")
            pool.wait_ge(s("cum"), HEADS)
            pool.dma_start(rope, a["rope"]).then_inc(s("rope_in"), 16)
            with pool.Fori(HEADS, 2 * HEADS) as i:
                mix0(i, False, "state_ret")
            for l, x in ((0, xt_dram), (1, x1_dram)):
                if l:
                    pool.wait_ge(s("evac"), T_OUT0 + 16)
                    pool.dma_start(x1_dram, wide[:, :, :]).then_inc(s("x1_out"), 16)
                    pool.wait_ge(s("x1_out"), 16)
                    layer1_pages(pool)
                pool.wait_ge(s("act_ready"), 32 * l + 32)
                with pool.Fori(0, 8) as j:
                    for t in range(2):
                        pool.wait_ge(s("evac"), j * 2 + (T_OUT1 if l else T_OUT0))
                        pool.sem_inc(s("pool_waited"), 1)
                        pool.dma_start(G[t], x[:, bass.ds(j * 2 + t, 1), :].rearrange("p c n -> p (c n)"))\
                            .then_inc(s(f"xj{t}"), 16)
                    if l:
                        for t in range(2):
                            pool.wait_ge(s("yo"), 2 * j + t + 1)
                            pool.sem_inc(s("pool_waited"), 1)
                            pool.dma_start(a["y_prompt_out"][0].rearrange("(q p) n -> p q n", p=P)
                                           [:, :, bass.ds(j * 256 + P * t, P)],
                                           yo[t].rearrange("p (q n) -> p q n", q=NT)).then_inc(s("y_out"), 16)
            pool.wait_ge(s("ys"), 16)
            pool.dma_start(a["y_sample_out"].rearrange("b o d -> (b o) d"), yrow).then_inc(s("ys_out"), 16)
            for name, value in (("ys_out", 16), ("y_out", 256), ("st_out", 128), ("s_out", 128), ("kv_out", 512),
                                ("cv_out", 128)):
                pool.wait_ge(s(name), value)

        return



_INS = ["x_prompt", "x_sample", "state_gla", "state_ret", "cache_k", "cache_v", "page_table",
        "c_prompt", "c_sample", "e_norm_g", "e_w_ada", "e_b_ada", "e_w_in", "e_w_a2", "e_b_a",
        "e_gla_norm_g", "e_ret_norm_g", "e_w_out", "o_norm_g", "o_w_ada", "o_b_ada", "o_w_in",
        "o_q_norm_g", "o_k_norm_g", "o_sb_offset", "o_v_norm_g", "o_w_s", "o_b_s", "o_w_out"]
_OUTS = [("y_prompt", (1, T, D)), ("y_sample", (NB, 1, D)),
         ("gla_prompt", (1, 1, HEADS, P, 256)), ("gla_sample", (1, NB, HEADS, P, 256)),
         ("ret_prompt", (1, 1, HEADS, P, 256)), ("ret_sample", (1, NB, HEADS, P, 256)),
         ("k_prompt", (1, 1, T, HC, P)), ("v_prompt", (1, 1, T, HC, P)),
         ("k_sample", (1, NB, 1, HC, P)), ("v_sample", (1, NB, 1, HC, P)), ("chunk_v", (1, NB, 1, BR))]


def kernel(**inputs):
    import concourse.bacc as bacc
    from concourse.bass_utils import run_bass_kernel_spmd

    nc = bacc.Bacc("TRN2", target_bir_lowering=False, num_devices=1)
    cst = constants()
    arrays, a, o = {}, {}, {}
    for name in _INS:
        x = np.ascontiguousarray(inputs[name])
        arrays["in_" + name] = x
        a[name] = nc.dram_tensor("in_" + name, x.shape, mybir.dt.from_np(x.dtype), kind="ExternalInput").ap()
    c_aps = {}
    for name, x in cst.items():
        arrays["const_" + name] = x
        c_aps[name] = nc.dram_tensor("const_" + name, x.shape, F32, kind="ExternalInput").ap()
    a["ret"], a["rope"] = c_aps["ret"], c_aps["rope"]
    for name, shape in _OUTS:
        a[name + "_out"] = nc.dram_tensor("out_" + name, shape, F32, kind="ExternalOutput").ap()
    build(nc, a, o, c_aps)
    r = run_bass_kernel_spmd(nc, [arrays], core_ids=[0])
    return tuple(r.results[0]["out_" + name] for name, _ in _OUTS)
```

```python
from contextlib import ExitStack

import numpy as np
import concourse.bass as bass
from concourse import mybir

F32 = mybir.dt.float32
F32R = mybir.dt.float32r
I32 = mybir.dt.int32
ALU = mybir.AluOpType
ACT = mybir.ActivationFunctionType

P = 128
D = 2048
KC = D // P
T = 512
NB = 8
N = T + NB
HALF = N // 2
NT = T // P
HEADS = 4
RANK = 16
CH = 64
NCH = T // CH
NPAGE, PAGE, NPOOL = 16, 128, 160
HC = 8
BR = D // 2
EPS = 1e-6
DH = P
SCALE = float(DH) ** -0.5
GELU = 1.5957691216057308
SB_OFF = {0: 0, 1: 512, 3: 896, 2: 1024}
SB_ALL = 1280
BIG = 3.0e38

E_QA, E_KA, E_VA, E_RA, E_GA = 0, 512, 1024, 2048, 2064
E_QB, E_KB, E_VB, E_GB = 3088, 3600, 4112, 5136
O_Q, O_K, O_V, O_G, O_U, O_VD, O_GD = (BR * n for n in range(7))

U_ADA0, U_RA, U_L0, U_GATE1, U_OUT0, U_L1A, U_L1B, U_OUT1 = 0, 96, 98, 258, 290, 322, 354, 434
T_RA, T_L0, T_OUT0, T_L1A, T_L1B, T_OUT1 = 0, 1, 49, 65, 81, 121
RAW_DEPTH = 4
TILE, MOD = "tile", "mod"
MOD_ORDER = [MOD] * 4
L0_ORDER = [TILE, MOD, TILE, MOD, TILE, MOD, TILE, MOD, TILE, TILE]
L1A_ORDER = [TILE] * 4
L1B_ORDER = [TILE] * 5
OUT_ORDER = [TILE] * 2
L1B_SLOTS = [2, 3, 0, 1, 4]
L0_TO, L1A_TO, L1B_TO = [0, 1, 3, 2, 4, 5], [0, 1, 2, 3], [4, 3, 2, 1, 0]

C_BADA, C_NORM, C_MIX, C_VN, C_QN, C_KN = (0, 48), (96, 112), 128, 144, 152, 153


def constants():
    c = {}
    c["ident"] = np.eye(P)
    t = np.arange(P)
    same = (t[:, None] // CH) == (t[None, :] // CH)
    mid = (t // CH) * CH + CH // 2 - 1
    upto = (same & (t[:, None] <= t[None, :])).astype(np.float64)
    to_mid = (same & (t[:, None] <= mid[None, :])).astype(np.float64)
    c["cum_mid"] = (upto - to_mid) / 16.0
    small = np.zeros((P, 6))
    for n in range(2):
        m, last = to_mid[:, n * CH], upto[:, n * CH + CH - 1]
        small[:, n], small[:, 2 + n], small[:, 4 + n] = m, last, last - m
    c["cum_small"] = small / 16.0
    c["chunk_mask"] = same & (t[:, None] <= t[None, :])
    c["below"] = t[:, None] < t[None, :]
    c["from_key"] = t[:, None] >= t[None, :]
    c["upto_t"] = t[:, None] <= t[None, :]
    c["swap"] = np.roll(np.eye(P), P // 2, axis=0)
    c["fold"] = np.concatenate([np.eye(9)] * 2, 0)
    c = {k: np.ascontiguousarray(v, dtype=np.float32) for k, v in c.items()}
    pos = np.concatenate([np.arange(T), np.full(NB, NPAGE * PAGE)]).astype(np.float32)
    half = P // 2
    inv = (np.float32(10000.0) ** (-np.arange(half, dtype=np.float32) / np.float32(half))).astype(np.float32)
    ang = (pos[None, :] * inv[:, None]).astype(np.float32).astype(np.float64)
    c["rope"] = np.stack([np.concatenate([np.cos(ang)] * 2, 0),
                          np.concatenate([-np.sin(ang), np.sin(ang)], 0)], 1).astype(np.float32)
    lg = np.log1p(-np.exp2(-5.0 - np.arange(HEADS)))
    rel = np.arange(T) % CH - (CH // 2 - 1)
    m, last = CH // 2, CH
    sm = np.zeros((HEADS, 32))
    for tile in range(NT):
        sm[:, 6 * tile:6 * tile + 6] = np.exp(lg[:, None] * np.array([m, m, last, last, last - m, last - m]))
    sm[:, 24:] = np.exp(lg)[:, None]
    ret = np.concatenate([np.exp(lg[:, None] * rel), np.exp(-lg[:, None] * rel), sm], 1)
    c["ret"] = ret[:, None, :].repeat(P, 1).astype(np.float32)
    return c


CHIP = ("ident", "cum_mid", "cum_small", "chunk_mask", "below", "from_key", "upto_t", "swap", "fold")


def build(nc, a, o, cst):
    ctx = ExitStack()
    with ctx:
        def sb(name, shape, dt=F32):
            return ctx.enter_context(nc.sbuf_tensor(name, shape, dt))

        sems = {}

        def s(name):
            if name not in sems:
                sems[name] = ctx.enter_context(nc.semaphore(name))
            return sems[name]

        xt_dram = nc.dram_tensor("xt_scratch", [P, KC, N], F32).ap()
        x1_dram = nc.dram_tensor("x1_scratch", [P, KC, N], F32).ap()

        act_hi = sb("act_hi", [P, KC, N], F32R)
        act_lo = sb("act_lo", [P, KC, N], F32R)
        wide = sb("wide", [P, KC, N])
        raw = sb("raw", [P, 5, 1024])
        w_hi = sb("w_hi", [P, 2, 1024], F32R)
        w_lo = sb("w_lo", [P, 2, 1024], F32R)
        cm = {k: sb("c_" + k, list(cst[k].shape)) for k in CHIP}
        ident = cm["ident"]
        ones = sb("ones", [P, P])
        mod = [sb("mod0", [P, 48, 9]), sb("mod1", [P, 48, 9])]
        cols = sb("cols", [P, 154])
        per_head = sb("per_head", [P, 3, HC])
        cond = sb("cond", [P, KC, 66], F32R)
        arena = sb("arena", [P, 15600])
        used = [0]

        def region(n):
            at = used[0]
            used[0] += n
            assert used[0] <= 15600, used[0]
            return arena[:, at:at + n]

        mrow = region(512)
        G = [region(N) for _ in range(6)]
        t0_at = used[0]
        tmp = [region(N) for _ in range(5)]
        base = used[0]
        la = region(NT * T).rearrange("p (t k) -> p t k", t=NT)
        rope = arena[:, base:base + 2 * N].rearrange("p (a n) -> p a n", a=2)
        decays = region(2 * T + 32)
        up, down, small = decays[:, 0:T], decays[:, T:2 * T], decays[:, 2 * T:2 * T + 32]
        vtok = region(NT * 256).rearrange("p (t d) -> p t d", t=NT)
        ktok = region(NT * P).rearrange("p (t d) -> p t d", t=NT)
        carry = region(8 * 256).rearrange("p (n d) -> p n d", n=8)
        st = region(8 * 256).rearrange("p (n d) -> p n d", n=8)
        S = region(2 * 256).rearrange("p (n d) -> p n d", n=2)
        sdec = region(32)
        lah = raw[:, 4, 0:512].rearrange("p (t k) -> p t k", t=NT)
        sct = raw[:, 4, 512:1024].rearrange("p (t k) -> p t k", t=NT)
        kmask = arena[0:NB, t0_at + N:t0_at + N + 1024].rearrange("p (b k) -> p b k", b=NB)
        srow0 = tmp[3][0:NB, 0:384]
        hs = G[5][:, 0:KC * NB].rearrange("p (c n) -> p c n", n=NB)
        used[0] = 512
        xin = region(5 * D).rearrange("p (t d) -> p t d", t=5)
        crow = region(D)
        rowa, rowb = region(P), region(P)
        csm = region(9 * KC)
        csm2 = region(9 * KC)
        wa2 = region(T)[0:RANK + 1, :]
        used[0] = base
        z = region(SB_ALL)
        za = region(SB_ALL)
        ktok1 = region(512).rearrange("p (t d) -> p t d", t=NT)
        vtok1 = region(512).rearrange("p (t d) -> p t d", t=NT)
        vntok = tmp[2][:, 0:T].rearrange("p (t d) -> p t d", t=NT)
        wst = region(P)
        ws = region(P)
        pages = region(4 * 1024).rearrange("p (n d) -> p n d", n=4)
        srow = mrow[:, 128:512]
        brow = mrow
        qb = region(1024)
        wv = mod[0].rearrange("p c n -> p (c n)")[:, 0:128]
        pair_a = arena[:, t0_at:t0_at + 2 * N]
        pair_b = arena[:, t0_at + 2 * N:t0_at + 4 * N]
        pair_c = arena[:, t0_at + 3 * N:t0_at + 5 * N]
        g01, g23, g45 = (arena[:, 512 + 2 * N * n:512 + 2 * N * n + 2 * N] for n in range(3))
        OS = region(64).rearrange("p (h b) -> p h b", h=HC)
        GS = region(64).rearrange("p (h b) -> p h b", h=HC)
        zs = region(128)
        zsa = region(128)
        dg = za[:, 0:1024]
        orow = z[0:NB, 0:1024]
        eps = sb("eps", [P, 1])
        vla = arena[:, 512:512 + 2048]
        sda = arena[:, 512 + 2048:512 + 2080]
        ptab = sb("ptab", [1, NB * NPAGE], I32)
        yrow = arena[0:NB, base:base + D]
        yo = [arena[:, base + D + 512 * n:base + D + 512 * n + 512] for n in range(2)]

        pt = [ctx.enter_context(nc.psum_tensor(f"pt{n}", [P, 2, 512], F32)) for n in range(2)]
        m012 = ctx.enter_context(nc.psum_tensor("m012", [P, 1536], F32))
        m3 = ctx.enter_context(nc.psum_tensor("m3", [P, 512], F32))
        M = [m012[:, 512 * n:512 * n + 512] for n in range(3)] + [m3[:, :]]

        ra_rows = G[0][0:RANK + 1, :]

        phases = {}
        have = [0] * 5
        for name, first, iters, order in (("ada0", U_ADA0, 12, [MOD] * 4), ("ra", U_RA, 1, [TILE]),
                                          ("l0", U_L0, 8, L0_ORDER), ("gate1", U_GATE1, 4, MOD_ORDER),
                                          ("out0", U_OUT0, 8, OUT_ORDER),
                                          ("l1a", U_L1A, 4, L1A_ORDER), ("l1b", U_L1B, 8, L1B_ORDER),
                                          ("out1", U_OUT1, 8, OUT_ORDER)):
            units = 2 * len(order)
            slots = [L1B_SLOTS[u % 5] if name == "l1b" else (first + u) % 4 for u in range(units + 2)]
            rank = [slots[:u].count(slots[u]) for u in range(units + 2)]
            per = [slots[:units].count(x) for x in range(5)]
            phases[name] = (first, units, slots, rank, per, list(have))
            have = [h + iters * p for h, p in zip(have, per)]

        def unit(name, i, u):
            first, units, slots, rank, per, before = phases[name]
            sl = slots[u]
            return first + i * units + u, sl, (i * per[sl] + (before[sl] + rank[u] + 1)) * 16

        class Chain:

            def __init__(self, eng, name):
                self.eng, self.name, self.base, self.at, self.n = eng, name, 0, 0, 0

            def body(self, i, first, per):
                self.at, self.n = self.base + (i - first) * per, 0

            def end(self, iters, per):
                assert self.n == per, (self.name, self.n)
                self.base += iters * per
                self.at, self.n = self.base, 0

            def __call__(self, ins):
                ins.then_inc(s(self.name), 1)
                self.n += 1
                self.eng.wait_ge(s(self.name), self.at + self.n)

            def straight(self):
                self.base, self.at, self.n = self.base + self.n, self.base + self.n, 0

        NCONST = len(CHIP) + 3 + 9 + 2 + 2
        block = ctx.enter_context(nc.Block())

        @block.sync
        def _(sp):
            def const(dst, src):
                sp.dma_start(dst, src).then_inc(s("const_in"), 16)

            const(crow[0:1, :], a["c_prompt"])
            const(crow[1:9, :], a["c_sample"])
            for k in CHIP:
                const(cm[k][:, :], cst[k])
            for n, src in enumerate((a["o_sb_offset"][0, :], a["o_w_s"][0, :, 0, 0], a["o_b_s"][0, :, 0])):
                with nc.allow_non_contiguous_dma(reason="eight scalars"):
                    const(per_head[:, n, :], src.partition_broadcast(P))
            const(rowa[0:48, :], a["e_b_ada"].rearrange("o (r c) -> (o r) c", c=P))
            const(rowa[48:96, :], a["o_b_ada"].rearrange("o (r c) -> (o r) c", c=P))
            at = 0
            for name, k in (("e_norm_g", 16), ("o_norm_g", 16), ("e_gla_norm_g", 8), ("e_ret_norm_g", 8),
                            ("o_v_norm_g", 8), ("o_q_norm_g", 1), ("o_k_norm_g", 1)):
                const(rowb[at:at + k, :], a[name].rearrange("o (r c) -> (o r) c", c=P))
                at += k
            const(wa2[0:RANK, :], a["e_w_a2"][0])
            const(wa2[RANK:RANK + 1, :], a["e_b_a"])

            def load(name, i, u, src):
                n, sl, _ = unit(name, i, u)
                if not (isinstance(n, int) and n < RAW_DEPTH):
                    sp.wait_ge(s("split_hi"), n - (RAW_DEPTH - 1))
                    sp.wait_ge(s("split_lo"), n - (RAW_DEPTH - 1))
                sp.dma_start(raw[:, sl, :].rearrange("p (c n) -> p c n", c=src.shape[1]), src)\
                    .then_inc(s(f"raw{sl}"), 16)

            def load_tile(name, i, u, w, col):
                for hh in range(2):
                    load(name, i, u + hh, w[:, 8 * hh:8 * hh + 8, bass.ds(col, P)])

            def load_mod(name, i, u, w, col, pair):
                for hh in range(2):
                    k = 2 * (2 * pair + hh)
                    load(name, i, u + hh, w[:, k:k + 2, bass.ds(col, 512)])

            def weights(name, i, order, w_tile, tile_cols, w_mod=None, mod_col=None):
                t = m = 0
                for n, what in enumerate(order):
                    if what is TILE:
                        load_tile(name, i, 2 * n, w_tile, tile_cols[t])
                        t += 1
                    else:
                        load_mod(name, i, 2 * n, w_mod, mod_col, m)
                        m += 1

            v = {k: a[k][0].rearrange("(c p) n -> p c n", p=P)
                 for k in ("e_w_ada", "o_w_ada", "e_w_in", "o_w_in", "e_w_out", "o_w_out")}
            for u in range(4):
                load("ada0", 0, u, v["e_w_ada"][:, 2 * u:2 * u + 2, 0:512])
            for t in range(NT):
                sp.dma_start(xin[:, t, :], a["x_prompt"][0, P * t:P * t + P, :]).then_inc(s("x_in"), 16)
            sp.dma_start(xin[0:NB, 4, :], a["x_sample"].rearrange("b o d -> (b o) d")).then_inc(s("x_in"), 16)
            for u in range(4, 8):
                load("ada0", 0, u, v["e_w_ada"][:, 2 * u:2 * u + 2, 0:512])
            with sp.Fori(1, 12) as g:
                weights("ada0", g, MOD_ORDER, None, None, v["e_w_ada"], g * 512)
            load_tile("ra", 0, 0, v["e_w_in"], E_RA)

            def gla_cols(i):
                return [i * 256 + E_VA, i * 256 + (E_VA + P), (i + E_KA // P) * P, i * P + E_QA,
                        i * 256 + E_GA, i * 256 + (E_GA + P)]

            def ret_cols(i):
                b = HEADS
                return [i * 256 + (E_VB - 256 * b), i * 256 + (E_VB + P - 256 * b), i * P + (E_KB - P * b),
                        i * P + (E_QB - P * b), i * 256 + (E_GB - 256 * b), i * 256 + (E_GB + P - 256 * b)]

            with sp.Fori(0, HEADS) as i:
                weights("l0", i, L0_ORDER, v["e_w_in"], gla_cols(i), v["o_w_ada"], i * 512)
            with sp.Fori(HEADS, 2 * HEADS) as i:
                weights("l0", i, L0_ORDER, v["e_w_in"], ret_cols(i), v["o_w_ada"], i * 512)
            with sp.Fori(0, 4) as g:
                weights("gate1", g, MOD_ORDER, None, None, v["o_w_ada"][:, :, 2 * D:3 * D], g * 512)
            with sp.Fori(0, 8) as j:
                weights("out0", j, OUT_ORDER, v["e_w_out"], [j * 256, j * 256 + P])
            with sp.Fori(0, 4) as j:
                weights("l1a", j, L1A_ORDER, v["o_w_in"],
                        [j * 256 + O_Q, j * 256 + (O_Q + P), j * 256 + O_VD, j * 256 + (O_VD + P)])
            with sp.Fori(0, 8) as i:
                weights("l1b", i, L1B_ORDER, v["o_w_in"], [i * P + c for c in (O_U, O_GD, O_G, O_V, O_K)])
            with sp.Fori(0, 8) as j:
                weights("out1", j, OUT_ORDER, v["o_w_out"], [j * 256, j * 256 + P])


        def go_on(mix):
            if mix is not None:
                next(mix, None)

        def finish(mix):
            for _ in mix:
                pass

        @block.tensor
        def _(pe):
            def mm(out, lhsT, rhs, start=True, stop=True):
                return pe.matmul(out, lhsT, rhs, start=start, stop=stop, skip_group_check=True)

            def tr(out, x):
                k = x.shape[0]
                return pe.transpose(out, x, ident[0:k, 0:k])

            def unit_ready(name, i, u):
                n, _, _ = unit(name, i, u)
                pe.wait_ge(s("split_hi"), n + 1)
                pe.wait_ge(s("split_lo"), n + 1)
                return (phases[name][0] + u) % 2

            def tile_unit(name, i, u, hh, par, stage):
                b = unit_ready(name, i, u)
                for k in range(8):
                    c = 8 * hh + k
                    if stage is not None:
                        pe.wait_ge(s("act_ready"), 16 * stage + c + 1)
                    hi, lo = w_hi[:, b, P * k:P * k + P], w_lo[:, b, P * k:P * k + P]
                    for w, x in ((hi, act_hi), (hi, act_lo), (lo, act_hi)):
                        for h in range(2):
                            last = mm(pt[par][:, h, 0:HALF], w, x[:, c, HALF * h:HALF * h + HALF],
                                      start=(c == 0 and w is hi and x is act_hi), stop=(c == 15 and w is lo))
                last.then_inc(s("pe_unit"), 1)

            def mod_unit(name, i, u, k0):
                b = unit_ready(name, i, u)
                for k in range(2):
                    c = k0 + k
                    for w in (w_hi, w_lo):
                        last = mm(M[3][0:66, :], cond[:, c, :], w[:, b, 512 * k:512 * k + 512],
                                  start=(c == 0 and w is w_hi), stop=(c == 15 and w is w_lo))
                last.then_inc(s("pe_unit"), 1)

            def mod_fold(g):
                pe.wait_ge(s("mod_row"), g + 1)
                for j in range(4):
                    last = mm(M[3][:, 9 * j:9 * j + 9], mrow[0:18, P * j:P * j + P], cm["fold"][:, :])
                last.then_inc(s("mod_col"), 1)

            def walk(name, i, order, tile0=None, par0=None, stage=None, group=None, late0=0, mix=None,
                     always=False):
                go_on(mix)
                t = m = 0
                fold = False
                for u in range(2 * len(order)):
                    kind, hh = order[u // 2], u % 2
                    if kind is TILE:
                        if hh == 0:
                            pe.wait_ge(s("evac"), tile0 + t - 1 + (late0 if t == 0 else 0))
                        tile_unit(name, i, u, hh, (par0 + t) % 2, stage if t == 0 else None)
                        t += hh
                    else:
                        if m == 0:
                            pe.wait_ge(s("mod_read"), group)
                        mod_unit(name, i, u, 2 * m)
                        m += 1
                    if fold:
                        mod_fold(group)
                        fold = False
                    fold = kind is MOD and m == 8
                    if kind is TILE or always:
                        go_on(mix)
                if fold:
                    mod_fold(group)

            pe.wait_ge(s("const_in"), 16 * NCONST)
            tr(M[0][:, 0:96], rowa[0:96, :])
            tr(M[0][:, 96:154], rowb[0:58, :]).then_inc(s("cols_t"), 1)
            for k in range(KC):
                last = tr(M[1][:, 9 * k:9 * k + 9], crow[0:9, P * k:P * k + P])
            last.then_inc(s("cond_t"), 1)
            pe.wait_ge(s("x_in"), 80)
            pe.wait_ge(s("cols"), 1)
            pe.wait_ge(s("cond_cols"), 1)
            for c in range(KC):
                b = c % 2
                if c >= 2:
                    pe.wait_ge(s("xt_a"), c - 1)
                    pe.wait_ge(s("xt_s"), c - 1)
                for t in range(NT):
                    tr(M[b][:, P * t:P * t + P], xin[:, t, P * c:P * c + P])
                tr(M[2 + b][:, 0:8], xin[0:NB, 4, P * c:P * c + P]).then_inc(s("xt"), 1)
            pe.wait_ge(s("cond"), 1)
            pe.wait_ge(s("xt_s"), KC)
            walk("ada0", 0, MOD_ORDER, group=0)
            with pe.Fori(1, 12) as g:
                walk("ada0", g, MOD_ORDER, group=g)

            def feature_sum(src, big, small_, done):
                mm(big, ones[:, :], src[:, 0:T])
                mm(small_, ones[:, :], src[:, T:N]).then_inc(s(done), 1)

            pe.wait_ge(s("x_sq"), 1)
            feature_sum(tmp[4], M[0], M[1][:, 0:8], "x_ss")
            walk("ra", 0, [TILE], 1, 0, stage=0)
            pe.wait_ge(s("ra"), 1)
            for t in range(NT):
                mm(M[t], ra_rows[:, P * t:P * t + P], wa2)
            for h in range(HEADS):
                last = mm(pt[1][:, 0, 8 * h:8 * h + 8], wa2[:, P * h:P * h + P], ra_rows[:, T:N])
            last.then_inc(s("la_x"), 1)
            pe.wait_ge(s("la"), 1)

            def mix0(i, gla):
                yield
                pe.wait_ge(s("evac"), i * 6 + (T_L0 + 6))
                if gla:
                    pe.wait_ge(s("lah"), i + 1)
                    for t in range(NT):
                        mm(M[0][:, P * t:P * t + P], lah[:, t, :], cm["cum_mid"][:, :])
                        last = mm(M[1][:, 6 * t:6 * t + 6], lah[:, t, :], cm["cum_small"][:, :])
                    last.then_inc(s("cum"), 1)
                else:
                    mm(M[0], cm["swap"][:, :], G[2][:, 0:T])
                    mm(M[1], cm["swap"][:, :], G[3][:, 0:T])
                    mm(M[2][:, 0:8], cm["swap"][:, :], G[2][:, T:N])
                    mm(M[2][:, 8:16], cm["swap"][:, :], G[3][:, T:N]).then_inc(s("swapped"), 1)
                yield
                pe.wait_ge(s("qk"), i + 1)
                for t in range(NT):
                    for d in range(2):
                        tr(M[1 + t // 2][:, 256 * (t % 2) + P * d:256 * (t % 2) + P * d + P],
                           G[d][:, P * t:P * t + P])
                tr(M[0][0:NB, 0:P], G[3][:, T:N])
                tr(M[0][0:NB, P:2 * P], G[0][:, T:N])
                tr(M[0][0:NB, 2 * P:3 * P], G[1][:, T:N]).then_inc(s("v_t"), 1)
                yield
                pe.wait_ge(s("srow0"), i + 1)
                for t in range(NT):
                    tr(M[0][:, P * t:P * t + P], G[3][:, P * t:P * t + P])
                pe.wait_ge(s("vtok"), i + 1)
                for t in range(NT):
                    last = mm(M[2][:, P * t:P * t + P], G[3][:, P * t:P * t + P], G[2][:, P * t:P * t + P])
                last.then_inc(s("sc"), 1)
                yield
                pe.wait_ge(s("ktok"), i + 1)
                for n in range(NCH):
                    if n == 4:
                        yield
                        pe.wait_ge(s("s_step"), i * 8 + 4)
                    r = CH * (n % 2)
                    last = mm(M[n % 2][:, 128 * (n % 4 - n % 2):128 * (n % 4 - n % 2) + 256],
                              ktok[r:r + CH, n // 2, :], vtok[r:r + CH, n // 2, :])
                    if n % 4 == 3:
                        last.then_inc(s("kv"), 1)
                yield
                pe.wait_ge(s("s_step"), i * 8 + 8)
                pe.wait_ge(s("kmask"), i + 1)
                pe.wait_ge(s("sct"), i + 1)
                pe.wait_ge(s("carry"), i * 7 + 7)
                for d in range(2):
                    if d:
                        pe.wait_ge(s("st_step"), i * 8 + 4)
                        pe.wait_ge(s("o_a"), i * 2 + 1)
                    for b in range(4 * d, 4 * d + 4):
                        last = mm(M[b // 2 % 2][:, 256 * (b % 2):256 * (b % 2) + 256], kmask[:, b, :],
                                  srow0[:, P:3 * P])
                    last.then_inc(s("outer"), 1)
                    for t in range(NT):
                        mm(M[2][:, P * t:P * t + P], vtok[:, t, P * d:P * d + P], sct[:, t, :],
                           start=True, stop=False)
                        for n in (2 * t, 2 * t + 1):
                            if n:
                                last = mm(M[2][:, CH * n:CH * n + CH], carry[:, n, P * d:P * d + P],
                                          G[2][:, CH * n:CH * n + CH], start=False, stop=True)
                    last.then_inc(s("o"), 1)
                    yield
                pe.wait_ge(s("st_step"), i * 8 + 8)
                for d in range(2):
                    for b in range(NB):
                        last = mm(M[0][:, 8 * d + b:8 * d + b + 1], st[:, b, P * d:P * d + P], G[2][:, T + b:T + b + 1])
                last.then_inc(s("os"), 1)
                yield
                pe.wait_ge(s("osq"), i + 1)
                feature_sum(tmp[2], M[0], M[1][:, 0:8], "oss")
                yield

            def l0(i, mix=None):
                walk("l0", i, L0_ORDER, i * 6 + T_L0, 1, group=i + 12, mix=mix)
                if mix is not None:
                    finish(mix)

            l0(0)
            with pe.Fori(1, HEADS) as i:
                l0(i, mix0(i - 1, True))
            l0(HEADS, mix0(HEADS - 1, True))
            with pe.Fori(HEADS + 1, 2 * HEADS) as i:
                l0(i, mix0(i - 1, False))
            mix = mix0(2 * HEADS - 1, False)
            walk("gate1", 0, MOD_ORDER, group=20, mix=mix, always=True)
            walk("gate1", 1, MOD_ORDER, group=21, mix=mix, always=True)
            finish(mix)
            with pe.Fori(2, 4) as g:
                walk("gate1", g, MOD_ORDER, group=g + 20)
            walk("out0", 0, OUT_ORDER, T_OUT0, T_OUT0 % 2, stage=1)
            with pe.Fori(1, 8) as j:
                walk("out0", j, OUT_ORDER, j * 2 + T_OUT0, T_OUT0 % 2)
            pe.wait_ge(s("x_sq"), 2)
            feature_sum(tmp[4], M[0], M[1][:, 0:8], "x_ss")

            def mix_qv(j, last_one=False):
                yield
                pe.wait_ge(s("q_sq"), j + 1)
                for t in range(2):
                    mm(M[t], ones[:, :], tmp[t][:, 0:T])
                    last = mm(M[2][:, 8 * t:8 * t + 8], ones[:, :], tmp[t][:, T:N])
                last.then_inc(s("q_ss"), 1)
                yield
                if last_one:
                    yield
                    spread_queries(0)
                    yield
                    yield
                    pe.wait_ge(s("vd_sq"), 4)
                    feature_sum(tmp[4], M[0], M[1][:, 0:8], "vd_ss")
                yield

            def spread_queries(b):
                pe.wait_ge(s("dg"), b + 1)
                for h in range(2):
                    last = mm(M[1 + h], ones[:, :], dg[:, 512 * h:512 * h + 512])
                last.then_inc(s("qb_t"), 1)

            def l1a(j, stage=None, mix=None):
                walk("l1a", j, L1A_ORDER, j * 4 + T_L1A, T_L1A % 2, stage=stage, mix=mix)

            l1a(0, stage=2)
            with pe.Fori(1, 4) as j:
                l1a(j, mix=mix_qv(j - 1))

            def mix1(i, tiles, head, values, out):
                yield
                if out:
                    pe.wait_ge(s("orow"), i - 1)
                    for h in range(HC):
                        last = mm(M[3][:, 16 + h:17 + h], orow[:, P * h:P * h + P], ident[0:NB, h:h + 1])
                if head:
                    pe.wait_ge(s("evac"), i * 5 + T_L1B)
                    pe.wait_ge(s("k_sq"), i)
                    pe.wait_ge(s("g1_clamp"), i)
                    pe.wait_ge(s("ws_in"), i * 32)
                    mm(M[0], ones[:, :], tmp[0][:, 0:T])
                    mm(M[3][:, 0:8], ones[:, :], tmp[0][:, T:N])
                    tr(M[3][0:NB, P:2 * P], G[1][:, T:N])
                    tr(M[3][0:NB, 2 * P:3 * P], tmp[2][:, T:N])
                    last = tr(M[3][:, 3 * P:4 * P], ws)
                last.then_inc(s("p0"), 1)
                if tiles and head:
                    spread_queries(i)
                yield
                if head:
                    pe.wait_ge(s("kn"), i)
                    if tiles:
                        pe.wait_ge(s("qb"), i + 1)
                    for t in range(NT):
                        tr(M[0][:, P * t:P * t + P], G[0][:, P * t:P * t + P])
                        tr(M[1][:, P * t:P * t + P], G[1][:, P * t:P * t + P])
                        tr(M[2][:, P * t:P * t + P], tmp[2][:, P * t:P * t + P])
                    tr(M[3][0:NB, 0:P], G[0][:, T:N])
                if values:
                    pe.wait_ge(s("s_rest"), i)
                    mm(M[3][:, 128:256], cm["from_key"][:, :], zsa, start=True, stop=False)
                    for j in range(1, NPAGE):
                        last = mm(M[3][:, 128:256 - 8 * j], ones[:, :], zsa[:, 8 * j:128], start=False, stop=(j == 15))
                    last.then_inc(s("p1"), 1)
                yield
                for k in range(8):
                    if head and k == 0:
                        pe.wait_ge(s("tok_a"), i)
                        pe.wait_ge(s("tok_v"), i)
                        for t in range(NT):
                            mm(M[0][:, P * t:P * t + P], vntok[:, t, :], wst, start=True, stop=False)
                            last = mm(M[0][:, P * t:P * t + P], ones[0:1, :], brow[0:1, 0:P], start=False, stop=True)
                        last.then_inc(s("sg"), 1)
                    if head and k == 1:
                        pe.wait_ge(s("od"), i)
                        for b in range(NT):
                            last = mm(m012[:, SB_OFF[b]:SB_OFF[b] + T - P * b], G[0][:, P * b:P * b + P],
                                      tmp[1][:, P * b:T])
                        last.then_inc(s("z"), 1)
                    if head and k == 2:
                        pe.wait_ge(s("rest"), i)
                        for b in range(NT):
                            off = SB_OFF[b]
                            last = mm(m012[:, off:off + T - P * b], cm["from_key"][:, :], za[:, off:off + T - P * b],
                                      start=True, stop=(b == 3))
                            for l in range(b + 1, NT):
                                last = mm(m012[:, off + P * (l - b):off + T - P * b], ones[:, :],
                                          za[:, SB_OFF[l]:SB_OFF[l] + T - P * l], start=False, stop=(l == 3))
                        last.then_inc(s("between"), 1)
                    if head and k == 3:
                        pe.wait_ge(s("weight"), i)
                        for b in range(NT):
                            last = mm(M[0][:, P * b:T], vtok1[:, b, :], za[:, SB_OFF[b]:SB_OFF[b] + T - P * b],
                                      start=(b == 0), stop=(b == 3))
                        last.then_inc(s("oc"), 1)
                    if values:
                        if k == 0:
                            pe.wait_ge(s("s_weight"), i)
                            pe.wait_ge(s("tok_v"), i)
                        for p in (2 * k, 2 * k + 1):
                            pe.wait_ge(s(f"page{2 + p % 2}"), ((i - 1) * 8 + (k + 1)) * 16)
                            for h in range(2):
                                last = mm(M[3][32 * h:32 * h + NB, :], wv[:, 8 * p:8 * p + 8],
                                          pages[:, 2 + p % 2, 512 * h:512 * h + 512],
                                          start=(p == 0), stop=(p == NPAGE - 1))
                            last.then_inc(s("v_free"), 1)
                    yield

            def l1b(i, mix, tiles=True):
                if tiles:
                    walk("l1b", i, L1B_ORDER, i * 5 + T_L1B, T_L1B % 2, late0=1, mix=mix)
                finish(mix)

            l1b(0, mix_qv(3, True))
            l1b(1, mix1(1, True, True, True, False))
            with pe.Fori(2, HC) as i:
                l1b(i, mix1(i, True, True, True, True))
            l1b(HC, mix1(HC, False, True, True, True), False)
            l1b(HC + 1, mix1(HC + 1, False, False, False, True), False)

            def transposed(j, t):
                pe.wait_ge(s("evac"), j * 2 + (T_OUT1 + t + 1))
                if not (isinstance(j, int) and j == 0):
                    pe.wait_ge(s("yo"), j * 2 + (t - 1))
                    pe.wait_ge(s("ys"), j * 2 + (t - 1))
                y = G[2 + t]
                for q in range(NT):
                    tr(M[t][:, P * q:P * q + P], y[:, P * q:P * q + P])
                tr(M[2 + t][0:NB, 0:P], y[:, T:N]).then_inc(s("y1_t"), 1)

            def turn(j, first):
                yield
                if not first:
                    transposed(j - 1, 1)
                yield
                yield
                transposed(j, 0)
                yield

            walk("out1", 0, OUT_ORDER, T_OUT1, 0, stage=3, mix=turn(0, True))
            with pe.Fori(1, 8) as j:
                walk("out1", j, OUT_ORDER, j * 2 + T_OUT1, 0, mix=turn(j, False))
            transposed(7, 1)

        @block.scalar
        def _(act):
            step = Chain(act, "act_step")

            def f(out, x, fn, **kw):
                return act.activation(out, x, fn, **kw)

            def hi(name, i, u):
                n, sl, loaded = unit(name, i, u)
                act.wait_ge(s(f"raw{sl}"), loaded)
                if not (isinstance(n, int) and n < 2):
                    act.wait_ge(s("pe_unit"), n - 1)
                f(w_hi[:, (phases[name][0] + u) % 2, :], raw[:, sl, :], ACT.Copy).then_inc(s("split_hi"), 1)

            def walk(name, i, order, mix=None, always=False, ahead=2):
                go_on(mix)
                for u in range(2 * len(order)):
                    if u < 2 * len(order) + ahead - 2:
                        hi(name, i, u + 2)
                    if order[u // 2] is TILE or always:
                        go_on(mix)

            def sigmoid(x):
                step(f(x, x, ACT.Exp, scale=-1.0))
                step(f(x, x, ACT.Ln, bias=1.0))
                return f(x, x, ACT.Exp, scale=-1.0)

            def rstd(dst, big, small_, width):
                f(dst[:, 0:T], big, ACT.Ln, scale=1.0 / width, bias=eps[:, 0:1])
                step(f(dst[:, T:N], small_, ACT.Ln, scale=1.0 / width, bias=eps[:, 0:1]))
                return f(dst, dst, ACT.Exp, scale=-0.5)

            def norm(k):
                act.wait_ge(s("x_ss"), k + 1)
                rstd(tmp[4], M[0], M[1][:, 0:8], D).then_inc(s("x_rs"), 1)
                act.wait_ge(s("ns"), k + 1)
                f(act_hi[:, :, T:N], hs, ACT.Copy).then_inc(s("ns_hi"), 1)
                for c in range(KC):
                    act.wait_ge(s("n_t"), 16 * k + c + 1)
                    f(act_hi[:, c, 0:T], tmp[c % 4][:, 0:T], ACT.Identity, bias=mod[k][:, c, 0:1])\
                        .then_inc(s("act_hi"), 1)

            def take_mixed():
                for c in range(KC):
                    f(act_hi[:, c, :], wide[:, c, :], ACT.Copy).then_inc(s("act_hi"), 1)

            act.preload_act_table_set("natural_log_exp_and_others")
            act.wait_ge(s("cond_cols"), 1)
            sigmoid(csm2).then_inc(s("cond_sig"), 1)
            act.wait_ge(s("cond_v"), 1)
            f(cond[:, :, 0:9], csm.rearrange("p (c n) -> p c n", n=9), ACT.Copy).then_inc(s("cond_hi"), 1)
            for c in range(KC):
                act.wait_ge(s("xt"), c + 1)
                f(wide[:, c, 0:T], M[c % 2], ACT.Copy).then_inc(s("xt_a"), 1)
            hi("ada0", 0, 0)
            hi("ada0", 0, 1)
            act.wait_ge(s("xt_a"), KC)
            act.wait_ge(s("xt_s"), KC)
            for c in range(KC):
                if c >= 2:
                    act.wait_ge(s("x_acc"), c - 1)
                f(tmp[2 + c % 2], wide[:, c, :], ACT.Square).then_inc(s("x_sqc"), 1)
            step.straight()
            walk("ada0", 0, MOD_ORDER)
            with act.Fori(1, 12) as g:
                walk("ada0", g, MOD_ORDER)
            norm(0)
            walk("ra", 0, [TILE])
            act.wait_ge(s("la_abs"), 1)
            step(f(vla, vla, ACT.Exp, scale=-1.0))
            f(vla, vla, ACT.Ln, bias=1.0)
            step(f(sda, sda, ACT.Exp, scale=-1.0))
            f(sda, sda, ACT.Ln, bias=1.0).then_inc(s("la_l"), 1)
            act.wait_ge(s("sd"), 1)
            f(sdec, sdec, ACT.Exp, scale=1.0 / 16.0).then_inc(s("sdec"), 1)
            act.wait_ge(s("sdec"), 1)
            act.wait_ge(s("la"), 1)
            step.straight()

            def mix0(i, gla):
                if gla:
                    f(lah, la[:, :, bass.ds(i * P, P)], ACT.Copy).then_inc(s("lah"), 1)
                yield
                if gla:
                    act.wait_ge(s("cum"), i + 1)
                    f(up, M[0], ACT.Exp)
                    f(down, M[0], ACT.Exp, scale=-1.0)
                    f(small[:, 0:24], M[1][:, 0:24], ACT.Exp)
                    f(small[:, 24:32], sdec[:, bass.ds(i * NB, NB)], ACT.Copy).then_inc(s("decay"), 1)
                act.wait_ge(s("g_clamp"), i + 1)
                sigmoid(pair_c).then_inc(s("g_sig"), 1)
                yield
                act.wait_ge(s("v_t"), i + 1)
                f(vtok[:, 0:2, :], M[1].rearrange("p (t d) -> p t d", t=2), ACT.Copy)
                f(vtok[:, 2:4, :], M[2].rearrange("p (t d) -> p t d", t=2), ACT.Copy).then_inc(s("vtok"), 1)
                yield
                act.wait_ge(s("sc"), i + 1)
                f(ktok, M[0].rearrange("p (t d) -> p t d", t=NT), ACT.Copy).then_inc(s("ktok"), 1)
                yield
                yield
                yield
                for d in range(2):
                    act.wait_ge(s("o"), i * 2 + (d + 1))
                    f(tmp[d][:, 0:T], M[2], ACT.Copy).then_inc(s("o_a"), 1)
                    yield
                act.wait_ge(s("o_a"), i * 2 + 2)
                act.wait_ge(s("o_s"), i + 1)
                f(pair_b, pair_a, ACT.Square).then_inc(s("o_sq"), 1)
                yield
                act.wait_ge(s("oss"), i + 1)
                rstd(tmp[3], M[0], M[1][:, 0:8], 256.0).then_inc(s("o_rs"), 1)
                yield

            def l0(i, mix=None):
                walk("l0", i, L0_ORDER, mix)
                if mix is not None:
                    finish(mix)

            l0(0)
            with act.Fori(1, HEADS) as i:
                step.body(i, 1, 3)
                l0(i, mix0(i - 1, True))
            step.end(HEADS - 1, 3)
            l0(HEADS, mix0(HEADS - 1, True))
            step.straight()
            with act.Fori(HEADS + 1, 2 * HEADS) as i:
                step.body(i, HEADS + 1, 3)
                l0(i, mix0(i - 1, False))
            step.end(HEADS - 1, 3)
            mix = mix0(2 * HEADS - 1, False)
            walk("gate1", 0, MOD_ORDER, mix, always=True)
            walk("gate1", 1, MOD_ORDER, mix, always=True)
            finish(mix)
            with act.Fori(2, 4) as g:
                walk("gate1", g, MOD_ORDER)
            act.wait_ge(s("mixed"), 16)
            take_mixed()

            def y_squares(j):
                yield
                yield
                for t in range(2):
                    act.wait_ge(s("evac"), j * 2 + (T_OUT0 + t + 1))
                    if isinstance(j, int) and j == 0:
                        pass
                    else:
                        act.wait_ge(s("y_acc"), j * 2 + t - 1)
                    f(tmp[2 + t], wide[:, bass.ds(j * 2 + t, 1), :].rearrange("p c n -> p (c n)"), ACT.Square)\
                        .then_inc(s("y_sq"), 1)
                    yield
                    yield

            def out0(j):
                mix = y_squares(j)
                walk("out0", j, OUT_ORDER, mix)
                finish(mix)

            out0(0)
            with act.Fori(1, 8) as j:
                out0(j)
            norm(1)
            step.straight()

            def mix_qv(j, last_one=False):
                act.wait_ge(s("evac"), j * 4 + (T_L1A + 4))
                f(pair_a, g01, ACT.Square).then_inc(s("q_sq"), 1)
                f(pair_b, g23, ACT.Square).then_inc(s("vd_x2"), 1)
                yield
                act.wait_ge(s("q_ss"), j + 1)
                for t in range(2):
                    f(tmp[t][:, 0:T], M[t], ACT.Ln, scale=1.0 / DH, bias=eps[:, 0:1])
                    last = f(tmp[t][:, T:N], M[2][:, 8 * t:8 * t + 8], ACT.Ln, scale=1.0 / DH, bias=eps[:, 0:1])
                step(last)
                f(pair_a, pair_a, ACT.Exp, scale=-0.5).then_inc(s("q_rs"), 1)
                yield
                act.wait_ge(s("vd_u"), j + 1)
                sigmoid(pair_b).then_inc(s("vd_sig"), 1)
                yield
                act.wait_ge(s("vd_g"), j + 1)
                f(pair_b, g23, ACT.Square).then_inc(s("vd_g2"), 1)
                if last_one:
                    take_queries(0)
                    yield
                    yield
                    act.wait_ge(s("vd_ss"), 1)
                    rstd(G[5], M[0], M[1][:, 0:8], BR).then_inc(s("rv"), 1)
                yield

            def take_queries(b):
                act.wait_ge(s("qb_t"), b + 1)
                f(qb, m012[:, 512:1536], ACT.Copy).then_inc(s("qb"), 1)

            def l1a(j, mix=None):
                walk("l1a", j, L1A_ORDER, mix)
                if mix is not None:
                    finish(mix)

            l1a(0)
            with act.Fori(1, 4) as j:
                step.body(j, 1, 3)
                l1a(j, mix_qv(j - 1))
            step.end(3, 3)

            def mix1(i, tiles, head, values, out):
                if head:
                    act.wait_ge(s("evac"), i * 5 + T_L1B)
                    f(tmp[0], G[0], ACT.Square).then_inc(s("k_sq"), 1)
                yield
                if head:
                    act.wait_ge(s("p0"), i)
                    rstd(tmp[0], M[0], M[3][:, 0:8], DH).then_inc(s("k_rs"), 1)
                if tiles and head:
                    take_queries(i)
                if values:
                    act.wait_ge(s("zs_abs"), i)
                    step(f(zsa, zsa, ACT.Exp, scale=-1.0))
                    f(zsa, zsa, ACT.Ln, bias=1.0).then_inc(s("zs_l"), 1)
                if head:
                    act.wait_ge(s("g1_clamp"), i)
                    sigmoid(pair_c).then_inc(s("g1_sig"), 1)
                yield
                if head:
                    act.wait_ge(s("p1"), i)
                    act.wait_ge(s("kv_out"), (i - 1) * 64)
                    f(ktok1, M[0].rearrange("p (t d) -> p t d", t=NT), ACT.Copy)
                    f(vtok1, M[1].rearrange("p (t d) -> p t d", t=NT), ACT.Copy).then_inc(s("tok_a"), 1)
                    act.wait_ge(s("s_lw"), i)
                    f(wv, zs, ACT.Exp).then_inc(s("s_weight"), 1)
                    act.wait_ge(s("kn"), i)
                    f(tmp[0], G[4], ACT.Square).then_inc(s("u_x2"), 1)
                yield
                if head:
                    act.wait_ge(s("tok_a"), i)
                    act.wait_ge(s("tok_v"), i)
                    for n, (src, big, small_) in enumerate(((ktok1, a["k_prompt_out"], a["k_sample_out"]),
                                                           (vtok1, a["v_prompt_out"], a["v_sample_out"]))):
                        act.dma_start(big[0, 0].rearrange("(t p) h d -> p t h d", p=P)[:, :, bass.ds(i - 1, 1), :]
                                      .rearrange("p t h d -> p t (h d)"), src).then_inc(s("kv_out"), 16)
                        act.dma_start(small_[0, :, 0, bass.ds(i - 1, 1), :].rearrange("b h d -> b (h d)"),
                                      srow[0:NB, P * n:P * n + P]).then_inc(s("kv_out"), 16)
                    act.dma_start(a["chunk_v_out"][0, :, 0, bass.ds((i - 1) * P, P)],
                                  srow[0:NB, 2 * P:3 * P]).then_inc(s("cv_out"), 16)
                    act.wait_ge(s("u_u"), i)
                    sigmoid(tmp[0]).then_inc(s("u_sig"), 1)
                yield
                if head:
                    act.wait_ge(s("z_abs"), i)
                    step(f(za, za, ACT.Exp, scale=-1.0))
                    f(za, za, ACT.Ln, bias=1.0).then_inc(s("z_l"), 1)
                yield
                if head:
                    act.wait_ge(s("lw"), i)
                    f(za, z, ACT.Exp).then_inc(s("w_e"), 1)
                yield

            def l1b(i, mix, tiles=True):
                if tiles:
                    walk("l1b", i, L1B_ORDER, mix)
                finish(mix)

            l1b(0, mix_qv(3, True))
            step.straight()
            l1b(1, mix1(1, True, True, True, False))
            step.straight()
            with act.Fori(2, HC) as i:
                step.body(i, 2, 7)
                l1b(i, mix1(i, True, True, True, True))
            step.end(HC - 2, 7)
            l1b(HC, mix1(HC, False, True, True, True), False)
            act.wait_ge(s("mixed1_all"), 1)
            take_mixed()
            act.wait_ge(s("kv_out"), 64 * HC)

            def rows_out(j, first):
                def rows(j, t):
                    act.wait_ge(s("y1_t"), j * 2 + (t + 1))
                    if not (isinstance(j, int) and j == 0):
                        act.wait_ge(s(f"y_out{t}"), j * 16)
                    f(yo[t], M[t], ACT.Copy).then_inc(s("yo"), 1)

                yield
                if not first:
                    rows(j - 1, 1)
                yield
                yield
                rows(j, 0)
                yield

            walk("out1", 0, OUT_ORDER, rows_out(0, True))
            with act.Fori(1, 7) as j:
                walk("out1", j, OUT_ORDER, rows_out(j, False))
            walk("out1", 7, OUT_ORDER, rows_out(7, False), ahead=0)
            act.wait_ge(s("y1_t"), 16)
            act.wait_ge(s("y_out1"), 7 * 16)
            f(yo[1], M[1], ACT.Copy).then_inc(s("yo"), 1)


        @block.vector
        def _(dve):
            step = Chain(dve, "dve_step")
            tt, ts_, stt, copy = dve.tensor_tensor, dve.tensor_scalar, dve.scalar_tensor_tensor, dve.tensor_copy

            def lo(name, i, u):
                n, sl, _ = unit(name, i, u)
                dve.wait_ge(s("split_hi"), n + 1)
                if not (isinstance(n, int) and n < 2):
                    dve.wait_ge(s("pe_unit"), n - 1)
                b = (phases[name][0] + u) % 2
                tt(w_lo[:, b, :], raw[:, sl, :], w_hi[:, b, :].bitcast(F32), ALU.subtract)\
                    .then_inc(s("split_lo"), 1)

            def halves(x):
                return x.rearrange("p (a n) -> p a n", a=2)

            def mod_rows(name, i, u):
                dve.wait_ge(s("pe_unit"), unit(name, i, u)[0] + 1)
                copy(mrow[0:18, :], M[3][0:18, :]).then_inc(s("mod_row"), 1)

            def mod_add(group, layer, col):
                dve.wait_ge(s("mod_col"), group + 1)
                tt(mod[layer][:, bass.ds(col, 4), :], M[3][:, 0:36].rearrange("p (j n) -> p j n", j=4),
                   cols[:, bass.ds(col + C_BADA[layer], 4)].unsqueeze(2).to_broadcast([P, 4, 9]),
                   ALU.add).then_inc(s("mod_read"), 1)

            def walk(name, i, order, evac=None, par0=0, group=None, layer=None, col=None, mix=None,
                     always=False, ahead=2, late=None):
                late = late or {}
                go_on(mix)
                t = m = 0
                fold = False

                def read_out(k, u):
                    dve.wait_ge(s("pe_unit"), unit(name, i, u)[0] + 1)
                    evac(k, pt[(par0 + k) % 2][:, :, 0:HALF]).then_inc(s("evac"), 1)

                for u in range(2 * len(order)):
                    for k, (at, last) in late.items():
                        if u == at:
                            read_out(k, last)
                    if u < 2 * len(order) + ahead - 2:
                        lo(name, i, u + 2)
                    if order[u // 2] is TILE and u % 2 == 1:
                        if t not in late:
                            read_out(t, u)
                        t += 1
                    if fold:
                        mod_add(group, layer, col)
                        fold = False
                    if order[u // 2] is MOD:
                        m += 1
                        if m == 8:
                            mod_rows(name, i, u)
                            fold = True
                    if order[u // 2] is TILE or always:
                        go_on(mix)
                if fold:
                    mod_add(group, layer, col)

            def mod_scale(k):
                g = cols[:, C_NORM[k]:C_NORM[k] + 16].unsqueeze(2).to_broadcast([P, 16, 9])
                stt(mod[k][:, 16:32, :], mod[k][:, 16:32, :], 1.0, g, ALU.add, ALU.mult)\
                    .then_inc(s("mod_scale"), 1)
                dve.wait_ge(s("mod_scale"), k + 1)

            def norm(k):
                dve.wait_ge(s("mod_read"), 12 + 12 * k)
                mod_scale(k)
                dve.wait_ge(s("x_rs"), k + 1)
                step(tt(hs, wide[:, :, T:N], tmp[4][:, T:N].unsqueeze(1).to_broadcast([P, KC, NB]), ALU.mult))
                step(tt(hs, hs, mod[k][:, 16:32, 1:9], ALU.mult))
                tt(hs, hs, mod[k][:, 0:16, 1:9], ALU.add).then_inc(s("ns"), 1)

                def scaled(c):
                    if c >= 4:
                        dve.wait_ge(s("act_ready"), 32 * k + c - 3)
                    stt(tmp[c % 4][:, 0:T], wide[:, c, 0:T], mod[k][:, 16 + c, 0:1], tmp[4][:, 0:T],
                        ALU.mult, ALU.mult).then_inc(s("n_t"), 1)

                scaled(0)
                dve.wait_ge(s("ns"), k + 1)
                dve.wait_ge(s("ns_hi"), k + 1)
                tt(act_lo[:, :, T:N], hs, act_hi[:, :, T:N].bitcast(F32), ALU.subtract)
                for c in range(KC):
                    if c + 1 < KC:
                        scaled(c + 1)
                    dve.wait_ge(s("n_t"), 16 * k + c + 1)
                    dve.wait_ge(s("act_hi"), 32 * k + c + 1)
                    stt(act_lo[:, c, 0:T], tmp[c % 4][:, 0:T], mod[k][:, c, 0:1],
                        act_hi[:, c, 0:T].bitcast(F32), ALU.add, ALU.subtract).then_inc(s("act_ready"), 1)

            def take_mixed(stage):
                for c in range(KC):
                    dve.wait_ge(s("act_hi"), 16 * stage + c + 1)
                    tt(act_lo[:, c, :], wide[:, c, :], act_hi[:, c, :].bitcast(F32), ALU.subtract)\
                        .then_inc(s("act_ready"), 1)

            dve.memset(eps[:, :], EPS)
            dve.memset(cond[:, :, :].bitcast(I32), 0)
            dve.memset(ones[:, :], 1.0).then_inc(s("ones"), 1)
            dve.wait_ge(s("ones"), 1)
            dve.wait_ge(s("cols_t"), 1)
            copy(cols[:, :], M[0][:, 0:154]).then_inc(s("cols"), 1)
            dve.wait_ge(s("cond_t"), 1)
            step(copy(csm, M[1][:, 0:144]))
            ts_(csm2, csm, -40.0, None, ALU.max).then_inc(s("cond_cols"), 1)
            dve.wait_ge(s("cond_sig"), 1)
            tt(csm, csm, csm2, ALU.mult).then_inc(s("cond_v"), 1)
            dve.wait_ge(s("cond_hi"), 1)
            tt(cond[:, :, 9:18], csm.rearrange("p (c n) -> p c n", n=9), cond[:, :, 0:9].bitcast(F32),
               ALU.subtract).then_inc(s("cond"), 1)
            for c in range(KC):
                dve.wait_ge(s("xt"), c + 1)
                copy(wide[:, c, T:N], M[2 + c % 2][:, 0:8]).then_inc(s("xt_s"), 1)
            lo("ada0", 0, 0)
            lo("ada0", 0, 1)
            for c in range(KC):
                dve.wait_ge(s("x_sqc"), c + 1)
                if c == 0:
                    copy(tmp[4], tmp[2]).then_inc(s("x_acc"), 1)
                else:
                    dve.wait_ge(s("x_acc"), c)
                    tt(tmp[4], tmp[4], tmp[2 + c % 2], ALU.add).then_inc(s("x_acc" if c < KC - 1 else "x_sq"), 1)
            step.straight()
            walk("ada0", 0, MOD_ORDER, group=0, layer=0, col=0)
            with dve.Fori(1, 12) as g:
                walk("ada0", g, MOD_ORDER, group=g, layer=0, col=g * 4)
            norm(0)
            step(dve.memset(ra_rows, 1.0))
            walk("ra", 0, [TILE], lambda k, x: copy(halves(G[0][0:RANK, :]), x[0:RANK]))
            dve.wait_ge(s("evac"), 1)
            dve.engine_nop().then_inc(s("ra"), 1)
            dve.wait_ge(s("la_x"), 1)
            for t in range(NT):
                copy(la[:, t, :], M[t])
            step(copy(sdec, pt[1][:, 0, 0:32]))
            laf = la.rearrange("p t k -> p (t k)")
            stt(vla, laf, -1.0, laf, ALU.mult, ALU.max)
            stt(sda, sdec, -1.0, sdec, ALU.mult, ALU.max).then_inc(s("la_abs"), 1)
            dve.wait_ge(s("la_l"), 1)
            stt(laf, laf, 0.0, vla, ALU.min, ALU.subtract).then_inc(s("la"), 1)
            stt(sdec, sdec, 0.0, sda, ALU.min, ALU.subtract).then_inc(s("sd"), 1)
            dve.wait_ge(s("sd"), 1)
            step.straight()

            def evac0(i, mixing):
                def evac(k, x):
                    to = L0_TO[k]
                    if mixing:
                        if to < 2:
                            dve.wait_ge(s("v_t"), i)
                        elif to == 3:
                            dve.wait_ge(s("sc"), i)
                        elif to == 2:
                            dve.wait_ge(s("os"), i)
                        else:
                            dve.wait_ge(s("mixed"), i * 2)
                    d = halves(G[to])
                    return ts_(d, x, SCALE, None, ALU.mult) if to == 2 else copy(d, x)
                return evac

            def mix0(i, gla):
                dve.wait_ge(s("evac"), i * 6 + (T_L0 + 6))
                dve.wait_ge(s("mixed"), i * 2)
                ts_(pair_c, g45, -40.0, None, ALU.max).then_inc(s("g_clamp"), 1)
                yield
                if gla:
                    dve.wait_ge(s("decay"), i + 1)
                else:
                    dve.wait_ge(s("ret_in"), i * 16 + (16 - 16 * HEADS))
                    dve.wait_ge(s("rope_in"), 16)
                    dve.wait_ge(s("swapped"), i + (1 - HEADS))
                    for k in range(2):
                        tt(tmp[k][:, 0:T], M[k], rope[:, 1, 0:T], ALU.mult)
                        tt(tmp[k][:, T:N], M[2][:, 8 * k:8 * k + 8], rope[:, 1, T:N], ALU.mult)
                        step(tt(G[2 + k], G[2 + k], rope[:, 0, :], ALU.mult))
                    tt(g23, g23, pair_a, ALU.add).then_inc(s("rotated"), 1)
                    dve.wait_ge(s("rotated"), i + (1 - HEADS))
                tt(G[2][:, 0:T], G[2][:, 0:T], up, ALU.mult)
                tt(G[3][:, 0:T], G[3][:, 0:T], down, ALU.mult).then_inc(s("qk"), 1)
                yield
                dve.wait_ge(s("g_sig"), i + 1)
                step(tt(g45, g45, pair_c, ALU.mult))
                dve.wait_ge(s("v_t"), i + 1)
                copy(srow0, M[0][0:NB, 0:384]).then_inc(s("srow0"), 1)
                dve.wait_ge(s("srow0"), i + 1)
                tt(kmask, srow0[:, 0:P].unsqueeze(1).to_broadcast([NB, NB, P]),
                   ident[0:NB, 0:NB].unsqueeze(2).to_broadcast([NB, NB, P]), ALU.mult).then_inc(s("kmask"), 1)
                yield
                dve.wait_ge(s("sc"), i + 1)
                stt(sct, M[2].rearrange("p (t k) -> p t k", t=NT), BIG,
                    cm["chunk_mask"][:, :].unsqueeze(1).to_broadcast([P, NT, P]), ALU.min, ALU.mult)\
                    .then_inc(s("sct"), 1)
                yield
                for n in range(NCH):
                    at = 6 * (n // 2) + n % 2
                    if n % 4 == 0:
                        if n:
                            yield
                        dve.wait_ge(s("kv"), i * 2 + (n // 4 + 1))
                    kv = M[n % 2][:, 128 * (n % 4 - n % 2):128 * (n % 4 - n % 2) + 256]
                    if n == 0:
                        ts_(S[:, 0, :], kv, small[:, at + 4:at + 5], None, ALU.mult).then_inc(s("s_step"), 1)
                    else:
                        step(ts_(tmp[4][:, 0:256], kv, small[:, at + 4:at + 5], None, ALU.mult))
                        if n >= 2:
                            dve.wait_ge(s("carry"), i * 7 + (n - 1))
                        elif n == 1:
                            dve.wait_ge(s("s_out"), i * 16)
                        stt(S[:, n % 2, :], S[:, (n - 1) % 2, :], small[:, at + 2:at + 3], tmp[4][:, 0:256],
                            ALU.mult, ALU.add).then_inc(s("s_step"), 1)
                        dve.wait_ge(s("s_step"), i * 8 + (n + 1))
                yield
                dve.wait_ge(s("st_in"), i * 16 + 16)
                for d in range(2):
                    dve.wait_ge(s("outer"), i * 2 + (d + 1))
                    for b in range(4 * d, 4 * d + 4):
                        stt(st[:, b, :], st[:, b, :], small[:, 24 + b:25 + b],
                            M[(b // 2) % 2][:, 256 * (b % 2):256 * (b % 2) + 256], ALU.mult, ALU.add)\
                            .then_inc(s("st_step"), 1)
                    yield
                dve.wait_ge(s("os"), i + 1)
                copy(pair_a.rearrange("p (d n) -> p d n", d=2)[:, :, T:N],
                     M[0][:, 0:16].rearrange("p (d n) -> p d n", d=2)).then_inc(s("o_s"), 1)
                dve.wait_ge(s("o_sq"), i + 1)
                tt(tmp[2], tmp[2], tmp[3], ALU.add).then_inc(s("osq"), 1)
                yield
                dve.wait_ge(s("o_rs"), i + 1)
                for d in range(2):
                    step(stt(tmp[d], tmp[d], cols[:, bass.ds(i * 2 + (C_MIX + d), 1)], tmp[3], ALU.mult, ALU.mult))
                    tt(wide[:, bass.ds(i * 2 + d, 1), :].rearrange("p c n -> p (c n)"), tmp[d], G[4 + d],
                       ALU.mult).then_inc(s("mixed"), 1)
                yield

            def l0(i, mix=None):
                walk("l0", i, L0_ORDER, evac0(i, mix is not None), 1, group=i + 12, layer=1, col=i * 4, mix=mix)
                if mix is not None:
                    finish(mix)

            l0(0)
            with dve.Fori(1, HEADS) as i:
                step.body(i, 1, 10)
                l0(i, mix0(i - 1, True))
            step.end(HEADS - 1, 10)
            l0(HEADS, mix0(HEADS - 1, True))
            step.straight()
            with dve.Fori(HEADS + 1, 2 * HEADS) as i:
                step.body(i, HEADS + 1, 12)
                l0(i, mix0(i - 1, False))
            step.end(HEADS - 1, 12)
            mix = mix0(2 * HEADS - 1, False)
            for g in range(2):
                walk("gate1", g, MOD_ORDER, group=g + 20, layer=1, col=4 * g + 32, mix=mix, always=True)
            finish(mix)
            with dve.Fori(2, 4) as g:
                walk("gate1", g, MOD_ORDER, group=g + 20, layer=1, col=g * 4 + 32)
            take_mixed(1)
            step.straight()

            def residual(l, x, j, t, y):
                yt = tmp[t]
                step(copy(halves(yt), x))
                dve.wait_ge(s(f"xj{t}"), j * 16 + (16 + l * 128))
                gate = mod[l][:, bass.ds(j * 2 + (32 + t), 1), :].rearrange("p c n -> p (c n)")
                stt(y[:, 0:T], yt[:, 0:T], gate[:, 0:1], G[t][:, 0:T], ALU.mult, ALU.add)
                step(tt(yt[:, T:N], yt[:, T:N], gate[:, 1:9], ALU.mult))
                return tt(y[:, T:N], yt[:, T:N], G[t][:, T:N], ALU.add)

            def add_squares(j, t, first=False, last=False):
                dve.wait_ge(s("y_sq"), j * 2 + (t + 1))
                if first:
                    copy(tmp[4], tmp[2 + t]).then_inc(s("y_acc"), 1)
                else:
                    dve.wait_ge(s("y_acc"), j * 2 + t)
                    tt(tmp[4], tmp[4], tmp[2 + t], ALU.add).then_inc(s("x_sq" if last else "y_acc"), 1)

            def sums(j, first):
                yield
                if not first:
                    add_squares(j - 1, 1)
                yield
                yield
                add_squares(j, 0, first)
                yield

            def out0(j, first=False):
                def evac(k, x):
                    dve.wait_ge(s("evac"), j * 2 + (T_OUT0 + k))
                    return residual(0, x, j, k, wide[:, bass.ds(j * 2 + k, 1), :].rearrange("p c n -> p (c n)"))

                mix = sums(j, first)
                walk("out0", j, OUT_ORDER, evac, T_OUT0 % 2, mix=mix)
                finish(mix)

            dve.wait_ge(s("act_ready"), 32)
            out0(0, True)
            step.straight()
            with dve.Fori(1, 8) as j:
                step.body(j, 1, 4)
                out0(j)
            step.end(7, 4)
            add_squares(7, 1, last=True)
            norm(1)
            dve.wait_ge(s("act_ready"), 48)
            dve.wait_ge(s("x1_out"), 16)
            step(dve.memset(tmp[4], 0.0))
            step.straight()

            def gelu_arg(y, x):
                step(ts_(y, y, 0.044715, 1.0, ALU.mult, ALU.add))
                step(stt(y, y, GELU, x, ALU.mult, ALU.mult))
                return ts_(y, y, -40.0, None, ALU.max)

            def spread(b):
                tt(dg.rearrange("p (h d) -> p h d", h=HC), ident[:, :].unsqueeze(1).to_broadcast([P, HC, P]),
                   wide[:, 0:HC, bass.ds(b + T, 1)].to_broadcast([P, HC, P]), ALU.mult).then_inc(s("dg"), 1)

            def key_pages(i, k):
                if k == 0:
                    dve.wait_ge(s("qb"), i + 1)
                for p in range(2):
                    dve.wait_ge(s(f"page{p}"), i * 128 + 16 * (k + 1))
                    for h in range(HC):
                        kpage = pages[:, p, P * h:P * h + P]
                        at = 8 * (2 * k + p) + h
                        last = dve.tensor_tensor_reduce(kpage, kpage, qb[:, P * h:P * h + P], 1.0, 0.0,
                                                        ALU.mult, ALU.add, zs[:, at:at + 1])
                    last.then_inc(s("k_free"), 1)

            def mix_qv(j, last_one=False):
                yield
                dve.wait_ge(s("vd_x2"), j + 1)
                gelu_arg(pair_b, g23).then_inc(s("vd_u"), 1)
                dve.wait_ge(s("q_rs"), j + 1)
                for t in range(2):
                    last = stt(wide[:, bass.ds(j * 2 + t, 1), :].rearrange("p c n -> p (c n)"), G[t],
                               cols[:, C_QN:C_QN + 1], tmp[t], ALU.mult, ALU.mult)
                step(last)
                yield
                if last_one:
                    spread(0)
                dve.wait_ge(s("vd_sig"), j + 1)
                tt(g23, g23, pair_b, ALU.mult).then_inc(s("vd_g"), 1)
                dve.wait_ge(s("vd_g"), j + 1)
                step(copy(wide[:, bass.ds(j * 2 + 8, 2), :].rearrange("p c n -> p (c n)"), g23))
                yield
                dve.wait_ge(s("vd_g2"), j + 1)
                step(tt(tmp[4], tmp[4], tmp[2], ALU.add))
                tt(tmp[4], tmp[4], tmp[3], ALU.add).then_inc(s("vd_sq"), 1)
                dve.wait_ge(s("vd_sq"), j + 1)
                if last_one:
                    for k in range(8):
                        key_pages(0, k)
                        yield
                yield

            def l1a(j, mix=None):
                walk("l1a", j, L1A_ORDER, lambda k, x: copy(halves(G[L1A_TO[k]]), x), T_L1A % 2, mix=mix)
                if mix is not None:
                    finish(mix)

            l1a(0)
            with dve.Fori(1, 4) as j:
                step.body(j, 1, 5)
                l1a(j, mix_qv(j - 1))
            step.end(3, 5)

            def masks(x):
                for off in (0, 512, 896, 1024):
                    last = tt(x[:, off:off + P], x[:, off:off + P], cm["below"][:, :], ALU.mult)
                return last

            def mix1(i, tiles, head, values, out):
                hd = i - 1
                if head:
                    dve.wait_ge(s("evac"), i * 5 + T_L1B)
                    dve.wait_ge(s("rv"), 1)
                    if not (isinstance(i, int) and i == 1):
                        dve.wait_ge(s("od"), i - 1)
                    copy(tmp[1], wide[:, bass.ds(hd, 1), :].rearrange("p c n -> p (c n)"))
                    stt(tmp[2], wide[:, bass.ds(hd + 8, 1), :].rearrange("p c n -> p (c n)"),
                        cols[:, bass.ds(hd + C_VN, 1)], G[5], ALU.mult, ALU.mult)
                    ts_(tmp[3], G[2], -40.0, None, ALU.max)
                    ts_(tmp[4], G[3], -40.0, None, ALU.max).then_inc(s("g1_clamp"), 1)
                    if tiles:
                        spread(i)
                yield
                if values:
                    dve.wait_ge(s("k_free"), i * 16)
                    zv = zs.rearrange("p (g h) -> p g h", h=HC)
                    step(stt(zv, zv, SCALE, per_head[:, 0:1, :].to_broadcast([P, NPAGE, HC]), ALU.mult, ALU.add))
                    stt(zsa, zs, -1.0, zs, ALU.mult, ALU.max).then_inc(s("zs_abs"), 1)
                dve.wait_ge(s("p0"), i)
                if head:
                    dve.wait_ge(s("k_rs"), i)
                if out:
                    copy(OS[:, :, bass.ds(i - 2, 1)].rearrange("p h b -> p (h b)"), M[3][:, 16:16 + HC])\
                        .then_inc(s("mixed1"), 1)
                if head:
                    dve.wait_ge(s("kv_out"), hd * 64)
                    dve.wait_ge(s("cv_out"), hd * 16)
                    copy(srow[0:NB, P:3 * P], M[3][0:NB, P:3 * P])
                    tt(wst, M[3][:, 3 * P:4 * P], cm["upto_t"][:, :], ALU.mult)
                    stt(G[0], G[0], cols[:, C_KN:C_KN + 1], tmp[0], ALU.mult, ALU.mult).then_inc(s("kn"), 1)
                if values:
                    dve.wait_ge(s("zs_l"), i)
                    stt(zsa, zs, 0.0, zsa, ALU.max, ALU.add).then_inc(s("s_rest"), 1)
                yield
                if head:
                    dve.wait_ge(s("p1"), i)
                    tt(zs, zs, M[3][:, 128:256], ALU.subtract).then_inc(s("s_lw"), 1)
                    copy(srow[0:NB, 0:P], M[3][0:NB, 0:P])
                    copy(vntok, M[2].rearrange("p (t d) -> p t d", t=NT)).then_inc(s("tok_v"), 1)
                    ts_(tmp[2][:, T:N], tmp[2][:, T:N], per_head[:, 1, bass.ds(hd, 1)],
                        per_head[:, 2, bass.ds(hd, 1)], ALU.mult, ALU.add)
                    dve.wait_ge(s("u_x2"), i)
                    gelu_arg(tmp[0], G[4]).then_inc(s("u_u"), 1)
                    dve.wait_ge(s("g1_sig"), i)
                    tt(G[2], G[2], tmp[3], ALU.mult)
                    step(tt(G[3], G[3], tmp[4], ALU.mult))
                yield
                for k in range(8):
                    if head and k == 0:
                        dve.wait_ge(s("u_sig"), i)
                        step(tt(G[4], G[4], tmp[0], ALU.mult))
                        step(tt(G[4], G[4], G[3], ALU.mult))
                        dve.wait_ge(s("sg"), i)
                        to = wide[:, bass.ds(hd + 8, 1), :].rearrange("p c n -> p (c n)")
                        copy(GS[:, bass.ds(hd, 1), :].rearrange("p c n -> p (c n)"), G[2][:, T:N])
                        tt(to[:, T:N], G[4][:, T:N], tmp[2][:, T:N], ALU.mult)
                        tt(to[:, 0:T], G[4][:, 0:T], M[0], ALU.mult).then_inc(s("od"), 1)
                        dve.wait_ge(s("od"), i)
                    if head and k == 1:
                        dve.wait_ge(s("z"), i)
                        step(ts_(z, m012[:, 0:SB_ALL], SCALE, per_head[:, 0, bass.ds(hd, 1)], ALU.mult, ALU.add))
                        step(masks(z))
                        stt(za, z, -1.0, z, ALU.mult, ALU.max).then_inc(s("z_abs"), 1)
                        dve.wait_ge(s("z_l"), i)
                        step(stt(za, z, 0.0, za, ALU.max, ALU.add))
                        masks(za).then_inc(s("rest"), 1)
                    if head and k == 2:
                        dve.wait_ge(s("between"), i)
                        tt(z, z, m012[:, 0:SB_ALL], ALU.subtract).then_inc(s("lw"), 1)
                    if tiles:
                        if k == 0 and values:
                            dve.wait_ge(s("s_weight"), i)
                        key_pages(i, k)
                    if head and k == 2:
                        dve.wait_ge(s("w_e"), i)
                        masks(za).then_inc(s("weight"), 1)
                    if head and k == 3:
                        dve.wait_ge(s("oc"), i)
                        step(tt(wide[:, bass.ds(hd, 1), 0:T].rearrange("p c n -> p (c n)"), G[2][:, 0:T], M[0],
                                ALU.mult))
                    if values and k == 7:
                        dve.wait_ge(s("v_free"), i * 16)
                        for h in range(2):
                            last = copy(orow[:, 512 * h:512 * h + 512], M[3][32 * h:32 * h + NB, :])
                        last.then_inc(s("orow"), 1)
                    yield

            def l1b(i, mix, tiles=True):
                if tiles:
                    walk("l1b", i, L1B_ORDER, lambda k, x: copy(halves(G[L1B_TO[k]]), x), T_L1B % 2, mix=mix,
                         late={0: (3, 1), 2: (6, 5)})
                finish(mix)

            l1b(0, mix_qv(3, True))
            l1b(1, mix1(1, True, True, True, False))
            step.straight()
            with dve.Fori(2, HC) as i:
                step.body(i, 2, 10)
                l1b(i, mix1(i, True, True, True, True))
            step.end(HC - 2, 10)
            l1b(HC, mix1(HC, False, True, True, True), False)
            l1b(HC + 1, mix1(HC + 1, False, False, False, True), False)
            dve.wait_ge(s("mixed1"), HC)
            tt(wide[:, 0:HC, T:N], OS, GS, ALU.mult).then_inc(s("mixed1_all"), 1)
            dve.wait_ge(s("mixed1_all"), 1)
            take_mixed(3)
            step.straight()

            def row(j, t):
                dve.wait_ge(s("y1_t"), j * 2 + (t + 1))
                copy(yrow[:, bass.ds(j * 256 + P * t, P)], M[2 + t][0:NB, 0:P]).then_inc(s("ys"), 1)

            def rows_out(j, first):
                yield
                if not first:
                    row(j - 1, 1)
                yield
                yield
                row(j, 0)
                yield

            def out1(j, first=False, ahead=2):
                def evac(k, x):
                    dve.wait_ge(s("evac"), j * 2 + (T_OUT1 + k))
                    if not first:
                        dve.wait_ge(s("y1_t"), j * 2 + (k - 1))
                    return residual(1, x, j, k, G[2 + k])

                mix = rows_out(j, first)
                walk("out1", j, OUT_ORDER, evac, 0, mix=mix, ahead=ahead)

            dve.wait_ge(s("act_ready"), 64)
            out1(0, True)
            step.straight()
            with dve.Fori(1, 7) as j:
                step.body(j, 1, 4)
                out1(j)
            step.end(6, 4)
            out1(7, ahead=0)
            row(7, 1)

        def layer1_pages(pool):
            pool.wait_ge(s("ptab"), 16)
            pool.wait_ge(s("st_out"), 128)
            pool.wait_ge(s("s_out"), 128)
            ck, cv = a["cache_k"][0].rearrange("n s h d -> n s (h d)"), a["cache_v"][0].rearrange("n s h d -> n s (h d)")

            def fetch(src, sample, p, slot):
                page = pool.value_load(ptab[0:1, bass.ds(sample * NPAGE + p, 1)], min_val=0, max_val=NPOOL - 1)
                pool.dma_start(pages[:, slot, :], src[bass.ds(page, 1)].rearrange("n s d -> (n s) d"))\
                    .then_inc(s(f"page{slot}"), 16)

            def body(i, keys, values):
                for k in range(8):
                    for x in range(2):
                        if keys:
                            pool.wait_ge(s("k_free"), i * 16 + (2 * k + x - 1 if k else 0))
                            pool.sem_inc(s("pool_waited"), 1)
                            fetch(ck, i, 2 * k + x, x)
                    for x in range(2):
                        if values:
                            pool.wait_ge(s("v_free"), (i - 1) * 16 + (2 * k + x - 1 if k else 0))
                            pool.sem_inc(s("pool_waited"), 1)
                            fetch(cv, i - 1, 2 * k + x, 2 + x)
                    if k == 3 and keys:
                        pool.wait_ge(s("sg"), i)
                        pool.dma_start(ws, a["o_w_s"][0, bass.ds(i, 1)].rearrange("g t s -> t (g s)"))\
                            .then_inc(s("ws_in"), 16)
                        pool.dma_start(brow[0:1, 0:P], a["o_b_s"][0, bass.ds(i, 1)]).then_inc(s("ws_in"), 16)

            with pool.Fori(0, 1) as i:
                body(i, True, False)
            with pool.Fori(1, NB) as i:
                body(i, True, True)
            with pool.Fori(NB, NB + 1) as i:
                body(i, False, True)

        @block.gpsimd
        def _(pool):
            pool.dma_start(ptab[:, :], a["page_table"].rearrange("(o b) p -> o (b p)", o=1)).then_inc(s("ptab"), 16)
            pool.wait_ge(s("xt_a"), KC)
            pool.wait_ge(s("xt_s"), KC)
            pool.dma_start(xt_dram, wide[:, :, :]).then_inc(s("xt_out"), 16)
            pool.wait_ge(s("xt_out"), 16)
            pool.wait_ge(s("la_x"), 1)

            def mix0(i, gla, states):
                pool.wait_ge(s("st_out"), i * 16)
                pool.sem_inc(s("pool_waited"), 1)
                pool.wait_ge(s("os"), i)
                pool.dma_start(st[:, :, :], a[states][0, :, bass.ds(i if gla else i - HEADS, 1)]
                               .rearrange("b h k v -> k b (h v)")).then_inc(s("st_in"), 16)
                if not gla:
                    pool.wait_ge(s("mixed"), i * 2)
                    pool.sem_inc(s("pool_waited"), 1)
                    pool.dma_start(decays, a["ret"][bass.ds(i - HEADS, 1)].rearrange("h p n -> p (h n)"))\
                        .then_inc(s("ret_in"), 16)
                for n in range(1, NCH):
                    pool.wait_ge(s("s_step"), i * 8 + n)
                    pool.sem_inc(s("pool_waited"), 1)
                    pool.tensor_scalar(carry[:, n, :], S[:, (n - 1) % 2, :],
                                       small[:, 6 * (n // 2) + n % 2:6 * (n // 2) + n % 2 + 1], None,
                                       ALU.mult).then_inc(s("carry"), 1)
                pool.wait_ge(s("s_step"), i * 8 + 8)
                pool.sem_inc(s("pool_waited"), 1)
                kind = "gla" if gla else "ret"
                h = i if gla else i - HEADS
                pool.dma_start(a[kind + "_prompt_out"][0, 0, bass.ds(h, 1)].rearrange("h k v -> k (h v)"),
                               S[:, 1, :]).then_inc(s("s_out"), 16)
                pool.wait_ge(s("st_step"), i * 8 + 8)
                pool.sem_inc(s("pool_waited"), 1)
                pool.dma_start(a[kind + "_sample_out"][0, :, bass.ds(h, 1)].rearrange("b h k v -> k b (h v)"),
                               st[:, :, :]).then_inc(s("st_out"), 16)

            with pool.Fori(0, HEADS) as i:
                mix0(i, True, "state_gla")
            pool.wait_ge(s("cum"), HEADS)
            pool.dma_start(rope, a["rope"]).then_inc(s("rope_in"), 16)
            with pool.Fori(HEADS, 2 * HEADS) as i:
                mix0(i, False, "state_ret")

            pool.wait_ge(s("act_ready"), 32)
            with pool.Fori(0, 8) as j:
                for t in range(2):
                    pool.wait_ge(s("evac"), j * 2 + (T_OUT0 + t - 1))
                    pool.sem_inc(s("pool_waited"), 1)
                    pool.dma_start(G[t], xt_dram[:, bass.ds(j * 2 + t, 1), :].rearrange("p c n -> p (c n)"))\
                        .then_inc(s(f"xj{t}"), 16)
            pool.wait_ge(s("evac"), T_OUT0 + 16)
            pool.dma_start(x1_dram, wide[:, :, :]).then_inc(s("x1_out"), 16)
            pool.wait_ge(s("x1_out"), 16)
            layer1_pages(pool)

            def fetch_x(j, t):
                pool.wait_ge(s("evac"), j * 2 + (T_OUT1 + t - 1))
                pool.sem_inc(s("pool_waited"), 1)
                pool.dma_start(G[t], x1_dram[:, bass.ds(j * 2 + t, 1), :].rearrange("p c n -> p (c n)"))\
                    .then_inc(s(f"xj{t}"), 16)

            def store_y(j, t):
                pool.wait_ge(s("yo"), j * 2 + (t + 1))
                pool.sem_inc(s("pool_waited"), 1)
                pool.dma_start(a["y_prompt_out"][0].rearrange("(q p) n -> p q n", p=P)
                               [:, :, bass.ds(j * 256 + P * t, P)],
                               yo[t].rearrange("p (q n) -> p q n", q=NT)).then_inc(s(f"y_out{t}"), 16)

            pool.wait_ge(s("act_ready"), 64)
            fetch_x(0, 0)
            fetch_x(0, 1)
            with pool.Fori(1, 8) as j:
                fetch_x(j, 0)
                store_y(j - 1, 0)
                fetch_x(j, 1)
                store_y(j - 1, 1)
            store_y(7, 0)
            store_y(7, 1)
            pool.wait_ge(s("ys"), 16)
            pool.dma_start(a["y_sample_out"].rearrange("b o d -> (b o) d"), yrow).then_inc(s("ys_out"), 16)
            for name, value in (("ys_out", 16), ("y_out0", 128), ("y_out1", 128), ("st_out", 128), ("s_out", 128), ("kv_out", 512),
                                ("cv_out", 128)):
                pool.wait_ge(s(name), value)

        return


_INS = ["x_prompt", "x_sample", "state_gla", "state_ret", "cache_k", "cache_v", "page_table",
        "c_prompt", "c_sample", "e_norm_g", "e_w_ada", "e_b_ada", "e_w_in", "e_w_a2", "e_b_a",
        "e_gla_norm_g", "e_ret_norm_g", "e_w_out", "o_norm_g", "o_w_ada", "o_b_ada", "o_w_in",
        "o_q_norm_g", "o_k_norm_g", "o_sb_offset", "o_v_norm_g", "o_w_s", "o_b_s", "o_w_out"]
_OUTS = [("y_prompt", (1, T, D)), ("y_sample", (NB, 1, D)),
         ("gla_prompt", (1, 1, HEADS, P, 256)), ("gla_sample", (1, NB, HEADS, P, 256)),
         ("ret_prompt", (1, 1, HEADS, P, 256)), ("ret_sample", (1, NB, HEADS, P, 256)),
         ("k_prompt", (1, 1, T, HC, P)), ("v_prompt", (1, 1, T, HC, P)),
         ("k_sample", (1, NB, 1, HC, P)), ("v_sample", (1, NB, 1, HC, P)), ("chunk_v", (1, NB, 1, BR))]


def kernel(**inputs):
    import concourse.bacc as bacc
    from concourse.bass_utils import run_bass_kernel_spmd

    nc = bacc.Bacc("TRN2", target_bir_lowering=False, num_devices=1)
    cst = constants()
    arrays, a, o = {}, {}, {}
    for name in _INS:
        x = np.ascontiguousarray(inputs[name])
        arrays["in_" + name] = x
        a[name] = nc.dram_tensor("in_" + name, x.shape, mybir.dt.from_np(x.dtype), kind="ExternalInput").ap()
    c_aps = {}
    for name, x in cst.items():
        arrays["const_" + name] = x
        c_aps[name] = nc.dram_tensor("const_" + name, x.shape, F32, kind="ExternalInput").ap()
    a["ret"], a["rope"] = c_aps["ret"], c_aps["rope"]
    for name, shape in _OUTS:
        a[name + "_out"] = nc.dram_tensor("out_" + name, shape, F32, kind="ExternalOutput").ap()
    build(nc, a, o, c_aps)
    r = run_bass_kernel_spmd(nc, [arrays], core_ids=[0])
    return tuple(r.results[0]["out_" + name] for name, _ in _OUTS)
```

```python
from contextlib import ExitStack

import numpy as np
import concourse.bass as bass
from concourse import mybir

F32 = mybir.dt.float32
F32R = mybir.dt.float32r
I32 = mybir.dt.int32
ALU = mybir.AluOpType
ACT = mybir.ActivationFunctionType

P = 128
D = 2048
KC = D // P
T = 512
NB = 8
N = T + NB
HALF = N // 2
NT = T // P
HEADS = 4
RANK = 16
CH = 64
NCH = T // CH
NPAGE, PAGE, NPOOL = 16, 128, 160
HC = 8
BR = D // 2
EPS = 1e-6
DH = P
SCALE = float(DH) ** -0.5
GELU = 1.5957691216057308
SB_OFF = {0: 0, 1: 512, 3: 896, 2: 1024}
SB_ALL = 1280
BIG = 3.0e38

E_QA, E_KA, E_VA, E_RA, E_GA = 0, 512, 1024, 2048, 2064
E_QB, E_KB, E_VB, E_GB = 3088, 3600, 4112, 5136
O_Q, O_K, O_V, O_G, O_U, O_VD, O_GD = (BR * n for n in range(7))

U_ADA0, U_RA, U_L0, U_GATE1, U_OUT0, U_L1A, U_L1B, U_OUT1 = 0, 96, 98, 258, 290, 322, 354, 434
T_RA, T_L0, T_OUT0, T_L1A, T_L1B, T_OUT1 = 0, 1, 49, 65, 81, 121
RAW_DEPTH = 4
TILE, MOD = "tile", "mod"
MOD_ORDER = [MOD] * 4
L0_ORDER = [TILE, MOD, TILE, MOD, TILE, MOD, TILE, MOD, TILE, TILE]
L1A_ORDER = [TILE] * 4
L1B_ORDER = [TILE] * 5
OUT_ORDER = [TILE] * 2
L1B_SLOTS = [2, 3, 0, 1, 4]
L0_TO, L1A_TO, L1B_TO = [0, 1, 3, 2, 4, 5], [0, 1, 2, 3], [4, 3, 2, 1, 0]

C_BADA, C_NORM, C_MIX, C_VN, C_QN, C_KN = (0, 48), (96, 112), 128, 144, 152, 153


def constants():
    c = {}
    c["ident"] = np.eye(P)
    t = np.arange(P)
    same = (t[:, None] // CH) == (t[None, :] // CH)
    mid = (t // CH) * CH + CH // 2 - 1
    upto = (same & (t[:, None] <= t[None, :])).astype(np.float64)
    to_mid = (same & (t[:, None] <= mid[None, :])).astype(np.float64)
    c["cum_mid"] = (upto - to_mid) / 16.0
    small = np.zeros((P, 6))
    for n in range(2):
        m, last = to_mid[:, n * CH], upto[:, n * CH + CH - 1]
        small[:, n], small[:, 2 + n], small[:, 4 + n] = m, last, last - m
    c["cum_small"] = small / 16.0
    c["chunk_mask"] = same & (t[:, None] <= t[None, :])
    c["below"] = t[:, None] < t[None, :]
    c["from_key"] = t[:, None] >= t[None, :]
    c["upto_t"] = t[:, None] <= t[None, :]
    c["swap"] = np.roll(np.eye(P), P // 2, axis=0)
    c = {k: np.ascontiguousarray(v, dtype=np.float32) for k, v in c.items()}
    pos = np.concatenate([np.arange(T), np.full(NB, NPAGE * PAGE)]).astype(np.float32)
    half = P // 2
    inv = (np.float32(10000.0) ** (-np.arange(half, dtype=np.float32) / np.float32(half))).astype(np.float32)
    ang = (pos[None, :] * inv[:, None]).astype(np.float32).astype(np.float64)
    c["rope"] = np.stack([np.concatenate([np.cos(ang)] * 2, 0),
                          np.concatenate([-np.sin(ang), np.sin(ang)], 0)], 1).astype(np.float32)
    lg = np.log1p(-np.exp2(-5.0 - np.arange(HEADS)))
    rel = np.arange(T) % CH - (CH // 2 - 1)
    m, last = CH // 2, CH
    sm = np.zeros((HEADS, 32))
    for tile in range(NT):
        sm[:, 6 * tile:6 * tile + 6] = np.exp(lg[:, None] * np.array([m, m, last, last, last - m, last - m]))
    sm[:, 24:] = np.exp(lg)[:, None]
    ret = np.concatenate([np.exp(lg[:, None] * rel), np.exp(-lg[:, None] * rel), sm], 1)
    c["ret"] = ret[:, None, :].repeat(P, 1).astype(np.float32)
    return c


CHIP = ("ident", "cum_mid", "cum_small", "chunk_mask", "below", "from_key", "upto_t", "swap")


def build(nc, a, o, cst):
    ctx = ExitStack()
    with ctx:
        def sb(name, shape, dt=F32):
            return ctx.enter_context(nc.sbuf_tensor(name, shape, dt))

        sems = {}

        def s(name):
            if name not in sems:
                sems[name] = ctx.enter_context(nc.semaphore(name))
            return sems[name]

        xt_dram = nc.dram_tensor("xt_scratch", [P, KC, N], F32).ap()
        x1_dram = nc.dram_tensor("x1_scratch", [P, KC, N], F32).ap()

        act_hi = sb("act_hi", [P, KC, N], F32R)
        act_lo = sb("act_lo", [P, KC, N], F32R)
        wide = sb("wide", [P, KC, N])
        raw = sb("raw", [P, 5, 1024])
        w_hi = sb("w_hi", [P, 2, 1024], F32R)
        w_lo = sb("w_lo", [P, 2, 1024], F32R)
        cm = {k: sb("c_" + k, list(cst[k].shape)) for k in CHIP}
        ident = cm["ident"]
        ones = sb("ones", [P, P])
        mod = [sb("mod0", [P, 48, 9]), sb("mod1", [P, 48, 9])]
        cols = sb("cols", [P, 154])
        per_head = sb("per_head", [P, 3, HC])
        cond = sb("cond", [P, KC, 9])
        arena = sb("arena", [P, 16600])
        used = [0]

        def region(n):
            at = used[0]
            used[0] += n
            assert used[0] <= 16600, used[0]
            return arena[:, at:at + n]

        mrow = region(512)
        G = [region(N) for _ in range(6)]
        t0_at = used[0]
        tmp = [region(N) for _ in range(5)]
        base = used[0]
        la = region(NT * T).rearrange("p (t k) -> p t k", t=NT)
        rope = arena[:, base:base + 2 * N].rearrange("p (a n) -> p a n", a=2)
        decays = region(2 * T + 32)
        up, down, small = decays[:, 0:T], decays[:, T:2 * T], decays[:, 2 * T:2 * T + 32]
        vtok = region(NT * 256).rearrange("p (t d) -> p t d", t=NT)
        ktok = region(NT * P).rearrange("p (t d) -> p t d", t=NT)
        carry = region(8 * 256).rearrange("p (n d) -> p n d", n=8)
        st = region(8 * 256).rearrange("p (n d) -> p n d", n=8)
        S = region(2 * 256).rearrange("p (n d) -> p n d", n=2)
        sdec = region(32)
        lah = raw[:, 4, 0:512].rearrange("p (t k) -> p t k", t=NT)
        sct = raw[:, 4, 512:1024].rearrange("p (t k) -> p t k", t=NT)
        kmask = arena[0:NB, t0_at + N:t0_at + N + 1024].rearrange("p (b k) -> p b k", b=NB)
        srow0 = tmp[3][0:NB, 0:384]
        hs = G[5][:, 0:KC * NB].rearrange("p (c n) -> p c n", n=NB)
        used[0] = 512
        xin = region(5 * D).rearrange("p (t d) -> p t d", t=5)
        crow = region(D)
        rowa, rowb = region(P), region(P)
        csm = region(9 * KC)
        csm2 = region(9 * KC)
        wa2 = region(T)[0:RANK + 1, :]
        used[0] = base
        z = region(SB_ALL)
        za = region(SB_ALL)
        ktok1 = region(512).rearrange("p (t d) -> p t d", t=NT)
        vtok1 = region(512).rearrange("p (t d) -> p t d", t=NT)
        vntok = tmp[2][:, 0:T].rearrange("p (t d) -> p t d", t=NT)
        wst = region(P)
        ws = region(P)
        pages = region(5 * 1024).rearrange("p (n d) -> p n d", n=5)
        srow = mrow[:, 128:512]
        brow = mrow
        qb = region(1024)
        wv = mod[0].rearrange("p c n -> p (c n)")[:, 0:128]
        pair_a = arena[:, t0_at:t0_at + 2 * N]
        pair_b = arena[:, t0_at + 2 * N:t0_at + 4 * N]
        pair_c = arena[:, t0_at + 3 * N:t0_at + 5 * N]
        g01, g23, g45 = (arena[:, 512 + 2 * N * n:512 + 2 * N * n + 2 * N] for n in range(3))
        OS = region(64).rearrange("p (h b) -> p h b", h=HC)
        GS = region(64).rearrange("p (h b) -> p h b", h=HC)
        zs = region(128)
        zsa = region(128)
        dg = za[:, 0:1024]
        orow = z[0:NB, 0:1024]
        eps = sb("eps", [P, 1])
        vla = arena[:, 512:512 + 2048]
        sda = arena[:, 512 + 2048:512 + 2080]
        ptab = sb("ptab", [1, NB * NPAGE], I32)
        yrow = arena[0:NB, base:base + D]
        yo = [arena[:, base + D + 512 * n:base + D + 512 * n + 512] for n in range(2)]

        pt = [ctx.enter_context(nc.psum_tensor(f"pt{n}", [P, 2, 512], F32)) for n in range(2)]
        m012 = ctx.enter_context(nc.psum_tensor("m012", [P, 1536], F32))
        m3 = ctx.enter_context(nc.psum_tensor("m3", [P, 512], F32))
        M = [m012[:, 512 * n:512 * n + 512] for n in range(3)] + [m3[:, :]]

        ra_rows = G[0][0:RANK + 1, :]

        phases = {}
        have = [0] * 5
        kinds, counts, count, stream = {}, {}, {TILE: 0, MOD: 0}, []
        for name, first, iters, order in (("ada0", U_ADA0, 12, [MOD] * 4), ("ra", U_RA, 1, [TILE]),
                                          ("l0", U_L0, 8, L0_ORDER), ("gate1", U_GATE1, 4, MOD_ORDER),
                                          ("out0", U_OUT0, 8, OUT_ORDER),
                                          ("l1a", U_L1A, 4, L1A_ORDER), ("l1b", U_L1B, 8, L1B_ORDER),
                                          ("out1", U_OUT1, 8, OUT_ORDER)):
            units = 2 * len(order)
            tiles = 2 * order.count(TILE)
            kinds[name] = [k for k in order for _ in range(2)]
            slots = [L1B_SLOTS[u % 5] if name == "l1b" else (first + u) % 4 for u in range(units + 2)]
            rank = [slots[:u].count(slots[u]) for u in range(units + 2)]
            per = [slots[:units].count(x) for x in range(5)]
            phases[name] = (first, units, slots, rank, per, list(have))
            counts[name] = (tiles, count[TILE], units - tiles, count[MOD])
            stream += kinds[name] * iters
            count[TILE] += iters * tiles
            count[MOD] += iters * (units - tiles)
            have = [h + iters * p for h, p in zip(have, per)]

        def unit(name, i, u):
            first, units, slots, rank, per, before = phases[name]
            sl = slots[u]
            return first + i * units + u, sl, (i * per[sl] + (before[sl] + rank[u] + 1)) * 16

        def tile_no(name, i, u):
            per, before, _, _ = counts[name]
            n = sum(k is TILE for k in kinds[name][:max(u, 0)]) + max(u - len(kinds[name]), 0)
            if u < 0:
                n = -sum(k is TILE for k in kinds[name][u:])
            return i * per + (before + n)

        def mod_no(name, i, u):
            _, _, per, before = counts[name]
            n = sum(k is MOD for k in kinds[name][:max(u, 0)])
            if u < 0:
                n = -sum(k is MOD for k in kinds[name][u:])
            return i * per + (before + n)

        def key_slot(p):
            return p % 2, p // 2 + 1

        def value_slot(p, keys):
            return (2 + p % 3, p // 3 + 1) if keys else ((p + 2) % 5, p // 5 + 1)

        def value_loads(i, slot, keys):
            if keys:
                return (i - 1) * (6 if slot == 2 else 5)
            return 8 * NB if slot < 2 else (NB - 1) * (6 if slot == 2 else 5)

        class Chain:

            def __init__(self, eng, name):
                self.eng, self.name, self.base, self.at, self.n = eng, name, 0, 0, 0

            def body(self, i, first, per):
                self.at, self.n = self.base + (i - first) * per, 0

            def end(self, iters, per):
                assert self.n == per, (self.name, self.n)
                self.base += iters * per
                self.at, self.n = self.base, 0

            def __call__(self, ins):
                ins.then_inc(s(self.name), 1)
                self.n += 1
                self.eng.wait_ge(s(self.name), self.at + self.n)

            def straight(self):
                self.base, self.at, self.n = self.base + self.n, self.base + self.n, 0

        NCONST = len(CHIP) - 1 + 3 + 2
        NFIRST = 12
        block = ctx.enter_context(nc.Block())

        @block.sync
        def _(sp):
            def const(dst, src):
                sp.dma_start(dst, src).then_inc(s("const_in"), 16)

            def first(dst, src):
                sp.dma_start(dst, src).then_inc(s("first_in"), 16)

            first(rowa[0:48, :], a["e_b_ada"].rearrange("o (r c) -> (o r) c", c=P))
            first(rowa[48:96, :], a["o_b_ada"].rearrange("o (r c) -> (o r) c", c=P))
            at = 0
            for name, k in (("e_norm_g", 16), ("o_norm_g", 16), ("e_gla_norm_g", 8), ("e_ret_norm_g", 8),
                            ("o_v_norm_g", 8), ("o_q_norm_g", 1), ("o_k_norm_g", 1)):
                first(rowb[at:at + k, :], a[name].rearrange("o (r c) -> (o r) c", c=P))
                at += k

            def constant_tables():
                for k in CHIP[1:]:
                    const(cm[k][:, :], cst[k])
                for n, src in enumerate((a["o_sb_offset"][0, :], a["o_w_s"][0, :, 0, 0], a["o_b_s"][0, :, 0])):
                    with nc.allow_non_contiguous_dma(reason="eight scalars"):
                        const(per_head[:, n, :], src.partition_broadcast(P))
                const(wa2[0:RANK, :], a["e_w_a2"][0])
                const(wa2[RANK:RANK + 1, :], a["e_b_a"])

            def kind_before(name, i, u):
                if isinstance(i, int):
                    return stream[unit(name, i, u)[0] - RAW_DEPTH]
                return kinds[name][u - RAW_DEPTH]

            def units_before(name, i, u, number):
                if isinstance(i, int):
                    return stream[:unit(name, i, u)[0] - RAW_DEPTH + 1].count(TILE if number is tile_no else MOD)
                return number(name, i, u - RAW_DEPTH + 1)

            def load(name, i, u, src):
                n, sl, _ = unit(name, i, u)
                if not (isinstance(n, int) and n < RAW_DEPTH):
                    if kind_before(name, i, u) is MOD:
                        sp.wait_ge(s("pe_mod"), units_before(name, i, u, mod_no))
                    else:
                        sp.wait_ge(s("split_hi"), units_before(name, i, u, tile_no))
                        sp.wait_ge(s("split_lo"), units_before(name, i, u, tile_no))
                sp.dma_start(raw[:, sl, :].rearrange("p (c n) -> p c n", c=src.shape[1]), src)\
                    .then_inc(s(f"raw{sl}"), 16)

            def load_tile(name, i, u, w, col):
                for hh in range(2):
                    load(name, i, u + hh, w[:, 8 * hh:8 * hh + 8, bass.ds(col, P)])

            def load_mod(name, i, u, w, col, pair):
                for hh in range(2):
                    k = 2 * (2 * pair + hh)
                    load(name, i, u + hh, w[:, k:k + 2, bass.ds(col, 512)])

            def weights(name, i, order, w_tile, tile_cols, w_mod=None, mod_col=None):
                t = m = 0
                for n, what in enumerate(order):
                    if what is TILE:
                        load_tile(name, i, 2 * n, w_tile, tile_cols[t])
                        t += 1
                    else:
                        load_mod(name, i, 2 * n, w_mod, mod_col, m)
                        m += 1

            v = {k: a[k][0].rearrange("(c p) n -> p c n", p=P)
                 for k in ("e_w_ada", "o_w_ada", "e_w_in", "o_w_in", "e_w_out", "o_w_out")}
            for u in range(4):
                load("ada0", 0, u, v["e_w_ada"][:, 2 * u:2 * u + 2, 0:512])
            constant_tables()
            for u in range(4, 8):
                load("ada0", 0, u, v["e_w_ada"][:, 2 * u:2 * u + 2, 0:512])
            with sp.Fori(1, 12) as g:
                weights("ada0", g, MOD_ORDER, None, None, v["e_w_ada"], g * 512)
            load_tile("ra", 0, 0, v["e_w_in"], E_RA)

            def gla_cols(i):
                return [i * 256 + E_VA, i * 256 + (E_VA + P), (i + E_KA // P) * P, i * P + E_QA,
                        i * 256 + E_GA, i * 256 + (E_GA + P)]

            def ret_cols(i):
                b = HEADS
                return [i * 256 + (E_VB - 256 * b), i * 256 + (E_VB + P - 256 * b), i * P + (E_KB - P * b),
                        i * P + (E_QB - P * b), i * 256 + (E_GB - 256 * b), i * 256 + (E_GB + P - 256 * b)]

            weights("l0", 0, L0_ORDER, v["e_w_in"], gla_cols(0), v["o_w_ada"], 0)
            with sp.Fori(1, HEADS) as i:
                weights("l0", i, L0_ORDER, v["e_w_in"], gla_cols(i), v["o_w_ada"], i * 512)
            with sp.Fori(HEADS, 2 * HEADS) as i:
                weights("l0", i, L0_ORDER, v["e_w_in"], ret_cols(i), v["o_w_ada"], i * 512)
            weights("gate1", 0, MOD_ORDER, None, None, v["o_w_ada"][:, :, 2 * D:3 * D], 0)
            with sp.Fori(1, 4) as g:
                weights("gate1", g, MOD_ORDER, None, None, v["o_w_ada"][:, :, 2 * D:3 * D], g * 512)
            weights("out0", 0, OUT_ORDER, v["e_w_out"], [0, P])
            with sp.Fori(1, 8) as j:
                weights("out0", j, OUT_ORDER, v["e_w_out"], [j * 256, j * 256 + P])
            with sp.Fori(0, 4) as j:
                weights("l1a", j, L1A_ORDER, v["o_w_in"],
                        [j * 256 + O_Q, j * 256 + (O_Q + P), j * 256 + O_VD, j * 256 + (O_VD + P)])
            with sp.Fori(0, 8) as i:
                weights("l1b", i, L1B_ORDER, v["o_w_in"], [i * P + c for c in (O_U, O_GD, O_G, O_V, O_K)])
            with sp.Fori(0, 8) as j:
                weights("out1", j, OUT_ORDER, v["o_w_out"], [j * 256, j * 256 + P])


        def split_ahead(order, ahead):
            us = [u for u in range(2 * len(order)) if order[u // 2] is TILE]
            after = us + [2 * len(order), 2 * len(order) + 1]
            return {u: after[k + 2] for k, u in enumerate(us) if k + 2 < len(us) + ahead}

        def goes_on(name, order, u, always):
            return order[u // 2] is TILE or always or (name == "l0" and u == 14)

        def go_on(mix):
            if mix is not None:
                next(mix, None)

        def finish(mix):
            for _ in mix:
                pass

        @block.tensor
        def _(pe):
            def mm(out, lhsT, rhs, start=True, stop=True):
                return pe.matmul(out, lhsT, rhs, start=start, stop=stop, skip_group_check=True)

            def tr(out, x):
                k = x.shape[0]
                return pe.transpose(out, x, ident[0:k, 0:k])

            def unit_ready(name, i, u):
                n = tile_no(name, i, u)
                pe.wait_ge(s("split_hi"), n + 1)
                pe.wait_ge(s("split_lo"), n + 1)
                return tile_no(name, 0, u) % 2

            def tile_unit(name, i, u, hh, par, stage):
                b = unit_ready(name, i, u)
                for k in range(8):
                    c = 8 * hh + k
                    if stage is not None:
                        pe.wait_ge(s("act_ready"), 16 * stage + c + 1)
                    hi, lo = w_hi[:, b, P * k:P * k + P], w_lo[:, b, P * k:P * k + P]
                    for w, x in ((hi, act_hi), (hi, act_lo), (lo, act_hi)):
                        for h in range(2):
                            last = mm(pt[par][:, h, 0:HALF], w, x[:, c, HALF * h:HALF * h + HALF],
                                      start=(c == 0 and w is hi and x is act_hi), stop=(c == 15 and w is lo))
                last.then_inc(s("pe_tile"), 1)

            def mod_unit(name, i, u, k0, bank):
                _, sl, loaded = unit(name, i, u)
                pe.wait_ge(s(f"raw{sl}"), loaded)
                for k in range(2):
                    c = k0 + k
                    last = mm(bank[0:9, :], cond[:, c, :], raw[:, sl, 512 * k:512 * k + 512],
                              start=(c == 0), stop=(c == 15))
                last.then_inc(s("pe_mod"), 1)

            def mod_fold(g, bank):
                pe.wait_ge(s("mod_row"), g + 1)
                for j in range(4):
                    last = mm(bank[:, 9 * j:9 * j + 9], mrow[0:9, P * j:P * j + P], ident[0:9, 0:9])
                last.then_inc(s("mod_col"), 1)

            def walk(name, i, order, tile0=None, par0=None, stage=None, group=None, late0=0, mix=None,
                     always=False):
                go_on(mix)
                t = m = 0
                fold = False
                for u in range(2 * len(order)):
                    kind, hh = order[u // 2], u % 2
                    if kind is TILE:
                        if hh == 0:
                            pe.wait_ge(s("evac"), tile0 + t - 1 + (late0 if t == 0 else 0))
                        tile_unit(name, i, u, hh, (par0 + t) % 2, stage if t == 0 else None)
                        t += hh
                    else:
                        if m == 0:
                            pe.wait_ge(s("mod_read"), group)
                        mod_unit(name, i, u, 2 * m, M[3])
                        m += 1
                    if fold:
                        mod_fold(group, M[3])
                        fold = False
                    fold = kind is MOD and m == 8
                    if goes_on(name, order, u, always):
                        go_on(mix)
                if fold:
                    mod_fold(group, M[3])

            pe.wait_ge(s("first_in"), 16 * NFIRST)
            tr(M[0][:, 0:96], rowa[0:96, :])
            tr(M[0][:, 96:154], rowb[0:58, :]).then_inc(s("cols_t"), 1)
            for k in range(KC):
                last = tr(M[1][:, 9 * k:9 * k + 9], crow[0:9, P * k:P * k + P])
            last.then_inc(s("cond_t"), 1)
            pe.wait_ge(s("x_in"), 80)
            pe.wait_ge(s("cols"), 1)
            pe.wait_ge(s("cond_cols"), 1)
            for c in range(KC):
                b = c % 2
                if c >= 2:
                    pe.wait_ge(s("xt_a"), c - 1)
                    pe.wait_ge(s("xt_s"), c - 1)
                for t in range(NT):
                    tr(M[b][:, P * t:P * t + P], xin[:, t, P * c:P * c + P])
                tr(M[2 + b][:, 0:8], xin[0:NB, 4, P * c:P * c + P]).then_inc(s("xt"), 1)
            pe.wait_ge(s("cond"), 1)
            pe.wait_ge(s("xt_s"), KC)

            def feature_sum(src, big, small_, done):
                mm(big, ones[:, :], src[:, 0:T])
                mm(small_, ones[:, :], src[:, T:N]).then_inc(s(done), 1)

            def ada0(g, odd):
                for u in range(8):
                    if u == 0 and not (isinstance(g, int) and g < 2):
                        pe.wait_ge(s("mod_read"), g - 1)
                    mod_unit("ada0", g, u, 2 * u, M[2 + odd])
                    if u == 0 and not (isinstance(g, int) and g == 0):
                        mod_fold(g - 1, M[3 - odd])

            ada0(0, 0)
            pe.wait_ge(s("x_sq"), 1)
            feature_sum(tmp[4], M[0], M[1][:, 0:8], "x_ss")
            ada0(1, 1)
            with pe.Fori(1, 6) as g:
                ada0(g * 2, 0)
                ada0(g * 2 + 1, 1)
            mod_fold(11, M[3])
            pe.wait_ge(s("const_in"), 16 * NCONST)

            walk("ra", 0, [TILE], 1, 0, stage=0)
            pe.wait_ge(s("ra"), 1)
            for t in range(NT):
                mm(M[t], ra_rows[:, P * t:P * t + P], wa2)
            for h in range(HEADS):
                last = mm(pt[1][:, 0, 8 * h:8 * h + 8], wa2[:, P * h:P * h + P], ra_rows[:, T:N])
            last.then_inc(s("la_x"), 1)
            pe.wait_ge(s("la_copied"), 1)

            def mix0(i, gla):
                yield
                pe.wait_ge(s("evac"), i * 6 + (T_L0 + 6))
                if gla:
                    pe.wait_ge(s("lah"), i + 1)
                    for t in range(NT):
                        mm(M[0][:, P * t:P * t + P], lah[:, t, :], cm["cum_mid"][:, :])
                        last = mm(M[1][:, 6 * t:6 * t + 6], lah[:, t, :], cm["cum_small"][:, :])
                    last.then_inc(s("cum"), 1)
                else:
                    mm(M[0], cm["swap"][:, :], G[2][:, 0:T])
                    mm(M[1], cm["swap"][:, :], G[3][:, 0:T])
                    mm(M[2][:, 0:8], cm["swap"][:, :], G[2][:, T:N])
                    mm(M[2][:, 8:16], cm["swap"][:, :], G[3][:, T:N]).then_inc(s("swapped"), 1)
                yield
                pe.wait_ge(s("qk"), i + 1)
                for t in range(NT):
                    for d in range(2):
                        tr(M[1 + t // 2][:, 256 * (t % 2) + P * d:256 * (t % 2) + P * d + P],
                           G[d][:, P * t:P * t + P])
                tr(M[0][0:NB, 0:P], G[3][:, T:N])
                tr(M[0][0:NB, P:2 * P], G[0][:, T:N])
                tr(M[0][0:NB, 2 * P:3 * P], G[1][:, T:N]).then_inc(s("v_t"), 1)
                yield
                pe.wait_ge(s("srow0"), i + 1)
                for t in range(NT):
                    tr(M[0][:, P * t:P * t + P], G[3][:, P * t:P * t + P])
                pe.wait_ge(s("vtok"), i + 1)
                for t in range(NT):
                    last = mm(M[2][:, P * t:P * t + P], G[3][:, P * t:P * t + P], G[2][:, P * t:P * t + P])
                last.then_inc(s("sc"), 1)
                yield
                pe.wait_ge(s("ktok"), i + 1)
                for n in range(NCH):
                    if n == 4:
                        yield
                        pe.wait_ge(s("s_step"), i * 8 + 4)
                    r = CH * (n % 2)
                    last = mm(M[n % 2][:, 128 * (n % 4 - n % 2):128 * (n % 4 - n % 2) + 256],
                              ktok[r:r + CH, n // 2, :], vtok[r:r + CH, n // 2, :])
                    if n % 4 == 3:
                        last.then_inc(s("kv"), 1)
                yield
                pe.wait_ge(s("s_step"), i * 8 + 8)
                pe.wait_ge(s("kmask"), i + 1)
                pe.wait_ge(s("sct"), i + 1)
                pe.wait_ge(s("carry"), i * 7 + 7)
                for d in range(2):
                    if d:
                        pe.wait_ge(s("st_step"), i * 8 + 4)
                        pe.wait_ge(s("o_a"), i * 2 + 1)
                    for b in range(4 * d, 4 * d + 4):
                        last = mm(M[b // 2 % 2][:, 256 * (b % 2):256 * (b % 2) + 256], kmask[:, b, :],
                                  srow0[:, P:3 * P])
                    last.then_inc(s("outer"), 1)
                    for t in range(NT):
                        mm(M[2][:, P * t:P * t + P], vtok[:, t, P * d:P * d + P], sct[:, t, :],
                           start=True, stop=False)
                        for n in (2 * t, 2 * t + 1):
                            if n:
                                last = mm(M[2][:, CH * n:CH * n + CH], carry[:, n, P * d:P * d + P],
                                          G[2][:, CH * n:CH * n + CH], start=False, stop=True)
                    last.then_inc(s("o"), 1)
                    yield
                pe.wait_ge(s("st_step"), i * 8 + 8)
                for d in range(2):
                    for b in range(NB):
                        last = mm(M[0][:, 8 * d + b:8 * d + b + 1], st[:, b, P * d:P * d + P], G[2][:, T + b:T + b + 1])
                    if d == 0:
                        yield
                last.then_inc(s("os"), 1)
                yield
                pe.wait_ge(s("osq"), i + 1)
                feature_sum(tmp[2], M[0], M[1][:, 0:8], "oss")
                yield

            def l0(i, mix=None):
                walk("l0", i, L0_ORDER, i * 6 + T_L0, 1, group=i + 12, mix=mix)
                if mix is not None:
                    finish(mix)

            l0(0)
            with pe.Fori(1, HEADS) as i:
                l0(i, mix0(i - 1, True))
            l0(HEADS, mix0(HEADS - 1, True))
            with pe.Fori(HEADS + 1, 2 * HEADS) as i:
                l0(i, mix0(i - 1, False))
            mix = mix0(2 * HEADS - 1, False)
            walk("gate1", 0, MOD_ORDER, group=20, mix=mix, always=True)
            walk("gate1", 1, MOD_ORDER, group=21, mix=mix, always=True)
            finish(mix)
            with pe.Fori(2, 4) as g:
                walk("gate1", g, MOD_ORDER, group=g + 20)
            walk("out0", 0, OUT_ORDER, T_OUT0, T_OUT0 % 2, stage=1)
            with pe.Fori(1, 8) as j:
                walk("out0", j, OUT_ORDER, j * 2 + T_OUT0, T_OUT0 % 2)
            pe.wait_ge(s("x_sq"), 2)
            feature_sum(tmp[4], M[0], M[1][:, 0:8], "x_ss")

            def mix_qv(j, last_one=False):
                yield
                pe.wait_ge(s("q_sq"), j + 1)
                for t in range(2):
                    mm(M[t], ones[:, :], tmp[t][:, 0:T])
                    last = mm(M[2][:, 8 * t:8 * t + 8], ones[:, :], tmp[t][:, T:N])
                last.then_inc(s("q_ss"), 1)
                yield
                if last_one:
                    yield
                    spread_queries(0)
                    yield
                    yield
                    pe.wait_ge(s("vd_sq"), 4)
                    feature_sum(tmp[4], M[0], M[1][:, 0:8], "vd_ss")
                yield

            def spread_queries(b):
                pe.wait_ge(s("dg"), b + 1)
                for h in range(2):
                    last = mm(M[1 + h], ones[:, :], dg[:, 512 * h:512 * h + 512])
                last.then_inc(s("qb_t"), 1)

            def l1a(j, stage=None, mix=None):
                walk("l1a", j, L1A_ORDER, j * 4 + T_L1A, T_L1A % 2, stage=stage, mix=mix)

            l1a(0, stage=2)
            with pe.Fori(1, 4) as j:
                l1a(j, mix=mix_qv(j - 1))

            def mix1(i, tiles, head, values, out):
                yield
                if out:
                    pe.wait_ge(s("orow"), i - 1)
                    for h in range(HC):
                        last = mm(M[3][:, 16 + h:17 + h], orow[:, P * h:P * h + P], ident[0:NB, h:h + 1])
                if head:
                    pe.wait_ge(s("evac"), i * 5 + T_L1B)
                    pe.wait_ge(s("k_sq"), i)
                    pe.wait_ge(s("g1_clamp"), i)
                    pe.wait_ge(s("ws_in"), i * 32)
                    mm(M[0], ones[:, :], tmp[0][:, 0:T])
                    mm(M[3][:, 0:8], ones[:, :], tmp[0][:, T:N])
                    tr(M[3][0:NB, P:2 * P], G[1][:, T:N])
                    tr(M[3][0:NB, 2 * P:3 * P], tmp[2][:, T:N])
                    last = tr(M[3][:, 3 * P:4 * P], ws)
                last.then_inc(s("p0"), 1)
                if tiles and head:
                    spread_queries(i)
                yield
                if head:
                    pe.wait_ge(s("kn"), i)
                    if tiles:
                        pe.wait_ge(s("qb"), i + 1)
                    for t in range(NT):
                        tr(M[0][:, P * t:P * t + P], G[0][:, P * t:P * t + P])
                        tr(M[1][:, P * t:P * t + P], G[1][:, P * t:P * t + P])
                        tr(M[2][:, P * t:P * t + P], tmp[2][:, P * t:P * t + P])
                    tr(M[3][0:NB, 0:P], G[0][:, T:N])
                if values:
                    pe.wait_ge(s("s_rest"), i)
                    mm(M[3][:, 128:256], cm["from_key"][:, :], zsa, start=True, stop=False)
                    for j in range(1, NPAGE):
                        last = mm(M[3][:, 128:256 - 8 * j], ones[:, :], zsa[:, 8 * j:128], start=False, stop=(j == 15))
                    last.then_inc(s("p1"), 1)
                yield
                for k in range(8):
                    if head and k == 0:
                        pe.wait_ge(s("tok_a"), i)
                        pe.wait_ge(s("tok_v"), i)
                        for t in range(NT):
                            mm(M[0][:, P * t:P * t + P], vntok[:, t, :], wst, start=True, stop=False)
                            last = mm(M[0][:, P * t:P * t + P], ones[0:1, :], brow[0:1, 0:P], start=False, stop=True)
                        last.then_inc(s("sg"), 1)
                    if head and k == 1:
                        pe.wait_ge(s("od"), i)
                        for b in range(NT):
                            last = mm(m012[:, SB_OFF[b]:SB_OFF[b] + T - P * b], G[0][:, P * b:P * b + P],
                                      tmp[1][:, P * b:T])
                        last.then_inc(s("z"), 1)
                    if head and k == 3:
                        pe.wait_ge(s("rest"), i)
                        for b in range(NT):
                            off = SB_OFF[b]
                            last = mm(m012[:, off:off + T - P * b], cm["from_key"][:, :], za[:, off:off + T - P * b],
                                      start=True, stop=(b == 3))
                            for l in range(b + 1, NT):
                                last = mm(m012[:, off + P * (l - b):off + T - P * b], ones[:, :],
                                          za[:, SB_OFF[l]:SB_OFF[l] + T - P * l], start=False, stop=(l == 3))
                        last.then_inc(s("between"), 1)
                    if head and k == 4:
                        pe.wait_ge(s("weight"), i)
                        for b in range(NT):
                            last = mm(M[0][:, P * b:T], vtok1[:, b, :], za[:, SB_OFF[b]:SB_OFF[b] + T - P * b],
                                      start=(b == 0), stop=(b == 3))
                        last.then_inc(s("oc"), 1)
                    if values:
                        if k == 0:
                            pe.wait_ge(s("s_weight"), i)
                            pe.wait_ge(s("tok_v"), i)
                        for p in (2 * k, 2 * k + 1):
                            slot, load = value_slot(p, tiles)
                            pe.wait_ge(s(f"page{slot}"), value_loads(i, slot, tiles) * 16 + load * 16)
                            for h in range(2):
                                last = mm(M[3][32 * h:32 * h + NB, :], wv[:, 8 * p:8 * p + 8],
                                          pages[:, slot, 512 * h:512 * h + 512],
                                          start=(p == 0), stop=(p == NPAGE - 1))
                            last.then_inc(s("v_free"), 1)
                    yield

            def l1b(i, mix, tiles=True):
                if tiles:
                    walk("l1b", i, L1B_ORDER, i * 5 + T_L1B, T_L1B % 2, late0=1, mix=mix)
                finish(mix)

            l1b(0, mix_qv(3, True))
            l1b(1, mix1(1, True, True, True, False))
            with pe.Fori(2, HC) as i:
                l1b(i, mix1(i, True, True, True, True))
            l1b(HC, mix1(HC, False, True, True, True), False)
            l1b(HC + 1, mix1(HC + 1, False, False, False, True), False)

            def transposed(j, t):
                pe.wait_ge(s("evac"), j * 2 + (T_OUT1 + t + 1))
                if not (isinstance(j, int) and j == 0):
                    pe.wait_ge(s("yo"), j * 2 + (t - 1))
                    pe.wait_ge(s("ys"), j * 2 + (t - 1))
                y = G[2 + t]
                for q in range(NT):
                    tr(M[t][:, P * q:P * q + P], y[:, P * q:P * q + P])
                tr(M[2 + t][0:NB, 0:P], y[:, T:N]).then_inc(s("y1_t"), 1)

            def turn(j, first):
                yield
                if not first:
                    transposed(j - 1, 1)
                yield
                yield
                transposed(j, 0)
                yield

            walk("out1", 0, OUT_ORDER, T_OUT1, 0, stage=3, mix=turn(0, True))
            walk("out1", 1, OUT_ORDER, T_OUT1 + 2, 0, mix=turn(1, False))
            with pe.Fori(2, 8) as j:
                walk("out1", j, OUT_ORDER, j * 2 + T_OUT1, 0, mix=turn(j, False))
            transposed(7, 1)

        @block.scalar
        def _(act):
            step = Chain(act, "act_step")

            def f(out, x, fn, **kw):
                return act.activation(out, x, fn, **kw)

            def hi(name, i, u):
                _, sl, loaded = unit(name, i, u)
                n = tile_no(name, i, u)
                act.wait_ge(s(f"raw{sl}"), loaded)
                if not (isinstance(n, int) and n < 2):
                    act.wait_ge(s("pe_tile"), n - 1)
                f(w_hi[:, tile_no(name, 0, u) % 2, :], raw[:, sl, :], ACT.Copy).then_inc(s("split_hi"), 1)

            def walk(name, i, order, mix=None, always=False, ahead=2):
                go_on(mix)
                split = split_ahead(order, ahead)
                for u in range(2 * len(order)):
                    if u in split:
                        hi(name, i, split[u])
                    if goes_on(name, order, u, always):
                        go_on(mix)

            def sigmoid(x):
                step(f(x, x, ACT.Exp, scale=-1.0))
                step(f(x, x, ACT.Ln, bias=1.0))
                return f(x, x, ACT.Exp, scale=-1.0)

            def rstd(dst, big, small_, width):
                f(dst[:, 0:T], big, ACT.Ln, scale=1.0 / width, bias=eps[:, 0:1])
                step(f(dst[:, T:N], small_, ACT.Ln, scale=1.0 / width, bias=eps[:, 0:1]))
                return f(dst, dst, ACT.Exp, scale=-0.5)

            def norm_rstd(k):
                act.wait_ge(s("x_ss"), k + 1)
                rstd(tmp[4], M[0], M[1][:, 0:8], D).then_inc(s("x_rs"), 1)

            def norm(k):
                act.wait_ge(s("ns"), k + 1)
                f(act_hi[:, :, T:N], hs, ACT.Copy).then_inc(s("ns_hi"), 1)
                for c in range(KC):
                    act.wait_ge(s("n_t"), 16 * k + c + 1)
                    f(act_hi[:, c, 0:T], tmp[c % 4][:, 0:T], ACT.Identity, bias=mod[k][:, c, 0:1])\
                        .then_inc(s("act_hi"), 1)

            def take_mixed():
                for c in range(KC):
                    f(act_hi[:, c, :], wide[:, c, :], ACT.Copy).then_inc(s("act_hi"), 1)

            for dst, src in ((crow[0:1, :], a["c_prompt"]), (crow[1:9, :], a["c_sample"]),
                             (cm["ident"][:, :], cst["ident"])):
                act.dma_start(dst, src).then_inc(s("first_in"), 16)
            for t in range(NT):
                act.dma_start(xin[:, t, :], a["x_prompt"][0, P * t:P * t + P, :]).then_inc(s("x_in"), 16)
            act.dma_start(xin[0:NB, 4, :], a["x_sample"].rearrange("b o d -> (b o) d")).then_inc(s("x_in"), 16)
            act.preload_act_table_set("natural_log_exp_and_others")
            act.wait_ge(s("cond_cols"), 1)
            sigmoid(csm2).then_inc(s("cond_sig"), 1)
            for c in range(KC):
                act.wait_ge(s("xt"), c + 1)
                f(wide[:, c, 0:T], M[c % 2], ACT.Copy).then_inc(s("xt_a"), 1)
            act.wait_ge(s("xt_a"), KC)
            act.wait_ge(s("xt_s"), KC)
            for c in range(KC):
                if c >= 2:
                    act.wait_ge(s("x_acc"), c - 1)
                f(tmp[2 + c % 2], wide[:, c, :], ACT.Square).then_inc(s("x_sqc"), 1)
            step.straight()
            norm_rstd(0)
            norm(0)
            hi("ra", 0, 0)
            hi("ra", 0, 1)
            walk("ra", 0, [TILE])
            act.wait_ge(s("la_abs"), 1)
            step(f(vla, vla, ACT.Exp, scale=-1.0))
            f(vla, vla, ACT.Ln, bias=1.0)
            step(f(sda, sda, ACT.Exp, scale=-1.0))
            f(sda, sda, ACT.Ln, bias=1.0).then_inc(s("la_l"), 1)
            act.wait_ge(s("sd"), 1)
            f(sdec, sdec, ACT.Exp, scale=1.0 / 16.0).then_inc(s("sdec"), 1)
            act.wait_ge(s("sdec"), 1)
            act.wait_ge(s("la"), 1)
            step.straight()

            def mix0(i, gla):
                if gla:
                    f(lah, la[:, :, bass.ds(i * P, P)], ACT.Copy).then_inc(s("lah"), 1)
                yield
                if gla:
                    act.wait_ge(s("cum"), i + 1)
                    f(up, M[0], ACT.Exp)
                    f(down, M[0], ACT.Exp, scale=-1.0)
                    f(small[:, 0:24], M[1][:, 0:24], ACT.Exp)
                    f(small[:, 24:32], sdec[:, bass.ds(i * NB, NB)], ACT.Copy).then_inc(s("decay"), 1)
                act.wait_ge(s("g_clamp"), i + 1)
                sigmoid(pair_c).then_inc(s("g_sig"), 1)
                yield
                act.wait_ge(s("v_t"), i + 1)
                f(vtok[:, 0:2, :], M[1].rearrange("p (t d) -> p t d", t=2), ACT.Copy)
                f(vtok[:, 2:4, :], M[2].rearrange("p (t d) -> p t d", t=2), ACT.Copy).then_inc(s("vtok"), 1)
                yield
                act.wait_ge(s("sc"), i + 1)
                f(ktok, M[0].rearrange("p (t d) -> p t d", t=NT), ACT.Copy).then_inc(s("ktok"), 1)
                yield
                yield
                yield
                for d in range(2):
                    act.wait_ge(s("o"), i * 2 + (d + 1))
                    f(tmp[d][:, 0:T], M[2], ACT.Copy).then_inc(s("o_a"), 1)
                    yield
                yield
                act.wait_ge(s("o_a"), i * 2 + 2)
                act.wait_ge(s("o_s"), i + 1)
                f(pair_b, pair_a, ACT.Square).then_inc(s("o_sq"), 1)
                yield
                act.wait_ge(s("oss"), i + 1)
                rstd(tmp[3], M[0], M[1][:, 0:8], 256.0).then_inc(s("o_rs"), 1)
                yield

            def l0(i, mix=None, ahead=2):
                walk("l0", i, L0_ORDER, mix, ahead=ahead)
                if mix is not None:
                    finish(mix)

            l0(0)
            with act.Fori(1, HEADS) as i:
                step.body(i, 1, 3)
                l0(i, mix0(i - 1, True))
            step.end(HEADS - 1, 3)
            l0(HEADS, mix0(HEADS - 1, True))
            step.straight()
            with act.Fori(HEADS + 1, 2 * HEADS - 1) as i:
                step.body(i, HEADS + 1, 3)
                l0(i, mix0(i - 1, False))
            step.end(HEADS - 2, 3)
            l0(2 * HEADS - 1, mix0(2 * HEADS - 2, False), ahead=0)
            mix = mix0(2 * HEADS - 1, False)
            finish(mix)
            act.wait_ge(s("mixed"), 16)
            take_mixed()
            hi("out0", 0, 0)
            hi("out0", 0, 1)

            def y_squares(j):
                yield
                yield
                for t in range(2):
                    act.wait_ge(s("evac"), j * 2 + (T_OUT0 + t + 1))
                    if isinstance(j, int) and j == 0:
                        pass
                    else:
                        act.wait_ge(s("y_acc"), j * 2 + t - 1)
                    f(tmp[2 + t], wide[:, bass.ds(j * 2 + t, 1), :].rearrange("p c n -> p (c n)"), ACT.Square)\
                        .then_inc(s("y_sq"), 1)
                    yield
                    yield

            def out0(j):
                mix = y_squares(j)
                walk("out0", j, OUT_ORDER, mix)
                finish(mix)

            out0(0)
            with act.Fori(1, 8) as j:
                out0(j)
            norm_rstd(1)
            norm(1)
            step.straight()

            def mix_qv(j, last_one=False):
                act.wait_ge(s("evac"), j * 4 + (T_L1A + 4))
                f(pair_a, g01, ACT.Square).then_inc(s("q_sq"), 1)
                f(pair_b, g23, ACT.Square).then_inc(s("vd_x2"), 1)
                yield
                act.wait_ge(s("q_ss"), j + 1)
                for t in range(2):
                    f(tmp[t][:, 0:T], M[t], ACT.Ln, scale=1.0 / DH, bias=eps[:, 0:1])
                    last = f(tmp[t][:, T:N], M[2][:, 8 * t:8 * t + 8], ACT.Ln, scale=1.0 / DH, bias=eps[:, 0:1])
                step(last)
                f(pair_a, pair_a, ACT.Exp, scale=-0.5).then_inc(s("q_rs"), 1)
                yield
                act.wait_ge(s("vd_u"), j + 1)
                sigmoid(pair_b).then_inc(s("vd_sig"), 1)
                yield
                act.wait_ge(s("vd_g"), j + 1)
                f(pair_b, g23, ACT.Square).then_inc(s("vd_g2"), 1)
                if last_one:
                    take_queries(0)
                    yield
                    yield
                    act.wait_ge(s("vd_ss"), 1)
                    rstd(G[5], M[0], M[1][:, 0:8], BR).then_inc(s("rv"), 1)
                yield

            def take_queries(b):
                act.wait_ge(s("qb_t"), b + 1)
                f(qb, m012[:, 512:1536], ACT.Copy).then_inc(s("qb"), 1)

            def l1a(j, mix=None):
                walk("l1a", j, L1A_ORDER, mix)
                if mix is not None:
                    finish(mix)

            l1a(0)
            with act.Fori(1, 4) as j:
                step.body(j, 1, 3)
                l1a(j, mix_qv(j - 1))
            step.end(3, 3)

            def mix1(i, tiles, head, values, out):
                if head:
                    act.wait_ge(s("evac"), i * 5 + T_L1B)
                    f(tmp[0], G[0], ACT.Square).then_inc(s("k_sq"), 1)
                yield
                if head:
                    act.wait_ge(s("p0"), i)
                    rstd(tmp[0], M[0], M[3][:, 0:8], DH).then_inc(s("k_rs"), 1)
                if tiles and head:
                    take_queries(i)
                if values:
                    act.wait_ge(s("zs_abs"), i)
                    step(f(zsa, zsa, ACT.Exp, scale=-1.0))
                    f(zsa, zsa, ACT.Ln, bias=1.0).then_inc(s("zs_l"), 1)
                if head:
                    act.wait_ge(s("g1_clamp"), i)
                    sigmoid(pair_c).then_inc(s("g1_sig"), 1)
                yield
                if head:
                    act.wait_ge(s("p1"), i)
                    act.wait_ge(s("kv_out"), (i - 1) * 64)
                    f(ktok1, M[0].rearrange("p (t d) -> p t d", t=NT), ACT.Copy)
                    f(vtok1, M[1].rearrange("p (t d) -> p t d", t=NT), ACT.Copy).then_inc(s("tok_a"), 1)
                    act.wait_ge(s("s_lw"), i)
                    f(wv, zs, ACT.Exp).then_inc(s("s_weight"), 1)
                    act.wait_ge(s("kn"), i)
                    f(tmp[0], G[4], ACT.Square).then_inc(s("u_x2"), 1)
                yield
                if head:
                    act.wait_ge(s("tok_a"), i)
                    act.wait_ge(s("tok_v"), i)
                    for n, (src, big, small_) in enumerate(((ktok1, a["k_prompt_out"], a["k_sample_out"]),
                                                           (vtok1, a["v_prompt_out"], a["v_sample_out"]))):
                        act.dma_start(big[0, 0].rearrange("(t p) h d -> p t h d", p=P)[:, :, bass.ds(i - 1, 1), :]
                                      .rearrange("p t h d -> p t (h d)"), src).then_inc(s("kv_out"), 16)
                        act.dma_start(small_[0, :, 0, bass.ds(i - 1, 1), :].rearrange("b h d -> b (h d)"),
                                      srow[0:NB, P * n:P * n + P]).then_inc(s("kv_out"), 16)
                    act.dma_start(a["chunk_v_out"][0, :, 0, bass.ds((i - 1) * P, P)],
                                  srow[0:NB, 2 * P:3 * P]).then_inc(s("cv_out"), 16)
                    act.wait_ge(s("u_u"), i)
                    sigmoid(tmp[0]).then_inc(s("u_sig"), 1)
                yield
                if head:
                    act.wait_ge(s("z_abs"), i)
                    step(f(za, za, ACT.Exp, scale=-1.0))
                    f(za, za, ACT.Ln, bias=1.0).then_inc(s("z_l"), 1)
                yield
                yield
                if head:
                    act.wait_ge(s("lw"), i)
                    f(za, z, ACT.Exp).then_inc(s("w_e"), 1)
                yield

            def l1b(i, mix, tiles=True):
                if tiles:
                    walk("l1b", i, L1B_ORDER, mix)
                finish(mix)

            l1b(0, mix_qv(3, True))
            step.straight()
            l1b(1, mix1(1, True, True, True, False))
            step.straight()
            with act.Fori(2, HC) as i:
                step.body(i, 2, 7)
                l1b(i, mix1(i, True, True, True, True))
            step.end(HC - 2, 7)
            l1b(HC, mix1(HC, False, True, True, True), False)
            act.wait_ge(s("mixed1_all"), 1)
            take_mixed()
            act.wait_ge(s("kv_out"), 64 * HC)

            def rows_out(j, first):
                def rows(j, t):
                    act.wait_ge(s("y1_t"), j * 2 + (t + 1))
                    if not (isinstance(j, int) and j == 0):
                        act.wait_ge(s(f"y_out{t}"), j * 16)
                    f(yo[t], M[t], ACT.Copy).then_inc(s("yo"), 1)

                yield
                if not first:
                    rows(j - 1, 1)
                yield
                yield
                rows(j, 0)
                yield

            walk("out1", 0, OUT_ORDER, rows_out(0, True))
            walk("out1", 1, OUT_ORDER, rows_out(1, False))
            with act.Fori(2, 7) as j:
                walk("out1", j, OUT_ORDER, rows_out(j, False))
            walk("out1", 7, OUT_ORDER, rows_out(7, False), ahead=0)
            act.wait_ge(s("y1_t"), 16)
            act.wait_ge(s("y_out1"), 7 * 16)
            f(yo[1], M[1], ACT.Copy).then_inc(s("yo"), 1)


        @block.vector
        def _(dve):
            step = Chain(dve, "dve_step")
            tt, ts_, stt, copy = dve.tensor_tensor, dve.tensor_scalar, dve.scalar_tensor_tensor, dve.tensor_copy

            def lo(name, i, u):
                sl = unit(name, i, u)[1]
                n = tile_no(name, i, u)
                dve.wait_ge(s("split_hi"), n + 1)
                if not (isinstance(n, int) and n < 2):
                    dve.wait_ge(s("pe_tile"), n - 1)
                b = tile_no(name, 0, u) % 2
                tt(w_lo[:, b, :], raw[:, sl, :], w_hi[:, b, :].bitcast(F32), ALU.subtract)\
                    .then_inc(s("split_lo"), 1)

            def halves(x):
                return x.rearrange("p (a n) -> p a n", a=2)

            def mod_rows(name, i, u, bank):
                dve.wait_ge(s("pe_mod"), mod_no(name, i, u) + 1)
                copy(mrow[0:9, :], bank[0:9, :]).then_inc(s("mod_row"), 1)

            def mod_add(group, layer, col, bank):
                dve.wait_ge(s("mod_col"), group + 1)
                tt(mod[layer][:, bass.ds(col, 4), :], bank[:, 0:36].rearrange("p (j n) -> p j n", j=4),
                   cols[:, bass.ds(col + C_BADA[layer], 4)].unsqueeze(2).to_broadcast([P, 4, 9]),
                   ALU.add).then_inc(s("mod_read"), 1)

            def walk(name, i, order, evac=None, par0=0, group=None, layer=None, col=None, mix=None,
                     always=False, ahead=2, late=None):
                late = late or {}
                go_on(mix)
                t = m = 0
                fold = False

                def read_out(k, u):
                    dve.wait_ge(s("pe_tile"), tile_no(name, i, u) + 1)
                    evac(k, pt[(par0 + k) % 2][:, :, 0:HALF]).then_inc(s("evac"), 1)

                split = split_ahead(order, ahead)
                for u in range(2 * len(order)):
                    for k, (at, last) in late.items():
                        if u == at:
                            read_out(k, last)
                    if u in split and name != "l1b":
                        lo(name, i, split[u])
                    if order[u // 2] is TILE and u % 2 == 1:
                        if t not in late:
                            read_out(t, u)
                        t += 1
                    if u in split and name == "l1b":
                        lo(name, i, split[u])
                    if fold:
                        mod_add(group, layer, col, M[3])
                        fold = False
                    if order[u // 2] is MOD:
                        m += 1
                        if m == 8:
                            mod_rows(name, i, u, M[3])
                            fold = True
                    if goes_on(name, order, u, always):
                        go_on(mix)
                if fold:
                    mod_add(group, layer, col, M[3])

            def mod_scale(k):
                g = cols[:, C_NORM[k]:C_NORM[k] + 16].unsqueeze(2).to_broadcast([P, 16, 9])
                stt(mod[k][:, 16:32, :], mod[k][:, 16:32, :], 1.0, g, ALU.add, ALU.mult)\
                    .then_inc(s("mod_scale"), 1)
                dve.wait_ge(s("mod_scale"), k + 1)

            def norm(k):
                dve.wait_ge(s("mod_read"), 8 + 16 * k)
                mod_scale(k)
                dve.wait_ge(s("x_rs"), k + 1)
                step(tt(hs, wide[:, :, T:N], tmp[4][:, T:N].unsqueeze(1).to_broadcast([P, KC, NB]), ALU.mult))
                step(tt(hs, hs, mod[k][:, 16:32, 1:9], ALU.mult))
                tt(hs, hs, mod[k][:, 0:16, 1:9], ALU.add).then_inc(s("ns"), 1)

                def scaled(c):
                    if c >= 4:
                        dve.wait_ge(s("act_ready"), 32 * k + c - 3)
                    stt(tmp[c % 4][:, 0:T], wide[:, c, 0:T], mod[k][:, 16 + c, 0:1], tmp[4][:, 0:T],
                        ALU.mult, ALU.mult).then_inc(s("n_t"), 1)

                scaled(0)
                dve.wait_ge(s("ns"), k + 1)
                dve.wait_ge(s("ns_hi"), k + 1)
                tt(act_lo[:, :, T:N], hs, act_hi[:, :, T:N].bitcast(F32), ALU.subtract)
                for c in range(KC):
                    if c + 1 < KC:
                        scaled(c + 1)
                    dve.wait_ge(s("n_t"), 16 * k + c + 1)
                    dve.wait_ge(s("act_hi"), 32 * k + c + 1)
                    stt(act_lo[:, c, 0:T], tmp[c % 4][:, 0:T], mod[k][:, c, 0:1],
                        act_hi[:, c, 0:T].bitcast(F32), ALU.add, ALU.subtract).then_inc(s("act_ready"), 1)
                    if c % 4 == 3:
                        yield

            def take_mixed(stage):
                for c in range(KC):
                    dve.wait_ge(s("act_hi"), 16 * stage + c + 1)
                    tt(act_lo[:, c, :], wide[:, c, :], act_hi[:, c, :].bitcast(F32), ALU.subtract)\
                        .then_inc(s("act_ready"), 1)

            dve.memset(eps[:, :], EPS)
            dve.memset(ones[:, :], 1.0).then_inc(s("ones"), 1)
            dve.wait_ge(s("ones"), 1)
            dve.wait_ge(s("cols_t"), 1)
            copy(cols[:, :], M[0][:, 0:154]).then_inc(s("cols"), 1)
            dve.wait_ge(s("cond_t"), 1)
            step(copy(csm, M[1][:, 0:144]))
            ts_(csm2, csm, -40.0, None, ALU.max).then_inc(s("cond_cols"), 1)
            dve.wait_ge(s("cond_sig"), 1)
            tt(cond[:, :, :], csm.rearrange("p (c n) -> p c n", n=9), csm2.rearrange("p (c n) -> p c n", n=9),
               ALU.mult).then_inc(s("cond"), 1)
            for c in range(KC):
                dve.wait_ge(s("xt"), c + 1)
                copy(wide[:, c, T:N], M[2 + c % 2][:, 0:8]).then_inc(s("xt_s"), 1)
            for c in range(KC):
                dve.wait_ge(s("x_sqc"), c + 1)
                if c == 0:
                    copy(tmp[4], tmp[2]).then_inc(s("x_acc"), 1)
                else:
                    dve.wait_ge(s("x_acc"), c)
                    tt(tmp[4], tmp[4], tmp[2 + c % 2], ALU.add).then_inc(s("x_acc" if c < KC - 1 else "x_sq"), 1)
            step.straight()

            def ada0(g, odd):
                mod_rows("ada0", g, 7, M[2 + odd])
                mod_add(g, 0, g * 4, M[2 + odd])

            with dve.Fori(0, 4) as g:
                ada0(g * 2, 0)
                ada0(g * 2 + 1, 1)
            mix = norm(0)
            for g in range(8, 12):
                go_on(mix)
                ada0(g, g % 2)
            finish(mix)
            lo("ra", 0, 0)
            lo("ra", 0, 1)
            step(dve.memset(ra_rows, 1.0))
            walk("ra", 0, [TILE], lambda k, x: copy(halves(G[0][0:RANK, :]), x[0:RANK]))
            dve.wait_ge(s("evac"), 1)
            dve.engine_nop().then_inc(s("ra"), 1)
            dve.wait_ge(s("la_x"), 1)
            for t in range(NT):
                copy(la[:, t, :], M[t])
            copy(sdec, pt[1][:, 0, 0:32]).then_inc(s("la_copied"), 1)
            dve.wait_ge(s("la_copied"), 1)
            laf = la.rearrange("p t k -> p (t k)")
            stt(vla, laf, -1.0, laf, ALU.mult, ALU.max)
            stt(sda, sdec, -1.0, sdec, ALU.mult, ALU.max).then_inc(s("la_abs"), 1)
            dve.wait_ge(s("la_l"), 1)
            stt(laf, laf, 0.0, vla, ALU.min, ALU.subtract).then_inc(s("la"), 1)
            stt(sdec, sdec, 0.0, sda, ALU.min, ALU.subtract).then_inc(s("sd"), 1)
            dve.wait_ge(s("sd"), 1)
            step.straight()

            def evac0(i, mixing):
                def evac(k, x):
                    to = L0_TO[k]
                    if mixing:
                        if to < 2:
                            dve.wait_ge(s("v_t"), i)
                        elif to == 3:
                            dve.wait_ge(s("sc"), i)
                        elif to == 2:
                            dve.wait_ge(s("os"), i)
                        else:
                            dve.wait_ge(s("mixed"), i * 2)
                    d = halves(G[to])
                    return ts_(d, x, SCALE, None, ALU.mult) if to == 2 else copy(d, x)
                return evac

            def mix0(i, gla):
                dve.wait_ge(s("evac"), i * 6 + (T_L0 + 6))
                if not (isinstance(i, int) and i == 0):
                    dve.wait_ge(s("mixed"), i * 2)
                ts_(pair_c, g45, -40.0, None, ALU.max).then_inc(s("g_clamp"), 1)
                yield
                if gla:
                    dve.wait_ge(s("decay"), i + 1)
                else:
                    dve.wait_ge(s("ret_in"), i * 16 + (16 - 16 * HEADS))
                    dve.wait_ge(s("rope_in"), 16)
                    dve.wait_ge(s("swapped"), i + (1 - HEADS))
                    for k in range(2):
                        tt(tmp[k][:, 0:T], M[k], rope[:, 1, 0:T], ALU.mult)
                        tt(tmp[k][:, T:N], M[2][:, 8 * k:8 * k + 8], rope[:, 1, T:N], ALU.mult)
                        step(tt(G[2 + k], G[2 + k], rope[:, 0, :], ALU.mult))
                    tt(g23, g23, pair_a, ALU.add).then_inc(s("rotated"), 1)
                    dve.wait_ge(s("rotated"), i + (1 - HEADS))
                tt(G[2][:, 0:T], G[2][:, 0:T], up, ALU.mult)
                tt(G[3][:, 0:T], G[3][:, 0:T], down, ALU.mult).then_inc(s("qk"), 1)
                yield
                dve.wait_ge(s("g_sig"), i + 1)
                step(tt(g45, g45, pair_c, ALU.mult))
                dve.wait_ge(s("v_t"), i + 1)
                copy(srow0, M[0][0:NB, 0:384]).then_inc(s("srow0"), 1)
                dve.wait_ge(s("srow0"), i + 1)
                tt(kmask, srow0[:, 0:P].unsqueeze(1).to_broadcast([NB, NB, P]),
                   ident[0:NB, 0:NB].unsqueeze(2).to_broadcast([NB, NB, P]), ALU.mult).then_inc(s("kmask"), 1)
                yield
                dve.wait_ge(s("sc"), i + 1)
                stt(sct, M[2].rearrange("p (t k) -> p t k", t=NT), BIG,
                    cm["chunk_mask"][:, :].unsqueeze(1).to_broadcast([P, NT, P]), ALU.min, ALU.mult)\
                    .then_inc(s("sct"), 1)
                yield
                for n in range(NCH):
                    at = 6 * (n // 2) + n % 2
                    if n % 4 == 0:
                        if n:
                            yield
                        dve.wait_ge(s("kv"), i * 2 + (n // 4 + 1))
                    kv = M[n % 2][:, 128 * (n % 4 - n % 2):128 * (n % 4 - n % 2) + 256]
                    if n == 0:
                        ts_(S[:, 0, :], kv, small[:, at + 4:at + 5], None, ALU.mult).then_inc(s("s_step"), 1)
                    else:
                        step(ts_(tmp[4][:, 0:256], kv, small[:, at + 4:at + 5], None, ALU.mult))
                        if n >= 2:
                            dve.wait_ge(s("carry"), i * 7 + (n - 1))
                        elif n == 1 and not (isinstance(i, int) and i == 0):
                            dve.wait_ge(s("s_out"), i * 16)
                        stt(S[:, n % 2, :], S[:, (n - 1) % 2, :], small[:, at + 2:at + 3], tmp[4][:, 0:256],
                            ALU.mult, ALU.add).then_inc(s("s_step"), 1)
                        dve.wait_ge(s("s_step"), i * 8 + (n + 1))
                yield
                dve.wait_ge(s("st_in"), i * 16 + 16)
                for d in range(2):
                    dve.wait_ge(s("outer"), i * 2 + (d + 1))
                    for b in range(4 * d, 4 * d + 4):
                        stt(st[:, b, :], st[:, b, :], small[:, 24 + b:25 + b],
                            M[(b // 2) % 2][:, 256 * (b % 2):256 * (b % 2) + 256], ALU.mult, ALU.add)\
                            .then_inc(s("st_step"), 1)
                    yield
                yield
                dve.wait_ge(s("os"), i + 1)
                copy(pair_a.rearrange("p (d n) -> p d n", d=2)[:, :, T:N],
                     M[0][:, 0:16].rearrange("p (d n) -> p d n", d=2)).then_inc(s("o_s"), 1)
                dve.wait_ge(s("o_sq"), i + 1)
                tt(tmp[2], tmp[2], tmp[3], ALU.add).then_inc(s("osq"), 1)
                yield
                dve.wait_ge(s("o_rs"), i + 1)
                for d in range(2):
                    step(stt(tmp[d], tmp[d], cols[:, bass.ds(i * 2 + (C_MIX + d), 1)], tmp[3], ALU.mult, ALU.mult))
                    tt(wide[:, bass.ds(i * 2 + d, 1), :].rearrange("p c n -> p (c n)"), tmp[d], G[4 + d],
                       ALU.mult).then_inc(s("mixed"), 1)
                yield

            def l0(i, mix=None, ahead=2):
                walk("l0", i, L0_ORDER, evac0(i, mix is not None), 1, group=i + 12, layer=1, col=i * 4, mix=mix,
                     ahead=ahead)
                if mix is not None:
                    finish(mix)

            l0(0)
            l0(1, mix0(0, True))
            step.straight()
            with dve.Fori(2, HEADS) as i:
                step.body(i, 2, 10)
                l0(i, mix0(i - 1, True))
            step.end(HEADS - 2, 10)
            l0(HEADS, mix0(HEADS - 1, True))
            step.straight()
            with dve.Fori(HEADS + 1, 2 * HEADS - 1) as i:
                step.body(i, HEADS + 1, 12)
                l0(i, mix0(i - 1, False))
            step.end(HEADS - 2, 12)
            l0(2 * HEADS - 1, mix0(2 * HEADS - 2, False), ahead=0)
            mix = mix0(2 * HEADS - 1, False)
            for g in range(2):
                walk("gate1", g, MOD_ORDER, group=g + 20, layer=1, col=4 * g + 32, mix=mix, always=True)
            finish(mix)
            take_mixed(1)
            with dve.Fori(2, 4) as g:
                walk("gate1", g, MOD_ORDER, group=g + 20, layer=1, col=g * 4 + 32)
            lo("out0", 0, 0)
            lo("out0", 0, 1)
            step.straight()

            def residual(l, x, j, t, y):
                yt = tmp[t]
                step(copy(halves(yt), x))
                dve.wait_ge(s(f"xj{t}"), j * 16 + (16 + l * 128))
                gate = mod[l][:, bass.ds(j * 2 + (32 + t), 1), :].rearrange("p c n -> p (c n)")
                stt(y[:, 0:T], yt[:, 0:T], gate[:, 0:1], G[t][:, 0:T], ALU.mult, ALU.add)
                step(tt(yt[:, T:N], yt[:, T:N], gate[:, 1:9], ALU.mult))
                return tt(y[:, T:N], yt[:, T:N], G[t][:, T:N], ALU.add)

            def add_squares(j, t, first=False, last=False):
                dve.wait_ge(s("y_sq"), j * 2 + (t + 1))
                if first:
                    copy(tmp[4], tmp[2 + t]).then_inc(s("y_acc"), 1)
                else:
                    dve.wait_ge(s("y_acc"), j * 2 + t)
                    tt(tmp[4], tmp[4], tmp[2 + t], ALU.add).then_inc(s("x_sq" if last else "y_acc"), 1)

            def sums(j, first):
                yield
                if not first:
                    add_squares(j - 1, 1)
                yield
                yield
                add_squares(j, 0, first)
                yield

            def out0(j, first=False):
                def evac(k, x):
                    dve.wait_ge(s("evac"), j * 2 + (T_OUT0 + k))
                    return residual(0, x, j, k, wide[:, bass.ds(j * 2 + k, 1), :].rearrange("p c n -> p (c n)"))

                mix = sums(j, first)
                walk("out0", j, OUT_ORDER, evac, T_OUT0 % 2, mix=mix)
                finish(mix)

            dve.wait_ge(s("act_ready"), 32)
            out0(0, True)
            step.straight()
            with dve.Fori(1, 8) as j:
                step.body(j, 1, 4)
                out0(j)
            step.end(7, 4)
            add_squares(7, 1, last=True)
            finish(norm(1))
            dve.wait_ge(s("act_ready"), 48)
            dve.wait_ge(s("x1_out"), 16)
            step(dve.memset(tmp[4], 0.0))
            step.straight()

            def gelu_arg(y, x):
                step(ts_(y, y, 0.044715, 1.0, ALU.mult, ALU.add))
                step(stt(y, y, GELU, x, ALU.mult, ALU.mult))
                return ts_(y, y, -40.0, None, ALU.max)

            def spread(b):
                tt(dg.rearrange("p (h d) -> p h d", h=HC), ident[:, :].unsqueeze(1).to_broadcast([P, HC, P]),
                   wide[:, 0:HC, bass.ds(b + T, 1)].to_broadcast([P, HC, P]), ALU.mult).then_inc(s("dg"), 1)

            def key_pages(i, k):
                if k == 0:
                    dve.wait_ge(s("qb"), i + 1)
                for p in range(2):
                    dve.wait_ge(s(f"page{p}"), i * 128 + 16 * (k + 1))
                    for h in range(HC):
                        kpage = pages[:, p, P * h:P * h + P]
                        at = 8 * (2 * k + p) + h
                        last = dve.tensor_tensor_reduce(kpage, kpage, qb[:, P * h:P * h + P], 1.0, 0.0,
                                                        ALU.mult, ALU.add, zs[:, at:at + 1])
                    last.then_inc(s("k_free"), 1)

            def mix_qv(j, last_one=False):
                yield
                dve.wait_ge(s("vd_x2"), j + 1)
                gelu_arg(pair_b, g23).then_inc(s("vd_u"), 1)
                dve.wait_ge(s("q_rs"), j + 1)
                for t in range(2):
                    last = stt(wide[:, bass.ds(j * 2 + t, 1), :].rearrange("p c n -> p (c n)"), G[t],
                               cols[:, C_QN:C_QN + 1], tmp[t], ALU.mult, ALU.mult)
                step(last)
                yield
                if last_one:
                    spread(0)
                dve.wait_ge(s("vd_sig"), j + 1)
                tt(g23, g23, pair_b, ALU.mult).then_inc(s("vd_g"), 1)
                dve.wait_ge(s("vd_g"), j + 1)
                step(copy(wide[:, bass.ds(j * 2 + 8, 2), :].rearrange("p c n -> p (c n)"), g23))
                yield
                dve.wait_ge(s("vd_g2"), j + 1)
                step(tt(tmp[4], tmp[4], tmp[2], ALU.add))
                tt(tmp[4], tmp[4], tmp[3], ALU.add).then_inc(s("vd_sq"), 1)
                dve.wait_ge(s("vd_sq"), j + 1)
                if last_one:
                    for k in range(8):
                        key_pages(0, k)
                        yield
                yield

            def l1a(j, mix=None):
                walk("l1a", j, L1A_ORDER, lambda k, x: copy(halves(G[L1A_TO[k]]), x), T_L1A % 2, mix=mix)
                if mix is not None:
                    finish(mix)

            l1a(0)
            with dve.Fori(1, 4) as j:
                step.body(j, 1, 5)
                l1a(j, mix_qv(j - 1))
            step.end(3, 5)

            def masks(x):
                for off in (0, 512, 896, 1024):
                    last = tt(x[:, off:off + P], x[:, off:off + P], cm["below"][:, :], ALU.mult)
                return last

            def mix1(i, tiles, head, values, out):
                hd = i - 1
                if head:
                    dve.wait_ge(s("evac"), i * 5 + T_L1B)
                    dve.wait_ge(s("rv"), 1)
                    if not (isinstance(i, int) and i == 1):
                        dve.wait_ge(s("od"), i - 1)
                    copy(tmp[1], wide[:, bass.ds(hd, 1), :].rearrange("p c n -> p (c n)"))
                    stt(tmp[2], wide[:, bass.ds(hd + 8, 1), :].rearrange("p c n -> p (c n)"),
                        cols[:, bass.ds(hd + C_VN, 1)], G[5], ALU.mult, ALU.mult)
                    ts_(tmp[3], G[2], -40.0, None, ALU.max)
                    ts_(tmp[4], G[3], -40.0, None, ALU.max).then_inc(s("g1_clamp"), 1)
                    if tiles:
                        spread(i)
                yield
                if values:
                    dve.wait_ge(s("k_free"), i * 16)
                    zv = zs.rearrange("p (g h) -> p g h", h=HC)
                    step(stt(zv, zv, SCALE, per_head[:, 0:1, :].to_broadcast([P, NPAGE, HC]), ALU.mult, ALU.add))
                    stt(zsa, zs, -1.0, zs, ALU.mult, ALU.max).then_inc(s("zs_abs"), 1)
                dve.wait_ge(s("p0"), i)
                if head:
                    dve.wait_ge(s("k_rs"), i)
                if out:
                    copy(OS[:, :, bass.ds(i - 2, 1)].rearrange("p h b -> p (h b)"), M[3][:, 16:16 + HC])\
                        .then_inc(s("mixed1"), 1)
                if head:
                    dve.wait_ge(s("kv_out"), hd * 64)
                    dve.wait_ge(s("cv_out"), hd * 16)
                    copy(srow[0:NB, P:3 * P], M[3][0:NB, P:3 * P])
                    tt(wst, M[3][:, 3 * P:4 * P], cm["upto_t"][:, :], ALU.mult)
                    stt(G[0], G[0], cols[:, C_KN:C_KN + 1], tmp[0], ALU.mult, ALU.mult).then_inc(s("kn"), 1)
                if values:
                    dve.wait_ge(s("zs_l"), i)
                    stt(zsa, zs, 0.0, zsa, ALU.max, ALU.add).then_inc(s("s_rest"), 1)
                yield
                if head:
                    dve.wait_ge(s("p1"), i)
                    tt(zs, zs, M[3][:, 128:256], ALU.subtract).then_inc(s("s_lw"), 1)
                    copy(srow[0:NB, 0:P], M[3][0:NB, 0:P])
                    copy(vntok, M[2].rearrange("p (t d) -> p t d", t=NT)).then_inc(s("tok_v"), 1)
                    ts_(tmp[2][:, T:N], tmp[2][:, T:N], per_head[:, 1, bass.ds(hd, 1)],
                        per_head[:, 2, bass.ds(hd, 1)], ALU.mult, ALU.add)
                    dve.wait_ge(s("u_x2"), i)
                    gelu_arg(tmp[0], G[4]).then_inc(s("u_u"), 1)
                    dve.wait_ge(s("g1_sig"), i)
                    tt(G[2], G[2], tmp[3], ALU.mult)
                    step(tt(G[3], G[3], tmp[4], ALU.mult))
                yield
                for k in range(8):
                    if head and k == 0:
                        dve.wait_ge(s("u_sig"), i)
                        step(tt(G[4], G[4], tmp[0], ALU.mult))
                        step(tt(G[4], G[4], G[3], ALU.mult))
                        dve.wait_ge(s("sg"), i)
                        to = wide[:, bass.ds(hd + 8, 1), :].rearrange("p c n -> p (c n)")
                        copy(GS[:, bass.ds(hd, 1), :].rearrange("p c n -> p (c n)"), G[2][:, T:N])
                        tt(to[:, T:N], G[4][:, T:N], tmp[2][:, T:N], ALU.mult)
                        tt(to[:, 0:T], G[4][:, 0:T], M[0], ALU.mult).then_inc(s("od"), 1)
                        dve.wait_ge(s("od"), i)
                    if head and k == 1:
                        dve.wait_ge(s("z"), i)
                        step(ts_(z, m012[:, 0:SB_ALL], SCALE, per_head[:, 0, bass.ds(hd, 1)], ALU.mult, ALU.add))
                        step(masks(z))
                        stt(za, z, -1.0, z, ALU.mult, ALU.max).then_inc(s("z_abs"), 1)
                        if tiles:
                            key_pages(i, k)
                        dve.wait_ge(s("z_l"), i)
                        step(stt(za, z, 0.0, za, ALU.max, ALU.add))
                        masks(za).then_inc(s("rest"), 1)
                    if head and k == 3:
                        dve.wait_ge(s("between"), i)
                        tt(z, z, m012[:, 0:SB_ALL], ALU.subtract).then_inc(s("lw"), 1)
                    if head and k == 3:
                        dve.wait_ge(s("w_e"), i)
                        masks(za).then_inc(s("weight"), 1)
                    if tiles and k != 1:
                        if k == 0 and values:
                            dve.wait_ge(s("s_weight"), i)
                        key_pages(i, k)
                    if head and k == 4:
                        dve.wait_ge(s("oc"), i)
                        step(tt(wide[:, bass.ds(hd, 1), 0:T].rearrange("p c n -> p (c n)"), G[2][:, 0:T], M[0],
                                ALU.mult))
                    if values and k == 7:
                        dve.wait_ge(s("v_free"), i * 16)
                        for h in range(2):
                            last = copy(orow[:, 512 * h:512 * h + 512], M[3][32 * h:32 * h + NB, :])
                        last.then_inc(s("orow"), 1)
                    yield

            def l1b(i, mix, tiles=True):
                if tiles:
                    walk("l1b", i, L1B_ORDER, lambda k, x: copy(halves(G[L1B_TO[k]]), x), T_L1B % 2, mix=mix,
                         late={0: (3, 1), 2: (7, 5)})
                finish(mix)

            l1b(0, mix_qv(3, True))
            l1b(1, mix1(1, True, True, True, False))
            step.straight()
            with dve.Fori(2, HC) as i:
                step.body(i, 2, 10)
                l1b(i, mix1(i, True, True, True, True))
            step.end(HC - 2, 10)
            l1b(HC, mix1(HC, False, True, True, True), False)
            l1b(HC + 1, mix1(HC + 1, False, False, False, True), False)
            dve.wait_ge(s("mixed1"), HC)
            tt(wide[:, 0:HC, T:N], OS, GS, ALU.mult).then_inc(s("mixed1_all"), 1)
            dve.wait_ge(s("mixed1_all"), 1)
            take_mixed(3)
            step.straight()

            def row(j, t):
                dve.wait_ge(s("y1_t"), j * 2 + (t + 1))
                copy(yrow[:, bass.ds(j * 256 + P * t, P)], M[2 + t][0:NB, 0:P]).then_inc(s("ys"), 1)

            def rows_out(j, first):
                yield
                if not first:
                    row(j - 1, 1)
                yield
                yield
                row(j, 0)
                yield

            def out1(j, first=False, ahead=2):
                def evac(k, x):
                    dve.wait_ge(s("evac"), j * 2 + (T_OUT1 + k))
                    if not first:
                        dve.wait_ge(s("y1_t"), j * 2 + (k - 1))
                    return residual(1, x, j, k, G[2 + k])

                mix = rows_out(j, first)
                walk("out1", j, OUT_ORDER, evac, 0, mix=mix, ahead=ahead)

            dve.wait_ge(s("act_ready"), 64)
            out1(0, True)
            step.straight()
            with dve.Fori(1, 7) as j:
                step.body(j, 1, 4)
                out1(j)
            step.end(6, 4)
            out1(7, ahead=0)
            row(7, 1)

        def layer1_pages(pool):
            pool.wait_ge(s("ptab"), 16)
            pool.wait_ge(s("st_out"), 128)
            pool.wait_ge(s("s_out"), 128)
            ck, cv = a["cache_k"][0].rearrange("n s h d -> n s (h d)"), a["cache_v"][0].rearrange("n s h d -> n s (h d)")

            def fetch(src, sample, p, slot):
                page = pool.value_load(ptab[0:1, bass.ds(sample * NPAGE + p, 1)], min_val=0, max_val=NPOOL - 1)
                pool.dma_start(pages[:, slot, :], src[bass.ds(page, 1)].rearrange("n s d -> (n s) d"))\
                    .then_inc(s(f"page{slot}"), 16)

            def value_page(i, p, keys):
                slot, load = value_slot(p, keys)
                if not keys and slot < 2 and load == 1:
                    pool.wait_ge(s("k_free"), 128)
                elif load > 1:
                    pool.wait_ge(s("v_free"), (i - 1) * 16 + (p - (3 if keys else 5) + 1))
                    pool.sem_inc(s("pool_waited"), 1)
                elif not (isinstance(i, int) and i == 1):
                    pool.wait_ge(s("v_free"), (i - 1) * 16 - (0, 2, 1)[p])
                    pool.sem_inc(s("pool_waited"), 1)
                fetch(cv, i - 1, p, slot)

            def body(i, keys, values):
                if values:
                    value_page(i, 0, keys)
                for k in range(8):
                    for p in (2 * k + 1, 2 * k + 2):
                        if values and p < NPAGE:
                            value_page(i, p, keys)
                    for p in (2 * k, 2 * k + 1):
                        if keys:
                            if k:
                                pool.wait_ge(s("k_free"), i * 16 + (p - 1))
                                pool.sem_inc(s("pool_waited"), 1)
                            elif not (isinstance(i, int) and i == 0):
                                pool.wait_ge(s("k_free"), i * 16)
                                pool.sem_inc(s("pool_waited"), 1)
                            fetch(ck, i, p, key_slot(p)[0])
                    if k == 3 and keys:
                        if not (isinstance(i, int) and i == 0):
                            pool.wait_ge(s("sg"), i)
                        pool.dma_start(ws, a["o_w_s"][0, bass.ds(i, 1)].rearrange("g t s -> t (g s)"))\
                            .then_inc(s("ws_in"), 16)
                        pool.dma_start(brow[0:1, 0:P], a["o_b_s"][0, bass.ds(i, 1)]).then_inc(s("ws_in"), 16)

            body(0, True, False)
            body(1, True, True)
            with pool.Fori(2, NB) as i:
                body(i, True, True)
            body(NB, False, True)

        @block.gpsimd
        def _(pool):
            pool.dma_start(ptab[:, :], a["page_table"].rearrange("(o b) p -> o (b p)", o=1)).then_inc(s("ptab"), 16)
            pool.wait_ge(s("xt_a"), KC)
            pool.wait_ge(s("xt_s"), KC)
            with pool.Fori(1, 9) as g:
                pool.wait_ge(s("mod_read"), g)
                pool.sem_inc(s("pool_waited"), 1)
                pool.dma_start(xt_dram[:, bass.ds(g * 2 - 2, 2), :], wide[:, bass.ds(g * 2 - 2, 2), :])\
                    .then_inc(s("xt_out"), 16)
            pool.wait_ge(s("xt_out"), 128)
            pool.wait_ge(s("la_x"), 1)

            def mix0(i, gla, states):
                if not (isinstance(i, int) and i == 0):
                    pool.wait_ge(s("st_out"), i * 16)
                    pool.sem_inc(s("pool_waited"), 1)
                    pool.wait_ge(s("os"), i)
                pool.dma_start(st[:, :, :], a[states][0, :, bass.ds(i if gla else i - HEADS, 1)]
                               .rearrange("b h k v -> k b (h v)")).then_inc(s("st_in"), 16)
                if not gla:
                    pool.wait_ge(s("mixed"), i * 2)
                    pool.sem_inc(s("pool_waited"), 1)
                    pool.dma_start(decays, a["ret"][bass.ds(i - HEADS, 1)].rearrange("h p n -> p (h n)"))\
                        .then_inc(s("ret_in"), 16)
                for n in range(1, NCH):
                    pool.wait_ge(s("s_step"), i * 8 + n)
                    pool.sem_inc(s("pool_waited"), 1)
                    pool.tensor_scalar(carry[:, n, :], S[:, (n - 1) % 2, :],
                                       small[:, 6 * (n // 2) + n % 2:6 * (n // 2) + n % 2 + 1], None,
                                       ALU.mult).then_inc(s("carry"), 1)
                pool.wait_ge(s("s_step"), i * 8 + 8)
                pool.sem_inc(s("pool_waited"), 1)
                kind = "gla" if gla else "ret"
                h = i if gla else i - HEADS
                pool.dma_start(a[kind + "_prompt_out"][0, 0, bass.ds(h, 1)].rearrange("h k v -> k (h v)"),
                               S[:, 1, :]).then_inc(s("s_out"), 16)
                pool.wait_ge(s("st_step"), i * 8 + 8)
                pool.sem_inc(s("pool_waited"), 1)
                pool.dma_start(a[kind + "_sample_out"][0, :, bass.ds(h, 1)].rearrange("b h k v -> k b (h v)"),
                               st[:, :, :]).then_inc(s("st_out"), 16)

            mix0(0, True, "state_gla")
            with pool.Fori(1, HEADS) as i:
                mix0(i, True, "state_gla")
            pool.wait_ge(s("cum"), HEADS)
            pool.dma_start(rope, a["rope"]).then_inc(s("rope_in"), 16)
            with pool.Fori(HEADS, 2 * HEADS) as i:
                mix0(i, False, "state_ret")

            pool.wait_ge(s("act_ready"), 32)
            with pool.Fori(0, 8) as j:
                for t in range(2):
                    pool.wait_ge(s("evac"), j * 2 + (T_OUT0 + t - 1))
                    pool.sem_inc(s("pool_waited"), 1)
                    pool.dma_start(G[t], xt_dram[:, bass.ds(j * 2 + t, 1), :].rearrange("p c n -> p (c n)"))\
                        .then_inc(s(f"xj{t}"), 16)
            pool.wait_ge(s("evac"), T_OUT0 + 16)
            pool.dma_start(x1_dram, wide[:, :, :]).then_inc(s("x1_out"), 16)
            pool.wait_ge(s("x1_out"), 16)
            layer1_pages(pool)

            def fetch_x(j, t):
                pool.wait_ge(s("evac"), j * 2 + (T_OUT1 + t - 1))
                pool.sem_inc(s("pool_waited"), 1)
                pool.dma_start(G[t], x1_dram[:, bass.ds(j * 2 + t, 1), :].rearrange("p c n -> p (c n)"))\
                    .then_inc(s(f"xj{t}"), 16)

            def store_y(j, t):
                pool.wait_ge(s("yo"), j * 2 + (t + 1))
                pool.sem_inc(s("pool_waited"), 1)
                pool.dma_start(a["y_prompt_out"][0].rearrange("(q p) n -> p q n", p=P)
                               [:, :, bass.ds(j * 256 + P * t, P)],
                               yo[t].rearrange("p (q n) -> p q n", q=NT)).then_inc(s(f"y_out{t}"), 16)

            pool.wait_ge(s("act_ready"), 64)
            fetch_x(0, 0)
            fetch_x(0, 1)
            with pool.Fori(1, 8) as j:
                fetch_x(j, 0)
                store_y(j - 1, 0)
                fetch_x(j, 1)
                store_y(j - 1, 1)
            store_y(7, 0)
            store_y(7, 1)
            pool.wait_ge(s("ys"), 16)
            pool.dma_start(a["y_sample_out"].rearrange("b o d -> (b o) d"), yrow).then_inc(s("ys_out"), 16)
            for name, value in (("ys_out", 16), ("y_out0", 128), ("y_out1", 128), ("st_out", 128), ("s_out", 128), ("kv_out", 512),
                                ("cv_out", 128)):
                pool.wait_ge(s(name), value)

        return


_INS = ["x_prompt", "x_sample", "state_gla", "state_ret", "cache_k", "cache_v", "page_table",
        "c_prompt", "c_sample", "e_norm_g", "e_w_ada", "e_b_ada", "e_w_in", "e_w_a2", "e_b_a",
        "e_gla_norm_g", "e_ret_norm_g", "e_w_out", "o_norm_g", "o_w_ada", "o_b_ada", "o_w_in",
        "o_q_norm_g", "o_k_norm_g", "o_sb_offset", "o_v_norm_g", "o_w_s", "o_b_s", "o_w_out"]
_OUTS = [("y_prompt", (1, T, D)), ("y_sample", (NB, 1, D)),
         ("gla_prompt", (1, 1, HEADS, P, 256)), ("gla_sample", (1, NB, HEADS, P, 256)),
         ("ret_prompt", (1, 1, HEADS, P, 256)), ("ret_sample", (1, NB, HEADS, P, 256)),
         ("k_prompt", (1, 1, T, HC, P)), ("v_prompt", (1, 1, T, HC, P)),
         ("k_sample", (1, NB, 1, HC, P)), ("v_sample", (1, NB, 1, HC, P)), ("chunk_v", (1, NB, 1, BR))]


def kernel(**inputs):
    import concourse.bacc as bacc
    from concourse.bass_utils import run_bass_kernel_spmd

    nc = bacc.Bacc("TRN2", target_bir_lowering=False, num_devices=1)
    cst = constants()
    arrays, a, o = {}, {}, {}
    for name in _INS:
        x = np.ascontiguousarray(inputs[name])
        arrays["in_" + name] = x
        a[name] = nc.dram_tensor("in_" + name, x.shape, mybir.dt.from_np(x.dtype), kind="ExternalInput").ap()
    c_aps = {}
    for name, x in cst.items():
        arrays["const_" + name] = x
        c_aps[name] = nc.dram_tensor("const_" + name, x.shape, F32, kind="ExternalInput").ap()
    a["ret"], a["rope"] = c_aps["ret"], c_aps["rope"]
    for name, shape in _OUTS:
        a[name + "_out"] = nc.dram_tensor("out_" + name, shape, F32, kind="ExternalOutput").ap()
    build(nc, a, o, c_aps)
    r = run_bass_kernel_spmd(nc, [arrays], core_ids=[0])
    return tuple(r.results[0]["out_" + name] for name, _ in _OUTS)
```
